# Optimizing a Trainium2 kernel written in Bass

```python
import math
import jax, jax.numpy as jnp
from jax import lax
import numpy as np

D_MODEL = 1024
BATCH = 1
SEQ = 1024
DEPTH = 1

SSM_D_INNER = D_MODEL
SSM_HEAD_DIM = 64
SSM_HEADS = SSM_D_INNER // SSM_HEAD_DIM
SSM_GROUPS = 4
SSM_STATE = 128
SSM_CONV = 4
SSM_CHUNK = 128
SSM_CONV_DIM = SSM_D_INNER + 2 * SSM_GROUPS * SSM_STATE
ATT_D = D_MODEL
ATT_HEAD_DIM = 64
ATT_HEADS = ATT_D // ATT_HEAD_DIM
ATT_BLOCK = 128
RMS_EPS = 1e-6
IN_SPLITS = (SSM_D_INNER, SSM_CONV_DIM, SSM_HEADS, ATT_D, ATT_D, ATT_D, ATT_HEADS, ATT_D, D_MODEL, D_MODEL)
IN_COLS = SSM_D_INNER + SSM_CONV_DIM + SSM_HEADS + 4 * ATT_D + ATT_HEADS + 2 * D_MODEL


def _offsets(sizes):
    out, acc = [], 0
    for s in sizes[:-1]:
        acc += s
        out.append(acc)
    return out

def _rmsnorm(x, g):
    xf = x.astype(jnp.float32)
    y = xf * lax.rsqrt(jnp.mean(xf * xf, axis=-1, keepdims=True) + RMS_EPS) * g.astype(jnp.float32)
    return y.astype(x.dtype)

def _causal_dwconv(u, w, b):
    y = lax.conv_general_dilated(u, w[:, None, :].astype(u.dtype), window_strides=(1,),
                                 padding=((SSM_CONV - 1, 0),),
                                 dimension_numbers=('NWC', 'WIO', 'NWC'),
                                 feature_group_count=u.shape[-1])
    return y + b.astype(u.dtype)

def _ssd_chunked(xs, dt, a, b_mat, c_mat, d_skip):
    bsz, seqlen, n_heads, p = xs.shape
    g, n = b_mat.shape[2], b_mat.shape[3]
    r = n_heads // g
    nc = seqlen // SSM_CHUNK
    q = SSM_CHUNK
    xdt = (xs * dt[..., None]).reshape(bsz, nc, q, g, r, p)
    bc = b_mat.reshape(bsz, nc, q, g, n)
    cc = c_mat.reshape(bsz, nc, q, g, n)
    da_cs = jnp.cumsum((dt * a).reshape(bsz, nc, q, g, r), axis=2)
    causal = jnp.tril(jnp.ones((q, q), dtype=bool))
    seg = da_cs[:, :, :, None] - da_cs[:, :, None, :]
    decay = jnp.exp(jnp.where(causal[None, None, :, :, None, None], seg, -jnp.inf))
    cb = jnp.einsum('bclgn,bcsgn->bclsg', cc, bc)
    y_diag = jnp.einsum('bclsgr,bcsgrp->bclgrp', cb[..., None] * decay, xdt)
    to_end = jnp.exp(da_cs[:, :, -1:] - da_cs)
    states = jnp.einsum('bcsgn,bcsgrp->bcgrpn', bc, xdt * to_end[..., None])
    chunk_decay = jnp.exp(da_cs[:, :, -1])

    def step(carry, inp):
        st, dec = inp
        return carry * dec[..., None, None] + st, carry

    init = jnp.zeros((bsz, g, r, p, n), states.dtype)
    _, prev = lax.scan(step, init, (jnp.moveaxis(states, 1, 0), jnp.moveaxis(chunk_decay, 1, 0)))
    prev = jnp.moveaxis(prev, 0, 1)
    y_off = jnp.einsum('bclgn,bcgrpn->bclgrp', cc, prev) * jnp.exp(da_cs)[..., None]
    y = (y_diag + y_off).reshape(bsz, seqlen, n_heads, p)
    return y + xs * d_skip[:, None]

def _forgetting_attention(q, k, v, log_f):
    seqlen = q.shape[2]
    scale = ATT_HEAD_DIM ** -0.5
    fcum = jnp.cumsum(log_f, axis=-1)
    outs = []
    for blk in range(seqlen // ATT_BLOCK):
        q0, q1 = blk * ATT_BLOCK, (blk + 1) * ATT_BLOCK
        s = jnp.einsum('bhqd,bhkd->bhqk', q[:, :, q0:q1], k[:, :, :q1]).astype(jnp.float32) * scale
        s = s + fcum[:, :, q0:q1, None] - fcum[:, :, None, :q1]
        qpos = q0 + jnp.arange(ATT_BLOCK)
        kpos = jnp.arange(q1)
        s = jnp.where(kpos[None, :] <= qpos[:, None], s, -jnp.inf)
        prob = jax.nn.softmax(s, axis=-1)
        outs.append(jnp.einsum('bhqk,bhkd->bhqd', prob.astype(v.dtype), v[:, :, :q1]))
    return jnp.concatenate(outs, axis=2)

def _hybrid_layer(x, pre_g, w_in, conv_w, conv_b, dt_bias, a_log, d_skip, ssm_norm_g,
                  fgate_b, w_branch_ssm, w_branch_att, w_out, post_g):
    bsz, seqlen, _ = x.shape
    f32 = jnp.float32
    h = _rmsnorm(x, pre_g)
    proj = jnp.einsum('bld,de->ble', h, w_in)
    z_ssm, xbc, dt_raw, q, k, v, f_raw, z_att, g_ssm, g_att = jnp.split(proj, _offsets(IN_SPLITS), axis=-1)

    xbc = jax.nn.silu(_causal_dwconv(xbc, conv_w, conv_b))
    gn = SSM_GROUPS * SSM_STATE
    xs, b_ssm, c_ssm = jnp.split(xbc, [SSM_D_INNER, SSM_D_INNER + gn], axis=-1)
    dt = jax.nn.softplus(dt_raw.astype(f32) + dt_bias.astype(f32))
    a = -jnp.exp(a_log.astype(f32))
    y = _ssd_chunked(xs.astype(f32).reshape(bsz, seqlen, SSM_HEADS, SSM_HEAD_DIM), dt, a,
                     b_ssm.astype(f32).reshape(bsz, seqlen, SSM_GROUPS, SSM_STATE),
                     c_ssm.astype(f32).reshape(bsz, seqlen, SSM_GROUPS, SSM_STATE),
                     d_skip.astype(f32))
    yg = (y.reshape(bsz, seqlen, SSM_D_INNER) * jax.nn.silu(z_ssm.astype(f32)))
    yg = yg.reshape(bsz, seqlen, SSM_GROUPS, SSM_D_INNER // SSM_GROUPS)
    yg = yg * lax.rsqrt(jnp.mean(yg * yg, axis=-1, keepdims=True) + RMS_EPS)
    y_ssm = (yg.reshape(bsz, seqlen, SSM_D_INNER) * ssm_norm_g.astype(f32)).astype(x.dtype)

    def heads(t):
        return t.reshape(bsz, seqlen, ATT_HEADS, ATT_HEAD_DIM).transpose(0, 2, 1, 3)
    log_f = jax.nn.log_sigmoid(f_raw.astype(f32) + fgate_b.astype(f32)).transpose(0, 2, 1)
    o = _forgetting_attention(heads(q), heads(k), heads(v), log_f)
    o = o.transpose(0, 2, 1, 3).reshape(bsz, seqlen, ATT_D)
    y_att = (o.astype(f32) * jax.nn.silu(z_att.astype(f32))).astype(x.dtype)

    p_ssm = jnp.einsum('ble,ed->bld', y_ssm, w_branch_ssm)
    p_att = jnp.einsum('ble,ed->bld', y_att, w_branch_att)
    merged = jax.nn.sigmoid(g_ssm) * p_ssm + jax.nn.sigmoid(g_att) * p_att
    out = jnp.einsum('bld,de->ble', merged, w_out)
    return x + _rmsnorm(out, post_g)

def first_inputs(seed: int = 0) -> dict:
    key = jax.random.key(seed)
    ks = jax.random.split(key, 16)
    f32 = jnp.float32
    nl = DEPTH
    nrm = jax.random.normal
    x = nrm(ks[0], (BATCH, SEQ, D_MODEL), f32)
    pre_norm_g = 1.0 + 0.05 * nrm(ks[1], (nl, D_MODEL), f32)
    w_in = nrm(ks[2], (nl, D_MODEL, IN_COLS), f32) * D_MODEL ** -0.5
    conv_w = nrm(ks[3], (nl, SSM_CONV, SSM_CONV_DIM), f32) * SSM_CONV ** -0.5
    conv_b = 0.02 * nrm(ks[4], (nl, SSM_CONV_DIM), f32)
    dt0 = jnp.exp(jax.random.uniform(ks[5], (nl, SSM_HEADS), f32, minval=math.log(1e-3), maxval=math.log(1e-1)))
    dt_bias = dt0 + jnp.log(-jnp.expm1(-dt0))
    a_log = jnp.log(jax.random.uniform(ks[6], (nl, SSM_HEADS), f32, minval=1.0, maxval=16.0))
    d_skip = 1.0 + 0.1 * nrm(ks[7], (nl, SSM_HEADS), f32)
    ssm_norm_g = 1.0 + 0.05 * nrm(ks[8], (nl, SSM_D_INNER), f32)
    fgate_b = jax.random.uniform(ks[9], (nl, ATT_HEADS), f32, minval=1.0, maxval=4.0)
    w_branch_ssm = nrm(ks[10], (nl, SSM_D_INNER, D_MODEL), f32) * SSM_D_INNER ** -0.5
    w_branch_att = nrm(ks[11], (nl, ATT_D, D_MODEL), f32) * ATT_D ** -0.5
    w_out = nrm(ks[12], (nl, D_MODEL, D_MODEL), f32) * D_MODEL ** -0.5
    post_norm_g = 1.0 + 0.05 * nrm(ks[13], (nl, D_MODEL), f32)
    return {'x': x, 'pre_norm_g': pre_norm_g, 'w_in': w_in, 'conv_w': conv_w, 'conv_b': conv_b,
            'dt_bias': dt_bias, 'a_log': a_log, 'd_skip': d_skip, 'ssm_norm_g': ssm_norm_g,
            'fgate_b': fgate_b, 'w_branch_ssm': w_branch_ssm, 'w_branch_att': w_branch_att,
            'w_out': w_out, 'post_norm_g': post_norm_g}

def first_block(x, pre_norm_g, w_in, conv_w, conv_b, dt_bias, a_log, d_skip, ssm_norm_g,
              fgate_b, w_branch_ssm, w_branch_att, w_out, post_norm_g):
    for i in range(DEPTH):
        x = _hybrid_layer(x, pre_norm_g[i], w_in[i], conv_w[i], conv_b[i], dt_bias[i], a_log[i],
                          d_skip[i], ssm_norm_g[i], fgate_b[i], w_branch_ssm[i], w_branch_att[i],
                          w_out[i], post_norm_g[i])
    return x


CONV_CH = D_MODEL // 2
CONV_WIDTH = 31
DA_HEADS = 4
DA_HEAD_DIM = 64
DA_V_DIM = 2 * DA_HEAD_DIM
ATTN_W = DA_HEADS * DA_V_DIM
N_BRANCH = 2
COL_CONV = 2 * CONV_CH
COL_Q = DA_HEADS * 2 * DA_HEAD_DIM
COL_K = DA_HEADS * 2 * DA_HEAD_DIM
COL_V = ATTN_W
COL_GATE = N_BRANCH * D_MODEL
IN_COLS_2 = COL_CONV + COL_Q + COL_K + COL_V + COL_GATE
N_GROUPS = 4
EXPERTS_PER_GROUP = 8
N_EXPERTS = N_GROUPS * EXPERTS_PER_GROUP
TOP_K_IN_GROUP = 2
D_EXPERT = D_MODEL // 2

Q_BLOCK = 128
ROW_BLOCK = 128
EPS = 1e-6


def rms_norm(x, g):
    xf = x.astype(jnp.float32)
    y = xf * lax.rsqrt(jnp.mean(xf * xf, axis=-1, keepdims=True) + EPS)
    return (y * g.astype(jnp.float32)).astype(x.dtype)

def layer_norm(x, g, b):
    xf = x.astype(jnp.float32)
    mu = jnp.mean(xf, axis=-1, keepdims=True)
    var = jnp.mean(jnp.square(xf - mu), axis=-1, keepdims=True)
    y = (xf - mu) * lax.rsqrt(var + EPS)
    return (y * g.astype(jnp.float32) + b.astype(jnp.float32)).astype(x.dtype)

def conformer_conv(u, dw_w, dw_b, ln_g, ln_b):
    a, gate = jnp.split(u, 2, axis=-1)
    y = a * jax.nn.sigmoid(gate)
    y = lax.conv_general_dilated(
        y, dw_w[:, None, :].astype(y.dtype), window_strides=(1,),
        padding=[(CONV_WIDTH - 1, 0)],
        dimension_numbers=("NWC", "WIO", "NWC"),
        feature_group_count=CONV_CH) + dw_b
    y = layer_norm(y, ln_g, ln_b)
    return jax.nn.silu(y)

def diff_attention(q, k, v, lam, subln_g, lam_init):
    B, S = q.shape[0], q.shape[1]
    nb = S // Q_BLOCK
    scale = DA_HEAD_DIM ** -0.5
    qb = q.reshape(B, nb, Q_BLOCK, DA_HEADS, 2, DA_HEAD_DIM).transpose(1, 0, 2, 3, 4, 5)
    key_pos = jnp.arange(S)

    def block(args):
        qi, bi = args
        s = jnp.einsum("bqhcd,bkhcd->bhcqk", qi, k,
                       preferred_element_type=jnp.float32) * scale
        q_pos = bi * Q_BLOCK + jnp.arange(Q_BLOCK)
        mask = key_pos[None, :] <= q_pos[:, None]
        s = jnp.where(mask, s, -jnp.inf)
        p = jax.nn.softmax(s, axis=-1)
        a = (p[:, :, 0] - lam * p[:, :, 1]).astype(v.dtype)
        return jnp.einsum("bhqk,bkhe->bqhe", a, v)

    o = lax.map(block, (qb, jnp.arange(nb)))
    o = o.transpose(1, 0, 2, 3, 4).reshape(B, S, DA_HEADS, DA_V_DIM)
    o = rms_norm(o, subln_g) * (1.0 - lam_init)
    return o.reshape(B, S, ATTN_W)

def hierarchical_moe(h, w_rg, b_rg, w_re, b_re, w_g, w_u, w_d):
    B, S, D = h.shape
    T = B * S
    hf = h.reshape(T, D)
    g_logits = jnp.matmul(hf, w_rg, preferred_element_type=jnp.float32) + b_rg.astype(jnp.float32)
    g_prob = jax.nn.softmax(g_logits, axis=-1)
    g_sel = jnp.argmax(g_logits, axis=-1)
    g_w = jnp.take_along_axis(g_prob, g_sel[:, None], axis=1)
    e_logits = (jnp.matmul(hf, w_re, preferred_element_type=jnp.float32)
                + b_re.astype(jnp.float32)).reshape(T, N_GROUPS, EXPERTS_PER_GROUP)
    e_logits = jnp.take_along_axis(e_logits, g_sel[:, None, None], axis=1)[:, 0]
    e_prob = jax.nn.softmax(e_logits, axis=-1)
    top_p, top_i = lax.top_k(e_prob, TOP_K_IN_GROUP)
    wts = top_p / jnp.sum(top_p, axis=-1, keepdims=True) * g_w
    eidx = g_sel[:, None] * EXPERTS_PER_GROUP + top_i

    A = T * TOP_K_IN_GROUP
    e_flat = eidx.reshape(A).astype(jnp.int32)
    tok_flat = jnp.repeat(jnp.arange(T, dtype=jnp.int32), TOP_K_IN_GROUP)
    w_flat = wts.reshape(A).astype(h.dtype)
    order = jnp.argsort(e_flat, stable=True)
    e_s, tok_s, w_s = e_flat[order], tok_flat[order], w_flat[order]
    counts = jnp.zeros((N_EXPERTS,), jnp.int32).at[e_flat].add(1)
    padded = (counts + ROW_BLOCK - 1) // ROW_BLOCK * ROW_BLOCK
    start = jnp.cumsum(counts) - counts
    pad_end = jnp.cumsum(padded)
    pstart = pad_end - padded
    dest = pstart[e_s] + jnp.arange(A, dtype=jnp.int32) - start[e_s]
    n_rows = A + N_EXPERTS * ROW_BLOCK
    n_blk = n_rows // ROW_BLOCK
    row_tok = jnp.zeros((n_rows,), jnp.int32).at[dest].set(tok_s)
    row_w = jnp.zeros((n_rows,), h.dtype).at[dest].set(w_s)
    blk_exp = jnp.clip(jnp.searchsorted(pad_end, jnp.arange(n_blk, dtype=jnp.int32) * ROW_BLOCK,
                                        side="right"), 0, N_EXPERTS - 1)

    def expert_block(args):
        toks, wb, e = args
        xb = hf[toks]
        hid = jax.nn.silu(jnp.matmul(xb, w_g[e])) * jnp.matmul(xb, w_u[e])
        return jnp.matmul(hid, w_d[e]) * wb[:, None]

    yb = lax.map(expert_block, (row_tok.reshape(n_blk, ROW_BLOCK),
                                row_w.reshape(n_blk, ROW_BLOCK), blk_exp))
    y = jnp.zeros_like(hf).at[row_tok].add(yb.reshape(n_rows, D))
    return y.reshape(B, S, D)

def second_inputs(seed: int = 0) -> dict:
    key = jax.random.key(seed)
    ks = jax.random.split(key, 26)
    f32 = jnp.float32

    def nrm(k, shape, scale):
        return jax.random.normal(k, shape, f32) * scale

    L, D, C = DEPTH, D_MODEL, CONV_CH
    return {
        "x": nrm(ks[0], (BATCH, SEQ, D), 1.0),
        "attn_norm_g": 1.0 + nrm(ks[1], (L, D), 0.05),
        "w_in": nrm(ks[2], (L, D, IN_COLS_2), D ** -0.5),
        "conv_dw_w": nrm(ks[3], (L, CONV_WIDTH, C), CONV_WIDTH ** -0.5),
        "conv_dw_b": nrm(ks[4], (L, C), 0.02),
        "conv_ln_g": 1.0 + nrm(ks[5], (L, C), 0.05),
        "conv_ln_b": nrm(ks[6], (L, C), 0.02),
        "w_conv_out": nrm(ks[7], (L, C, D), C ** -0.5),
        "q_norm_g": 1.0 + nrm(ks[8], (L, DA_HEAD_DIM), 0.05),
        "k_norm_g": 1.0 + nrm(ks[9], (L, DA_HEAD_DIM), 0.05),
        "lambda_q1": nrm(ks[10], (L, DA_HEAD_DIM), 0.1),
        "lambda_k1": nrm(ks[11], (L, DA_HEAD_DIM), 0.1),
        "lambda_q2": nrm(ks[12], (L, DA_HEAD_DIM), 0.1),
        "lambda_k2": nrm(ks[13], (L, DA_HEAD_DIM), 0.1),
        "subln_g": 1.0 + nrm(ks[14], (L, DA_V_DIM), 0.05),
        "w_attn_out": nrm(ks[15], (L, ATTN_W, D), ATTN_W ** -0.5),
        "w_out": nrm(ks[16], (L, D, D), D ** -0.5),
        "ffn_norm_g": 1.0 + nrm(ks[17], (L, D), 0.05),
        "w_router_group": nrm(ks[18], (L, D, N_GROUPS), D ** -0.5),
        "b_router_group": nrm(ks[19], (L, N_GROUPS), 0.01),
        "w_router_expert": nrm(ks[20], (L, D, N_EXPERTS), D ** -0.5),
        "b_router_expert": nrm(ks[21], (L, N_EXPERTS), 0.01),
        "w_gate_e": nrm(ks[22], (L, N_EXPERTS, D, D_EXPERT), D ** -0.5),
        "w_up_e": nrm(ks[23], (L, N_EXPERTS, D, D_EXPERT), D ** -0.5),
        "w_down_e": nrm(ks[24], (L, N_EXPERTS, D_EXPERT, D), D_EXPERT ** -0.5),
    }

def second_block(x, attn_norm_g, w_in, conv_dw_w, conv_dw_b, conv_ln_g, conv_ln_b, w_conv_out,
              q_norm_g, k_norm_g, lambda_q1, lambda_k1, lambda_q2, lambda_k2, subln_g,
              w_attn_out, w_out, ffn_norm_g, w_router_group, b_router_group,
              w_router_expert, b_router_expert, w_gate_e, w_up_e, w_down_e):
    B, S, D = x.shape
    for l in range(DEPTH):
        lam_init = 0.8 - 0.6 * math.exp(-0.3 * l)
        h = rms_norm(x, attn_norm_g[l])
        proj = jnp.matmul(h, w_in[l])
        o0 = COL_CONV
        o1 = o0 + COL_Q
        o2 = o1 + COL_K
        o3 = o2 + COL_V
        u_conv = proj[..., :o0]
        q = proj[..., o0:o1].reshape(B, S, DA_HEADS, 2, DA_HEAD_DIM)
        k = proj[..., o1:o2].reshape(B, S, DA_HEADS, 2, DA_HEAD_DIM)
        v = proj[..., o2:o3].reshape(B, S, DA_HEADS, DA_V_DIM)
        gates = jax.nn.sigmoid(proj[..., o3:]).reshape(B, S, N_BRANCH, D)

        conv_out = conformer_conv(u_conv, conv_dw_w[l], conv_dw_b[l], conv_ln_g[l], conv_ln_b[l])

        q = rms_norm(q, q_norm_g[l])
        k = rms_norm(k, k_norm_g[l])
        lam = (jnp.exp(jnp.sum(lambda_q1[l].astype(jnp.float32) * lambda_k1[l].astype(jnp.float32)))
               - jnp.exp(jnp.sum(lambda_q2[l].astype(jnp.float32) * lambda_k2[l].astype(jnp.float32)))
               + lam_init)
        attn_out = diff_attention(q, k, v, lam, subln_g[l], lam_init)

        merged = (gates[:, :, 0] * jnp.matmul(conv_out, w_conv_out[l])
                  + gates[:, :, 1] * jnp.matmul(attn_out, w_attn_out[l]))
        x = x + jnp.matmul(merged, w_out[l])
        h2 = rms_norm(x, ffn_norm_g[l])
        x = x + hierarchical_moe(h2, w_router_group[l], b_router_group[l], w_router_expert[l],
                                 b_router_expert[l], w_gate_e[l], w_up_e[l], w_down_e[l])
    return x


def setup_inputs(seed=0):
    out = dict(first_inputs(seed))
    for name, value in second_inputs(seed + 1).items():
        if name != "x":
            out[name + "_2"] = value
    return out


def reference(
    x, pre_norm_g, w_in, conv_w, conv_b, dt_bias, a_log, d_skip, ssm_norm_g, fgate_b,
    w_branch_ssm, w_branch_att, w_out, post_norm_g, attn_norm_g_2, w_in_2, conv_dw_w_2,
    conv_dw_b_2, conv_ln_g_2, conv_ln_b_2, w_conv_out_2, q_norm_g_2, k_norm_g_2, lambda_q1_2,
    lambda_k1_2, lambda_q2_2, lambda_k2_2, subln_g_2, w_attn_out_2, w_out_2, ffn_norm_g_2,
    w_router_group_2, b_router_group_2, w_router_expert_2, b_router_expert_2, w_gate_e_2,
    w_up_e_2, w_down_e_2,
):
    x = first_block(
        x, pre_norm_g, w_in, conv_w, conv_b, dt_bias, a_log, d_skip, ssm_norm_g, fgate_b,
        w_branch_ssm, w_branch_att, w_out, post_norm_g,
    )
    return second_block(
        x, attn_norm_g_2, w_in_2, conv_dw_w_2, conv_dw_b_2, conv_ln_g_2, conv_ln_b_2,
        w_conv_out_2, q_norm_g_2, k_norm_g_2, lambda_q1_2, lambda_k1_2, lambda_q2_2,
        lambda_k2_2, subln_g_2, w_attn_out_2, w_out_2, ffn_norm_g_2, w_router_group_2,
        b_router_group_2, w_router_expert_2, b_router_expert_2, w_gate_e_2, w_up_e_2,
        w_down_e_2,
    )


_drawn_inputs = setup_inputs


def setup_inputs(seed=0):
    import zlib

    import numpy as np

    out = dict(_drawn_inputs(seed))
    spreads = {}
    factors = {'conv_dw_b_2': 3.686,
     'conv_ln_b_2': 6.175,
     'q_norm_g_2': 3.197,
     'k_norm_g_2': 3.254,
     'lambda_q1_2': 3.608,
     'lambda_k1_2': 8.0,
     'b_router_group_2': 3.933,
     'b_router_expert_2': 7.66}
    for name, (base, spread) in spreads.items():
        noise = np.random.default_rng([zlib.crc32(name.encode()), seed]).standard_normal(out[name].shape)
        drawn = base * np.exp(spread * noise) if base else spread * noise
        out[name] = __import__('jax').numpy.asarray(drawn.astype(out[name].dtype))
    for name, factor in factors.items():
        out[name] = (out[name] * factor).astype(out[name].dtype)
    return out
```

```python
from contextlib import ExitStack

import concourse.bass as bass
from concourse import mybir

F32 = mybir.dt.float32
BF16 = mybir.dt.bfloat16
I32 = mybir.dt.int32
U32 = mybir.dt.uint32
ACT = mybir.ActivationFunctionType
ALU = mybir.AluOpType
AX = mybir.AxisListType

P = 128
SEQ = 1024
D = 1024
TT = SEQ // P
KC = D // P
BANK = 512
EPS = 1e-6

HEADS, HD = 16, 64
GROUPS, STATE, CONV = 4, 128, 4
HPG = HEADS // GROUPS
XBC = D + 2 * GROUPS * STATE
C_Z, C_XBC = 0, D
C_DT = C_XBC + XBC
C_Q = C_DT + HEADS
C_K, C_V = C_Q + D, C_Q + 2 * D
C_F = C_Q + 3 * D
C_ZA = C_F + HEADS
C_GS, C_GA = C_ZA + D, C_ZA + 2 * D

CCH, CW = D // 2, 31
DH, DHD = 4, 64
DV = 2 * DHD
C2_Q = 2 * CCH
C2_K = C2_Q + DH * DV
C2_V = C2_K + DH * DV
C2_G = C2_V + DH * DV
LAM_INIT = 0.8 - 0.6
NG, EPG = 4, 8
NE = NG * EPG
DE = D // 2
ASSIGN = 2 * SEQ
EXTRA = ASSIGN // P
SLOTS = (NE + EXTRA) * P

NEG = -1e30
REGION = 8192


class Steps:

    def __init__(self, eng, sem, base=0):
        self.eng, self.sem, self.base, self.n = eng, sem, base, 0

    def done(self, ins):
        ins.then_inc(self.sem, 1)
        self.n += 1
        return self.n

    def then_wait(self, ins):
        self.done(ins)
        self.eng.wait_ge(self.sem, self.base + self.n)


class Chip:

    def __init__(self, nc, ctx):
        self.nc, self.ctx = nc, ctx
        sb = lambda name, shape, dt=F32: ctx.enter_context(nc.sbuf_tensor(name, shape, dt))
        self.arena = sb("arena", [P, 6 * REGION])
        self.ps = ctx.enter_context(nc.psum_tensor("ps", [P, 8, BANK], F32))
        self.ident = sb("ident", [P, P])
        self.ones = sb("ones", [P, P])
        self.upto = sb("upto", [P, P])
        self.before = sb("before", [P, P])
        self.identb = sb("identb", [P, P], BF16)
        self.maskb = sb("maskb", [P, P], BF16)
        self.maskTb = sb("maskTb", [P, 4, P], BF16)
        self.small = sb("small", [P, 1600])
        ints = sb("ints", [P, 512], I32)
        self.dest = [ints[:, 8 * j:8 * j + 8] for j in range(2)]
        self.slot_token = ints[:, 16:16 + SLOTS // P]
        self.gather_at = [ints[:, 64 + j:65 + j] for j in range(2)]
        self.found = [ints[:, 66 + 64 * j:130 + 64 * j] for j in range(2)]
        self.expert_no = ints[:, 194:194 + NE]
        self.token_no = ints[:, 226:226 + TT]
        self.extra_expert = ints[:, 234:234 + EXTRA]
        self.extra_count = ints[:, 250:251]
        self.zeros_i = ints[:, 256:256 + SLOTS // P]
        self.slot_rows = ints[0:SLOTS // P, 320:320 + P]
        self.expert_gain = self.small[:, 1408 + 24:1408 + 32]
        self.weight = [self.small[:, 1408 + 32 + 8 * j:1408 + 40 + 8 * j] for j in range(2)]

    def at(self, region, offset, size):
        a = region * REGION + offset
        return self.arena[:, a:a + size]

    def sem(self, ctx, name):
        s = ctx.enter_context(self.nc.semaphore(name))
        ctx.callback(lambda: self.nc.gpsimd.sem_clear(s))
        return s


def cols(ap):
    return ap.rearrange("(k p) n -> p k n", p=P)


def phase_constants(c, zero, extra_dram, zeroed):
    nc = c.nc
    with ExitStack() as ctx:
        filled, shaped = c.sem(ctx, "const_filled"), c.sem(ctx, "const_shaped")
        zero_set = c.sem(ctx, "zero_set")
        block = ctx.enter_context(nc.Block())

        @block.vector
        def _(dve):
            nc.vector.memset(zero, 0.0).then_inc(zero_set, 1)

        @block.sync
        def _(sp):
            sp.wait_ge(zero_set, 1)
            for b in range(EXTRA):
                sp.dma_start(extra_dram[b * P:(b + 1) * P, :], zero).then_inc(zeroed, 16)

        @block.gpsimd
        def _(pool):
            for m, v in ((c.ident, 0.0), (c.ones, 1.0), (c.upto, 1.0), (c.before, 1.0),
                         (c.identb, 0.0), (c.maskb, 0.0), (c.maskTb, 0.0)):
                pool.memset(m[:], v).then_inc(filled, 1)
            pool.wait_ge(filled, 7)
            one = [[-1, P]]
            up = [[1, P]]
            for m in (c.ident, c.identb):
                pool.affine_select(out=m[:], in_=m[:], compare_op=ALU.not_equal, fill=1.0, base=0,
                                   pattern=one, channel_multiplier=1).then_inc(shaped, 1)
            pool.affine_select(out=c.upto[:], in_=c.upto[:], compare_op=ALU.is_ge, fill=0.0, base=0,
                               pattern=up, channel_multiplier=-1).then_inc(shaped, 1)
            pool.affine_select(out=c.before[:], in_=c.before[:], compare_op=ALU.is_gt, fill=0.0,
                               base=0, pattern=up, channel_multiplier=-1).then_inc(shaped, 1)
            pool.affine_select(out=c.maskb[:], in_=c.maskb[:], compare_op=ALU.is_ge, fill=NEG,
                               base=0, pattern=one, channel_multiplier=1).then_inc(shaped, 1)
            pool.affine_select(out=c.maskTb[:], in_=c.maskTb[:], compare_op=ALU.is_ge, fill=NEG,
                               base=0, pattern=[[0, 4], [1, P]], channel_multiplier=-1)\
                .then_inc(shaped, 1)
            pool.wait_ge(shaped, 6)


def phase_norm_T(c, name, src, dst, xn, gain_dram, src_dram=None, xn_dram=None, also=None):
    nc = c.nc
    with ExitStack() as ctx:
        loaded = [c.sem(ctx, f"{name}_loaded{t}") for t in range(2)]
        squared, rooted = c.sem(ctx, f"{name}_squared"), c.sem(ctx, f"{name}_rooted")
        step = c.sem(ctx, f"{name}_step")
        turned, placed = c.sem(ctx, f"{name}_turned"), c.sem(ctx, f"{name}_placed")
        stored = c.sem(ctx, f"{name}_stored")
        ss, rstd, gain = c.small[:, 0:8], c.small[:, 8:16], c.small[:, 16:24]
        block = ctx.enter_context(nc.Block())
        srcv = src.rearrange("p (t d) -> p t d", t=TT)
        xnv = xn.rearrange("p (t d) -> p t d", t=TT)
        dstv = dst.rearrange("p (k s) -> p k s", k=KC)

        @block.sync
        def _(sp):
            with nc.allow_non_contiguous_dma(reason="a gain vector by chunks"):
                sp.dma_start(gain, gain_dram.rearrange("(k p) -> p k", p=P)).then_inc(loaded[0], 16)
            if src_dram is not None:
                rows = src_dram.rearrange("(t p) d -> p t d", p=P)
                for t in range(2):
                    sp.dma_start(srcv[:, 4 * t:4 * t + 4, :], rows[:, 4 * t:4 * t + 4, :])\
                        .then_inc(loaded[t], 16)
            if xn_dram is not None:
                rows = xn_dram.rearrange("(t p) d -> p t d", p=P)
                for t in range(TT):
                    sp.wait_ge(step, 3 + t)
                    sp.dma_start(rows[:, t, :], xnv[:, t, :]).then_inc(stored, 16)
                sp.wait_ge(stored, 16 * TT)
            if also is not None:
                sp.wait_ge(*also)

        @block.scalar
        def _(act):
            for t in range(TT):
                if src_dram is not None and t % 4 == 0:
                    act.wait_ge(loaded[t // 4], 32 if t == 0 else 16)
                nc.scalar.activation(xnv[:, t, :], srcv[:, t, :], ACT.Square,
                                     accum_out=ss[:, t:t + 1]).then_inc(squared, 1)
            act.wait_ge(step, 1)
            nc.scalar.activation(rstd, rstd, ACT.Sqrt).then_inc(rooted, 1)

        @block.vector
        def _(dve):
            st = Steps(dve, step)
            dve.wait_ge(squared, TT)
            st.done(nc.vector.tensor_scalar(rstd, ss, 1.0 / D, EPS, ALU.mult, ALU.add))
            dve.wait_ge(rooted, 1)
            st.then_wait(nc.vector.reciprocal(rstd, rstd))
            for t in range(TT):
                st.done(nc.vector.tensor_scalar(xnv[:, t, :], srcv[:, t, :], rstd[:, t:t + 1], None,
                                                ALU.mult))
            dve.wait_ge(loaded[0], 16 if src_dram is None else 32)
            for n in range(2 * TT):
                t, h = divmod(n, 2)
                dve.wait_ge(turned, n + 1)
                nc.vector.tensor_tensor(
                    dstv[:, 4 * h:4 * h + 4, t * P:(t + 1) * P],
                    c.ps[:, n % 8, :].rearrange("p (k s) -> p k s", k=4),
                    gain[:, 4 * h:4 * h + 4].unsqueeze(2).to_broadcast([P, 4, P]),
                    ALU.mult).then_inc(placed, 1)

        @block.tensor
        def _(pe):
            for n in range(2 * TT):
                t, h = divmod(n, 2)
                pe.wait_ge(step, 3 + t)
                if n >= 8:
                    pe.wait_ge(placed, n - 7)
                for k in range(4):
                    kk = 4 * h + k
                    mm = nc.tensor.transpose(c.ps[:, n % 8, k * P:(k + 1) * P],
                                             xnv[:, t, kk * P:(kk + 1) * P], c.ident[:])
                mm.then_inc(turned, 1)


def phase_xbc(c, hT, w_in, conv_w, conv_b, tok, bcT, temps, wslots):
    nc = c.nc
    NB = XBC // P
    hv = hT.rearrange("p (k s) -> p k s", k=KC)
    tokv = tok.rearrange("p (t n) -> p t n", t=TT)
    u = [temps[:, s * 1028:s * 1028 + CONV - 1 + SEQ] for s in range(2)]
    acc = [temps[:, 2056 + s * SEQ:2056 + (s + 1) * SEQ] for s in range(2)]
    act_out = [temps[:, 4104 + s * SEQ:4104 + (s + 1) * SEQ] for s in range(2)]
    w = [wslots[:, s * D:(s + 1) * D].rearrange("p (k n) -> p k n", k=KC) for s in range(2)]
    taps = c.small[:, 0:NB * CONV].rearrange("p (j b) -> p j b", j=CONV)
    bias = c.small[:, 64:64 + NB]
    wv = cols(w_in)
    with ExitStack() as ctx:
        params = c.sem(ctx, "xbc_params")
        wload = [c.sem(ctx, f"xbc_wload{s}") for s in range(2)]
        projected = c.sem(ctx, "xbc_projected")
        evacuated = c.sem(ctx, "xbc_evacuated")
        convolved = c.sem(ctx, "xbc_convolved")
        silued = c.sem(ctx, "xbc_silued")
        turned = c.sem(ctx, "xbc_turned")
        placed = c.sem(ctx, "xbc_placed")
        kept = c.sem(ctx, "xbc_kept")
        tapped = c.sem(ctx, "xbc_tapped")
        block = ctx.enter_context(nc.Block())

        @block.sync
        def _(sp):
            with nc.allow_non_contiguous_dma(reason="per-channel vectors by chunks"):
                for j in range(CONV):
                    sp.dma_start(taps[:, j, :], conv_w[j].rearrange("(b p) -> p b", p=P))\
                        .then_inc(params, 16)
                sp.dma_start(bias, conv_b.rearrange("(b p) -> p b", p=P)).then_inc(params, 16)
            for s in range(2):
                sp.dma_start(w[s], wv[:, :, C_XBC + s * P:C_XBC + (s + 1) * P]).then_inc(wload[s], 16)
            with sp.Fori(1, NB // 2) as i:
                for s in range(2):
                    sp.wait_ge(projected, i * 2 + (s - 1))
                    sp.dma_start(w[s], wv[:, :, bass.ds(i * (2 * P) + (C_XBC + s * P), P)])\
                        .then_inc(wload[s], 16)

        @block.tensor
        def _(pe):
            def transposes(i, s):
                pe.wait_ge(silued, i * 2 + (s + 3))
                pe.wait_ge(placed, i * 2 + (s + 1))
                for t in range(TT):
                    mm = nc.tensor.transpose(
                        c.ps[:, 4 + 2 * s + t // 4, (t % 4) * P:(t % 4 + 1) * P],
                        act_out[s][:, t * P:(t + 1) * P], c.ident[:])
                mm.then_inc(turned, 1)

            def project(i, s):
                pe.wait_ge(wload[s], i * 16 + 16)
                pe.wait_ge(evacuated, i * 2 + (s + 1))
                for k in range(KC):
                    for h in range(2):
                        mm = nc.tensor.matmul(c.ps[:, 2 * s + h, :], w[s][:, k, :],
                                              hv[:, k, h * BANK:(h + 1) * BANK],
                                              start=(k == 0), stop=(k == KC - 1))
                mm.then_inc(projected, 1)

            pe.sem_inc(turned, 2)
            project(0, 0)
            with pe.Fori(0, NB // 2 - 1) as i:
                project(i, 1)
                transposes(i, 0)
                project(i + 1, 0)
                transposes(i, 1)
            project(NB // 2 - 1, 1)
            transposes(NB // 2 - 1, 0)
            transposes(NB // 2 - 1, 1)

        @block.scalar
        def _(act):
            def evacuate(i, s):
                act.wait_ge(projected, i * 2 + (s + 1))
                act.wait_ge(convolved, i * 2 + (s + 1))
                nc.scalar.activation(u[s][:, CONV - 1:],
                                     c.ps[:, 2 * s:2 * s + 2, :].rearrange("p b n -> p (b n)"),
                                     ACT.Identity).then_inc(evacuated, 1)

            def silu(i, s):
                act.wait_ge(convolved, i * 2 + (s + 3))
                act.wait_ge(turned, i * 2 + (s + 1))
                act.wait_ge(kept, i * 2 + (s + 1))
                nc.scalar.activation(act_out[s], acc[s], ACT.Silu).then_inc(silued, 1)

            act.sem_inc(evacuated, 2)
            evacuate(0, 0)
            with act.Fori(0, NB // 2 - 1) as i:
                evacuate(i, 1)
                silu(i, 0)
                evacuate(i + 1, 0)
                silu(i, 1)
            evacuate(NB // 2 - 1, 1)
            silu(NB // 2 - 1, 0)
            silu(NB // 2 - 1, 1)

        @block.vector
        def _(dve):
            def convolve(i, s):
                dve.wait_ge(evacuated, i * 2 + (s + 3))
                dve.wait_ge(silued, i * 2 + (s + 1))
                tap = lambda j: taps[:, j, bass.ds(i * 2 + s, 1)]
                base = 3 * s
                nc.vector.tensor_scalar(acc[s], u[s][:, 3:3 + SEQ], tap(3),
                                        bias[:, bass.ds(i * 2 + s, 1)], ALU.mult, ALU.add)\
                    .then_inc(tapped, 1)
                for j in (2, 1, 0):
                    dve.wait_ge(tapped, i * 6 + (base + 3 - j))
                    x = nc.vector.scalar_tensor_tensor(out=acc[s], in0=u[s][:, j:j + SEQ],
                                                       scalar=tap(j), in1=acc[s], op0=ALU.mult,
                                                       op1=ALU.add)
                    x.then_inc(tapped if j else convolved, 1)

            def place(i, s):
                dve.wait_ge(turned, i * 2 + (s + 3))
                nc.vector.tensor_copy(tokv[:, :, bass.ds(i * (2 * P) + s * P, P)],
                                      c.ps[:, 4 + 2 * s:6 + 2 * s, :]
                                      .rearrange("p b (t n) -> p (b t) n", t=4)).then_inc(placed, 1)

            dve.sem_inc(silued, 2)
            dve.sem_inc(placed, 2)
            for s in range(2):
                nc.vector.memset(u[s][:, 0:CONV - 1], 0.0).then_inc(convolved, 1)
            dve.wait_ge(convolved, 2)
            dve.wait_ge(params, 16 * (CONV + 1))
            convolve(0, 0)
            with dve.Fori(0, NB // 2 - 1) as i:
                convolve(i, 1)
                place(i, 0)
                convolve(i + 1, 0)
                place(i, 1)
            convolve(NB // 2 - 1, 1)
            place(NB // 2 - 1, 0)
            place(NB // 2 - 1, 1)

        @block.gpsimd
        def _(pool):
            pool.sem_inc(kept, 2)
            pool.sem_inc(kept, D // P)
            first = D // P // 2
            with pool.Fori(first, NB // 2) as i:
                for s in range(2):
                    pool.wait_ge(silued, i * 2 + (s + 3))
                    nc.gpsimd.tensor_copy(bcT[:, bass.ds((i - first) * (2 * SEQ) + s * SEQ, SEQ)],
                                          act_out[s]).then_inc(kept, 1)


def bcast(row, n):
    return row.rearrange("(a n) -> a n", a=1).to_broadcast([P, n])


class Decays:

    def __init__(self, c):
        take = lambda n: c.small[:, P * (n + 1):P * (n + 2)]
        self.dt, self.ncs, self.ecs, self.dte, self.cdec, self.dta = (take(n) for n in range(6))
        self.skip = c.small[:, 7 * P:7 * P + HEADS]


def phase_decays(c, hT, w_in, dt_bias, a_log, d_skip, fgate_b, fcum_dram, tmp):
    nc = c.nc
    n2 = 2 * HEADS
    W = TT * n2
    d = Decays(c)
    hv = hT.rearrange("p (k s) -> p k s", k=KC)
    w = tmp[:, 0:KC * n2].rearrange("p (k n) -> p k n", k=KC)
    wide = lambda j: tmp[:, 256 + j * W:256 + (j + 1) * W]
    v3 = lambda ap: ap.rearrange("p (t n) -> p t n", t=TT)
    x, ax, e, u1, ln, eq, res = (wide(j) for j in range(7))
    bias = tmp[:, 2048:2048 + n2]
    a_neg = tmp[:, 2080:2080 + HEADS]
    run = tmp[0:HEADS, 4096:4096 + SEQ]
    one_row = tmp[0:HEADS, 5120:5120 + SEQ]
    fT = tmp[0:HEADS, 6144:6144 + SEQ]
    heads = lambda t, lo: v3(t)[:, :, lo:lo + HEADS]
    with ExitStack() as ctx:
        loaded, logits = c.sem(ctx, "dec_loaded"), c.sem(ctx, "dec_logits")
        step, act_step = c.sem(ctx, "dec_step"), c.sem(ctx, "dec_act")
        summed, turned = c.sem(ctx, "dec_summed"), c.sem(ctx, "dec_turned")
        stored = c.sem(ctx, "dec_stored")
        block = ctx.enter_context(nc.Block())

        @block.sync
        def _(sp):
            wv = cols(w_in)
            with nc.allow_non_contiguous_dma(reason="narrow columns and broadcasts, once"):
                sp.dma_start(w[:, :, 0:HEADS], wv[:, :, C_DT:C_DT + HEADS]).then_inc(loaded, 16)
                sp.dma_start(w[:, :, HEADS:n2], wv[:, :, C_F:C_F + HEADS]).then_inc(loaded, 16)
                sp.dma_start(bias[:, 0:HEADS], bcast(dt_bias, HEADS)).then_inc(loaded, 16)
                sp.dma_start(bias[:, HEADS:n2], bcast(fgate_b, HEADS)).then_inc(loaded, 16)
                sp.dma_start(a_neg, bcast(a_log, HEADS)).then_inc(loaded, 16)
                sp.dma_start(d.skip, bcast(d_skip, HEADS)).then_inc(loaded, 16)
            sp.wait_ge(step, RUN_DONE)
            sp.dma_start(fcum_dram, run).then_inc(stored, 16)
            sp.wait_ge(stored, 16)

        @block.tensor
        def _(pe):
            pe.wait_ge(loaded, 96)
            for t in range(TT):
                for k in range(KC):
                    mm = nc.tensor.matmul(c.ps[:, 0, t * n2:(t + 1) * n2], hv[:, k, t * P:(t + 1) * P],
                                          w[:, k, :], start=(k == 0), stop=(k == KC - 1))
            mm.then_inc(logits, 1)
            pe.wait_ge(step, DTA_DONE)
            nc.tensor.matmul(c.ps[:, 1, 0:P], c.upto[:], d.dta, start=True, stop=True)
            nc.tensor.matmul(c.ps[:, 2, 0:P], c.ones[:], d.dta, start=True, stop=True)\
                .then_inc(summed, 1)
            for t in range(TT):
                mm = nc.tensor.transpose(c.ps[0:HEADS, 3 + t // 4, (t % 4) * P:(t % 4 + 1) * P],
                                         heads(res, HEADS)[:, t, :], c.ident[:])
            mm.then_inc(turned, 1)

        @block.scalar
        def _(act):
            act.wait_ge(loaded, 96)
            nc.scalar.activation(a_neg, a_neg, ACT.Exp).then_inc(act_step, 1)
            act.wait_ge(step, 3)
            nc.scalar.activation(e, ax, ACT.Exp, scale=-1.0).then_inc(act_step, 1)
            act.wait_ge(step, 4)
            nc.scalar.activation(ln, u1, ACT.Ln).then_inc(act_step, 1)
            act.wait_ge(step, DECAY_ARGS)
            nc.scalar.activation(d.ecs, d.ncs, ACT.Exp, scale=-1.0).then_inc(act_step, 1)
            nc.scalar.activation(d.dte, d.dte, ACT.Exp).then_inc(act_step, 1)
            nc.scalar.activation(d.cdec, d.cdec, ACT.Exp).then_inc(act_step, 1)

        @block.vector
        def _(dve):
            st = Steps(dve, step)
            V = nc.vector
            dve.wait_ge(logits, 1)
            psv = c.ps[:, 0, 0:W]
            b = lambda t, n: t.unsqueeze(1).to_broadcast([P, TT, n])
            st.then_wait(V.tensor_tensor(v3(x), v3(psv), b(bias, n2), ALU.add))
            st.then_wait(V.tensor_scalar(heads(x, HEADS), heads(x, HEADS), -1.0, None, ALU.mult))
            st.then_wait(V.scalar_tensor_tensor(out=ax, in0=x, scalar=-1.0, in1=x, op0=ALU.mult,
                                                op1=ALU.max))
            dve.wait_ge(act_step, 2)
            st.then_wait(V.tensor_scalar(u1, e, 1.0, None, ALU.add))
            st.then_wait(V.tensor_scalar(eq, u1, 1.0, None, ALU.is_equal))
            st.then_wait(V.scalar_tensor_tensor(out=ax, in0=u1, scalar=-1.0, in1=eq, op0=ALU.add,
                                                op1=ALU.add))
            st.then_wait(V.reciprocal(ax, ax))
            dve.wait_ge(act_step, 3)
            st.then_wait(V.tensor_tensor(ln, ln, eq, ALU.add))
            st.then_wait(V.tensor_tensor(ln, ln, ax, ALU.mult))
            st.then_wait(V.tensor_tensor(ln, ln, e, ALU.mult))
            st.then_wait(V.scalar_tensor_tensor(out=res, in0=x, scalar=0.0, in1=ln, op0=ALU.max,
                                                op1=ALU.add))
            st.then_wait(V.tensor_scalar(a_neg, a_neg, -1.0, None, ALU.mult))
            st.done(V.tensor_copy(v3(d.dt), heads(res, 0)))
            st.done(V.tensor_tensor(v3(d.dta), heads(res, 0), b(a_neg, HEADS), ALU.mult))
            assert st.n == DTA_DONE
            st.done(V.memset(one_row, 1.0))
            dve.wait_ge(summed, 1)
            st.then_wait(V.tensor_scalar(d.ncs, c.ps[:, 1, 0:P], -1.0, None, ALU.mult))
            st.done(V.tensor_tensor(d.dte, c.ps[:, 2, 0:P], d.ncs, ALU.add))
            st.done(V.tensor_copy(d.cdec, c.ps[:, 2, 0:P]))
            assert st.n == DECAY_ARGS
            dve.wait_ge(turned, 1)
            st.then_wait(V.tensor_scalar(fT, c.ps[0:HEADS, 3:5, :].rearrange("p b n -> p (b n)"),
                                         float(HD) ** 0.5, None, ALU.mult))
            st.done(V.tensor_tensor_scan(run, one_row, fT, 0.0, ALU.mult, ALU.add))
            assert st.n == RUN_DONE
            dve.wait_ge(act_step, 5)
            st.then_wait(V.tensor_tensor(d.dte, d.dte, d.dt, ALU.mult))


DTA_DONE, DECAY_ARGS, RUN_DONE = 14, 18, 20


def phase_ssd(c, tok, bcT, y, tmp):
    nc = c.nc
    d = Decays(c)
    tokv = tok.rearrange("p (t n) -> p t n", t=TT)
    bcv = bcT.rearrange("p (b s) -> p b s", b=2 * GROUPS)
    N = HPG * P
    take = lambda a, n=512: tmp[:, a:a + n]
    decayed_in = [take(0), take(512)]
    dec = [take(1024), take(1536)]
    bTc, cTc, btok = take(2048), take(2560), take(3072)
    xdt, xde = take(3584, 1024), take(4608, 1024)
    prev, skipped = take(5632, 1024), take(6656, 1024)
    hv = lambda ap: ap.rearrange("p (h n) -> p h n", n=HD)
    with ExitStack() as ctx:
        S = lambda n: c.sem(ctx, "ssd_" + n)
        staged = S("staged")
        laid = S("laid")
        cb = S("cb")
        spread = S("spread")
        decayed = S("decayed")
        weighted = S("weighted")
        scaled = S("scaled")
        y_off, y_diag = S("y_off"), S("y_diag")
        state = S("state")
        skip = S("skip")
        part = S("part")
        carried = S("carried")
        summed = S("summed")
        block = ctx.enter_context(nc.Block())

        @block.scalar
        def _(act):
            act.sem_inc(y_diag, 4)
            act.sem_inc(state, 1)
            act.sem_inc(y_off, 1)
            with act.Fori(0, TT) as i:
                act.wait_ge(state, i + 1)
                for dst, src in ((bTc.rearrange("p (g s) -> p g s", g=4), bcv[:, 0:4, bass.ds(i * P, P)]),
                                 (cTc.rearrange("p (g s) -> p g s", g=4), bcv[:, 4:8, bass.ds(i * P, P)]),
                                 (btok, tokv[:, bass.ds(i, 1), D:D + 512].rearrange("p a n -> p (a n)"))):
                    nc.scalar.activation(dst, src, ACT.Identity).then_inc(staged, 1)
                for g in range(GROUPS):
                    act.wait_ge(spread, i * 4 + (g + 5))
                    act.wait_ge(y_diag, i * 4 + (g + 3))
                    for r in range(HPG):
                        h = g * HPG + r
                        x = nc.scalar.activation(dec[g % 2][:, r * P:(r + 1) * P],
                                                 c.ps[:, 1 + g % 2, r * P:(r + 1) * P], ACT.Exp,
                                                 bias=d.ncs[:, bass.ds(i * HEADS + h, 1)])
                    x.then_inc(decayed, 1)

        @block.gpsimd
        def _(pool):
            pool.sem_inc(spread, 4)
            with pool.Fori(0, TT) as i:
                for g in range(GROUPS):
                    pool.wait_ge(spread, i * 4 + (g + 3))
                    nc.gpsimd.tensor_tensor(
                        decayed_in[g % 2].rearrange("p (r l) -> p r l", r=HPG),
                        c.upto[:].unsqueeze(1).to_broadcast([P, HPG, P]),
                        d.dta[:, bass.ds(i * HEADS + g * HPG, HPG)].unsqueeze(2)
                        .to_broadcast([P, HPG, P]), ALU.mult).then_inc(laid, 1)
                pool.wait_ge(summed, i + 1)
                nc.gpsimd.tensor_tensor(
                    hv(skipped), hv(tokv[:, bass.ds(i, 1), 0:D].rearrange("p a n -> p (a n)")),
                    d.skip.unsqueeze(2).to_broadcast([P, HEADS, HD]), ALU.mult).then_inc(skip, 1)

        @block.tensor
        def _(pe):
            with pe.Fori(0, TT) as i:
                pe.wait_ge(staged, i * 3 + 3)
                pe.wait_ge(weighted, i * 4 + 4)
                pe.wait_ge(carried, i + 1)
                for g in range(GROUPS):
                    mm = nc.tensor.matmul(c.ps[:, 0, g * P:(g + 1) * P], bTc[:, g * P:(g + 1) * P],
                                          cTc[:, g * P:(g + 1) * P], start=True, stop=True)
                mm.then_inc(cb, 1)

                def running(g):
                    pe.wait_ge(laid, i * 4 + (g + 1))
                    pe.wait_ge(decayed, i * 4 + (g + 3))
                    bank = c.ps[:, 1 + g % 2, :]
                    nc.tensor.matmul(bank, c.identb[:], c.maskTb[:].rearrange("p r l -> p (r l)"),
                                     start=True, stop=False, skip_group_check=True)
                    nc.tensor.matmul(bank, c.ones[:], decayed_in[g % 2], start=False, stop=True,
                                     skip_group_check=True).then_inc(spread, 1)

                def diagonal(g):
                    pe.wait_ge(weighted, i * 4 + (g + 5))
                    for r in range(HPG):
                        h = g * HPG + r
                        mm = nc.tensor.matmul(c.ps[:, 3 + h // 8, (h % 8) * HD:(h % 8 + 1) * HD],
                                              dec[g % 2][:, r * P:(r + 1) * P],
                                              xdt[:, h * HD:(h + 1) * HD], start=True, stop=True)
                    mm.then_inc(y_diag, 1)

                running(0)
                running(1)
                pe.wait_ge(summed, i + 1)
                for g in range(GROUPS):
                    mm = nc.tensor.matmul(c.ps[:, 5 + g // 2, (g % 2) * 256:(g % 2 + 1) * 256],
                                          cTc[:, g * P:(g + 1) * P],
                                          prev[:, g * 256:(g + 1) * 256], start=True, stop=True)
                mm.then_inc(y_off, 1)
                running(2)
                pe.wait_ge(scaled, i * 2 + 2)
                diagonal(0)
                running(3)
                for g in range(1, GROUPS):
                    diagonal(g)
                for g in range(GROUPS):
                    mm = nc.tensor.matmul(c.ps[:, (7, 0)[g // 2], (g % 2) * 256:(g % 2 + 1) * 256],
                                          btok[:, g * P:(g + 1) * P],
                                          xde[:, g * 256:(g + 1) * 256], start=True, stop=True)
                mm.then_inc(state, 1)

        @block.vector
        def _(dve):
            V = nc.vector
            dve.sem_inc(decayed, 4)
            dve.sem_inc(weighted, 4)
            dve.sem_inc(summed, 1)
            dve.sem_inc(part, 1)
            V.memset(prev, 0.0).then_inc(carried, 1)
            with dve.Fori(0, TT) as i:
                xs = hv(tokv[:, bass.ds(i, 1), 0:D].rearrange("p a n -> p (a n)"))
                col = lambda t: t[:, bass.ds(i * HEADS, HEADS)].unsqueeze(2)\
                    .to_broadcast([P, HEADS, HD])
                dve.wait_ge(state, i + 1)
                V.tensor_tensor(hv(xdt), xs, col(d.dt), ALU.mult).then_inc(scaled, 1)
                V.tensor_tensor(hv(xde), xs, col(d.dte), ALU.mult).then_inc(scaled, 1)
                dve.wait_ge(cb, i + 1)
                for g in range(GROUPS):
                    dve.wait_ge(decayed, i * 4 + (g + 5))
                    m = dec[g % 2].rearrange("p (r l) -> p r l", r=HPG)
                    V.tensor_tensor(m, m, c.ps[:, 0, g * P:(g + 1) * P].unsqueeze(1)
                                    .to_broadcast([P, HPG, P]), ALU.mult).then_inc(weighted, 1)
                dve.wait_ge(y_off, i + 2)
                yc = y[:, bass.ds(i * D, D)]
                flat = lambda b: c.ps[:, b:b + 2, :].rearrange("p b n -> p (b n)")
                V.tensor_tensor(hv(yc), hv(flat(5)), col(d.ecs), ALU.mult).then_inc(part, 1)
                dve.wait_ge(carried, i + 1)
                V.tensor_tensor(hv(prev), hv(prev), col(d.cdec), ALU.mult).then_inc(part, 1)
                dve.wait_ge(part, i * 4 + 3)
                dve.wait_ge(y_diag, i * 4 + 8)
                V.tensor_tensor(yc, yc, flat(3), ALU.add).then_inc(part, 1)
                dve.wait_ge(state, i + 2)
                V.tensor_tensor(prev[:, 0:512], prev[:, 0:512], c.ps[:, 7, :], ALU.add)\
                    .then_inc(part, 1)
                V.tensor_tensor(prev[:, 512:1024], prev[:, 512:1024], c.ps[:, 0, :], ALU.add)\
                    .then_inc(carried, 1)
                dve.wait_ge(part, i * 4 + 5)
                dve.wait_ge(skip, i + 1)
                V.tensor_tensor(yc, yc, skipped, ALU.add).then_inc(summed, 1)


def phase_dense(c, name, jobs, wslots):
    nc = c.nc
    last_use = len(jobs)
    with ExitStack() as ctx:
        wload = [c.sem(ctx, f"{name}_wload{s}") for s in range(2)]
        product = c.sem(ctx, f"{name}_product")
        by_act = c.sem(ctx, f"{name}_by_act")
        by_vec = c.sem(ctx, f"{name}_by_vec")
        multiplied = c.sem(ctx, f"{name}_multiplied")
        block = ctx.enter_context(nc.Block())
        kc = [j[1].shape[1] for j in jobs]
        w = [wslots[n % 2][:, 0:kc[n] * BANK].rearrange("p (k n) -> p k n", k=kc[n])
             for n in range(last_use)]
        on_act = [j[2] == "act" for j in jobs]
        before = lambda n, act: TT * sum(1 for x in on_act[:n] if x == act)

        @block.sync
        def _(sp):
            for n, job in enumerate(jobs):
                if n >= 2:
                    sp.wait_ge(product, TT * (n - 1))
                sp.dma_start(w[n], job[1]).then_inc(wload[n % 2], 16)

        @block.tensor
        def _(pe):
            for n, job in enumerate(jobs):
                pe.wait_ge(wload[n % 2], 16 * (n // 2 + 1))
                for t in range(TT):
                    if n >= 1:
                        pe.wait_ge(by_act if on_act[n - 1] else by_vec,
                                   before(n - 1, on_act[n - 1]) + t + 1)
                    for k in range(kc[n]):
                        mm = nc.tensor.matmul(c.ps[:, t, :], job[0][:, k, t * P:(t + 1) * P],
                                              w[n][:, k, :], start=(k == 0), stop=(k == kc[n] - 1))
                    mm.then_inc(product, 1)

        @block.scalar
        def _(act):
            for n, (_, _, kind, dst, func) in enumerate(jobs):
                if kind == "act":
                    for t in range(TT):
                        act.wait_ge(product, TT * n + t + 1)
                        nc.scalar.activation(dst[:, t, :], c.ps[:, t, :], func).then_inc(by_act, 1)

        @block.vector
        def _(dve):
            pairs = 0
            for n, (_, _, kind, dst, other) in enumerate(jobs):
                if kind == "act":
                    continue
                if before(n, True):
                    dve.wait_ge(by_act, before(n, True))
                for t in range(TT):
                    dve.wait_ge(product, TT * n + t + 1)
                    src = c.ps[:, t, :]
                    if kind == "mul":
                        x = nc.vector.tensor_tensor(dst[:, t, :], src, other[:, t, :], ALU.mult)
                    elif kind == "add":
                        x = nc.vector.tensor_tensor(dst[:, t, :], src, dst[:, t, :], ALU.add)
                    else:
                        nc.vector.tensor_tensor(other[:, t, :], src, other[:, t, :], ALU.mult)\
                            .then_inc(multiplied, 1)
                        pairs += 1
                        dve.wait_ge(multiplied, pairs)
                        x = nc.vector.tensor_tensor(dst[:, t, :], other[:, t, :], dst[:, t, :],
                                                    ALU.add)
                    x.then_inc(by_vec, 1)


def phase_turn(c, name, src, dst, gate=None, groups=0, gain_dram=None, gain_times=1.0, width=D):
    nc = c.nc
    n_k = width // P
    gw = width // max(groups, 1)
    sv = src.rearrange("p (t d) -> p t d", t=TT)
    gv = gate.rearrange("p (t d) -> p t d", t=TT) if gate is not None else None
    dv = dst.rearrange("p (k s) -> p k s", k=n_k)
    ng = max(groups, 1)
    ss = c.small[:, 0:TT * ng]
    rstd, gain = c.small[:, 32:32 + TT * ng], c.small[:, 64:64 + n_k]
    with ExitStack() as ctx:
        loaded, squared = c.sem(ctx, f"{name}_loaded"), c.sem(ctx, f"{name}_squared")
        gated, rooted = c.sem(ctx, f"{name}_gated"), c.sem(ctx, f"{name}_rooted")
        step, ready = c.sem(ctx, f"{name}_step"), c.sem(ctx, f"{name}_ready")
        turned, placed = c.sem(ctx, f"{name}_turned"), c.sem(ctx, f"{name}_placed")
        block = ctx.enter_context(nc.Block())
        halves = n_k // 4

        @block.sync
        def _(sp):
            if gain_dram is not None:
                with nc.allow_non_contiguous_dma(reason="a gain vector by chunks"):
                    g = gain_dram.rearrange("(k p) -> p k", p=P)
                    if g.shape[1] == 1 and n_k > 1:
                        for k in range(n_k):
                            sp.dma_start(gain[:, k:k + 1], g).then_inc(loaded, 16)
                    else:
                        sp.dma_start(gain, g).then_inc(loaded, 16)

        loads = 0 if gain_dram is None else (16 * n_k if gain_dram.shape[0] == P else 16)

        @block.scalar
        def _(act):
            if groups:
                for t in range(TT):
                    if gate is not None:
                        act.wait_ge(gated, t + 1)
                    for g in range(groups):
                        nc.scalar.activation(dst[:, t * width + g * gw:t * width + (g + 1) * gw],
                                             sv[:, t, g * gw:(g + 1) * gw], ACT.Square,
                                             accum_out=ss[:, t * ng + g:t * ng + g + 1])\
                            .then_inc(squared, 1)
                act.wait_ge(step, 1)
                nc.scalar.activation(rstd, rstd, ACT.Sqrt).then_inc(rooted, 1)

        @block.vector
        def _(dve):
            V = nc.vector
            if gate is not None:
                for t in range(TT):
                    V.tensor_tensor(sv[:, t, :], sv[:, t, :], gv[:, t, :], ALU.mult).then_inc(gated, 1)
            if groups:
                st = Steps(dve, step)
                dve.wait_ge(squared, TT * groups)
                st.done(V.tensor_scalar(rstd, ss, 1.0 / gw, EPS, ALU.mult, ALU.add))
                dve.wait_ge(rooted, 1)
                st.then_wait(V.reciprocal(rstd, rstd))
                for t in range(TT):
                    row = sv[:, t, :].rearrange("p (g n) -> p g n", g=groups)
                    V.tensor_tensor(row, row, rstd[:, t * ng:(t + 1) * ng].unsqueeze(2)
                                    .to_broadcast([P, groups, gw]), ALU.mult).then_inc(ready, 1)
            if gain_dram is not None:
                dve.wait_ge(loaded, loads)
                if gain_times != 1.0:
                    V.tensor_scalar(gain, gain, gain_times, None, ALU.mult).then_inc(loaded, 16)
                    dve.wait_ge(loaded, loads + 16)
            for n in range(halves * TT):
                t, h = divmod(n, halves)
                dve.wait_ge(turned, n + 1)
                out = dv[:, 4 * h:4 * h + 4, t * P:(t + 1) * P]
                ps = c.ps[:, n % 8, :].rearrange("p (k s) -> p k s", k=4)
                if gain_dram is None:
                    x = V.tensor_copy(out, ps)
                else:
                    x = V.tensor_tensor(out, ps, gain[:, 4 * h:4 * h + 4].unsqueeze(2)
                                        .to_broadcast([P, 4, P]), ALU.mult)
                x.then_inc(placed, 1)

        @block.tensor
        def _(pe):
            for n in range(halves * TT):
                t, h = divmod(n, halves)
                if groups:
                    pe.wait_ge(ready, t + 1)
                elif gate is not None:
                    pe.wait_ge(gated, t + 1)
                if n >= 8:
                    pe.wait_ge(placed, n - 7)
                for k in range(4):
                    mm = nc.tensor.transpose(c.ps[:, n % 8, k * P:(k + 1) * P],
                                             sv[:, t, (4 * h + k) * P:(4 * h + k + 1) * P],
                                             c.ident[:])
                mm.then_inc(turned, 1)


def phase_forget_attention(c, hT, w_in, fcum_dram, v, o, qk, wslots, probs):
    nc = c.nc
    hv = hT.rearrange("p (k s) -> p k s", k=KC)
    vv = v.rearrange("p (t n) -> p t n", t=TT)
    ov = o.rearrange("p (t n) -> p t n", t=TT)
    SCALE = float(HD) ** -0.5
    q = [qk[:, r * SEQ:(r + 1) * SEQ] for r in range(2)]
    k_ = [qk[:, (2 + r) * SEQ:(3 + r) * SEQ] for r in range(2)]
    w = [wslots[:, s * D:(s + 1) * D].rearrange("p (k n) -> p k n", k=KC) for s in range(2)]
    prob = [probs[:, r * SEQ:(r + 1) * SEQ] for r in range(2)]
    probT = [probs[:, (2 + r) * SEQ:(3 + r) * SEQ] for r in range(2)]
    negmax, rowsum, rinv = c.small[:, 1400:1402], c.small[:, 1402:1404], c.small[:, 1404:1406]
    PAIRS = HEADS // 2
    UNITS = [(r, t) for r in range(2) for t in range(TT)]
    NU = len(UNITS)
    GROUPSOF = [(u, g) for u, (r, t) in enumerate(UNITS) for g in range(t // 4 + 1)]
    NGR = len(GROUPSOF)
    first_group = {u: n for n, (u, g) in reversed(list(enumerate(GROUPSOF)))}
    S_BANK, T_BANK, O_BANK = (4, 6), (0, 1), (2, 3)
    with ExitStack() as ctx:
        S = lambda n: c.sem(ctx, "fa_" + n)
        wload = [S("wload0"), S("wload1")]
        sums = S("sums")
        ones_row = S("ones_row")
        projected = S("projected")
        split = S("split")
        scored = S("scored")
        maxed = S("maxed")
        negated = S("negated")
        exped = S("exped")
        turned = S("turned")
        placed = S("placed")
        summed = S("summed")
        inverted = S("inverted")
        normed = S("normed")
        block = ctx.enter_context(nc.Block())

        @block.sync
        def _(sp):
            wv = cols(w_in)
            with sp.Fori(0, PAIRS) as i:
                sp.wait_ge(split, i * 4 + 4)
                sp.dma_start(w[0], wv[:, :, bass.ds(i * P + C_Q, P)]).then_inc(wload[0], 16)
                sp.dma_start(w[1], wv[:, :, bass.ds(i * P + C_K, P)]).then_inc(wload[1], 16)
                sp.wait_ge(summed, i * NU + 2)
                for r in range(2):
                    sp.dma_start(k_[r][HD:HD + 1, :], fcum_dram[bass.ds(i * 2 + r, 1), :])\
                        .then_inc(sums, 16)

        @block.tensor
        def _(pe):
            pe.sem_inc(summed, 2)
            with pe.Fori(0, PAIRS) as i:
                pe.wait_ge(normed, i * NU + 2)
                for j in range(2):
                    pe.wait_ge(wload[j], i * 16 + 16)
                    for k in range(KC):
                        for h in range(2):
                            mm = nc.tensor.matmul(c.ps[:, 2 * j + h, :], w[j][:, k, :],
                                                  hv[:, k, h * BANK:(h + 1) * BANK],
                                                  start=(k == 0), stop=(k == KC - 1))
                    mm.then_inc(projected, 1)
                pe.wait_ge(split, i * 4 + 8)
                pe.wait_ge(sums, i * 32 + 32)

                def score(u):
                    r, t = UNITS[u]
                    n = (t + 1) * P
                    pe.wait_ge(exped, i * NU + (u + 1))
                    for b in range((n + BANK - 1) // BANK):
                        width = min(BANK, n - b * BANK)
                        has_diag = (b + 1) * BANK >= n
                        mm = nc.tensor.matmul(c.ps[:, S_BANK[u % 2] + b, 0:width],
                                              q[r][0:HD + 1, t * P:(t + 1) * P],
                                              k_[r][0:HD + 1, b * BANK:b * BANK + width],
                                              start=True, stop=not has_diag, skip_group_check=True)
                    mm = nc.tensor.matmul(c.ps[:, S_BANK[u % 2] + b, width - P:width],
                                          c.identb[:], c.maskb[:], start=False, stop=True,
                                          skip_group_check=True)
                    mm.then_inc(scored, 1)

                def values(u):
                    r, t = UNITS[u]
                    pe.wait_ge(exped, i * NU + (u + 3))
                    for g in range(t // 4 + 1):
                        n = first_group[u] + g
                        pe.wait_ge(placed, i * NGR + (n + 1))
                        blocks = min(4, t + 1 - 4 * g)
                        for b in range(blocks):
                            mm = nc.tensor.transpose(
                                c.ps[:, T_BANK[n % 2], b * P:(b + 1) * P],
                                prob[u % 2][:, (4 * g + b) * P:(4 * g + b + 1) * P], c.ident[:])
                        mm.then_inc(turned, 1)
                    pe.wait_ge(normed, i * NU + (u + 1))
                    pe.wait_ge(placed, i * NGR + (first_group[u] + t // 4 + 3))
                    for b in range(t + 1):
                        mm = nc.tensor.matmul(c.ps[:, O_BANK[u % 2], 0:HD],
                                              probT[u % 2][:, b * P:(b + 1) * P],
                                              vv[:, b, bass.ds(i * P + r * HD, HD)],
                                              start=(b == 0), stop=(b == t))
                    mm.then_inc(summed, 1)

                score(0)
                for u in range(NU):
                    if u + 1 < NU:
                        score(u + 1)
                    values(u)

        @block.scalar
        def _(act):
            act.sem_inc(exped, 2)
            with act.Fori(0, PAIRS) as i:
                act.wait_ge(projected, i * 2 + 1)
                for r in range(2):
                    nc.scalar.activation(
                        q[r][0:HD, :], c.ps[r * HD:(r + 1) * HD, 0:2, :].rearrange("p b n -> p (b n)"),
                        ACT.Identity).then_inc(split, 1)
                for u, (r, t) in enumerate(UNITS):
                    n = (t + 1) * P
                    act.wait_ge(negated, i * NU + (u + 3))
                    act.wait_ge(summed, i * NU + (u + 1))
                    nc.scalar.activation(
                        prob[u % 2][:, 0:n],
                        c.ps[:, S_BANK[u % 2]:S_BANK[u % 2] + 2, :]
                        .rearrange("p b n -> p (b n)")[:, 0:n], ACT.Exp, scale=SCALE,
                        bias=negmax[:, u % 2:u % 2 + 1],
                        accum_out=rowsum[:, u % 2:u % 2 + 1]).then_inc(exped, 1)

        @block.vector
        def _(dve):
            V = nc.vector
            dve.sem_inc(split, 4)
            dve.sem_inc(negated, 2)
            dve.sem_inc(placed, 2)
            dve.sem_inc(normed, 2)
            for r in range(2):
                V.memset(q[r][HD:HD + 1, :], 1.0).then_inc(ones_row, 1)
            dve.wait_ge(ones_row, 2)
            with dve.Fori(0, PAIRS) as i:
                dve.wait_ge(projected, i * 2 + 2)
                for r in range(2):
                    V.tensor_copy(k_[r][0:HD, :], c.ps[r * HD:(r + 1) * HD, 2:4, :]
                                  .rearrange("p b n -> p (b n)")).then_inc(split, 1)

                def maxima(u):
                    r, t = UNITS[u]
                    n = (t + 1) * P
                    dve.wait_ge(scored, i * NU + (u + 1))
                    dve.wait_ge(exped, i * NU + (u + 1))
                    V.tensor_reduce(negmax[:, u % 2:u % 2 + 1],
                                    c.ps[:, S_BANK[u % 2]:S_BANK[u % 2] + 2, :]
                                    .rearrange("p b n -> p (b n)")[:, 0:n], AX.X, ALU.max)\
                        .then_inc(maxed, 1)
                    dve.wait_ge(maxed, i * NU + (u + 1))
                    V.tensor_scalar(negmax[:, u % 2:u % 2 + 1], negmax[:, u % 2:u % 2 + 1], -SCALE,
                                    None, ALU.mult).then_inc(negated, 1)

                def take(u):
                    r, t = UNITS[u]
                    for g in range(t // 4 + 1):
                        n = first_group[u] + g
                        dve.wait_ge(turned, i * NGR + (n + 1))
                        width = min(4, t + 1 - 4 * g) * P
                        if g == 0:
                            dve.wait_ge(summed, i * NU + (u + 1))
                        V.tensor_copy(probT[u % 2][:, 4 * g * P:4 * g * P + width],
                                      c.ps[:, T_BANK[n % 2], 0:width]).then_inc(placed, 1)

                def norm(u):
                    r, t = UNITS[u]
                    V.reciprocal(rinv[:, u % 2:u % 2 + 1], rowsum[:, u % 2:u % 2 + 1])\
                        .then_inc(inverted, 1)
                    dve.wait_ge(inverted, i * NU + (u + 1))
                    dve.wait_ge(summed, i * NU + (u + 3))
                    V.tensor_scalar(ov[:, t, bass.ds(i * P + r * HD, HD)],
                                    c.ps[:, O_BANK[u % 2], 0:HD], rinv[:, u % 2:u % 2 + 1], None,
                                    ALU.mult).then_inc(normed, 1)

                maxima(0)
                for u in range(NU):
                    if u + 1 < NU:
                        maxima(u + 1)
                    take(u)
                    norm(u)


def phase_post(c, x_dram, gain_dram, src, dst, tmp):
    nc = c.nc
    v = lambda r: r.rearrange("p (t d) -> p t d", t=TT)
    sv, dv = v(src), v(dst)
    gain = tmp[:, 0:D]
    sq = tmp[:, D:2 * D]
    ss, rstd = c.small[:, 0:8], c.small[:, 8:16]
    with ExitStack() as ctx:
        loaded = [c.sem(ctx, f"post_loaded{t}") for t in range(3)]
        squared, rooted = c.sem(ctx, "post_squared"), c.sem(ctx, "post_rooted")
        step = c.sem(ctx, "post_step")
        block = ctx.enter_context(nc.Block())

        @block.sync
        def _(sp):
            sp.dma_start(gain, bcast(gain_dram, D)).then_inc(loaded[2], 16)
            rows = x_dram.rearrange("(t p) d -> p t d", p=P)
            for t in range(2):
                sp.dma_start(dv[:, 4 * t:4 * t + 4, :], rows[:, 4 * t:4 * t + 4, :])\
                    .then_inc(loaded[t], 16)

        @block.scalar
        def _(act):
            for t in range(TT):
                if t:
                    act.wait_ge(squared, t)
                nc.scalar.activation(sq, sv[:, t, :], ACT.Square, accum_out=ss[:, t:t + 1])\
                    .then_inc(squared, 1)
            act.wait_ge(step, 1)
            nc.scalar.activation(rstd, rstd, ACT.Sqrt).then_inc(rooted, 1)

        @block.vector
        def _(dve):
            V = nc.vector
            st = Steps(dve, step)
            dve.wait_ge(squared, TT)
            st.done(V.tensor_scalar(rstd, ss, 1.0 / D, EPS, ALU.mult, ALU.add))
            dve.wait_ge(rooted, 1)
            st.then_wait(V.reciprocal(rstd, rstd))
            dve.wait_ge(loaded[2], 16)
            for t in range(TT):
                st.then_wait(V.scalar_tensor_tensor(out=sv[:, t, :], in0=sv[:, t, :],
                                                    scalar=rstd[:, t:t + 1], in1=gain,
                                                    op0=ALU.mult, op1=ALU.mult))
                if t % 4 == 0:
                    dve.wait_ge(loaded[t // 4], 16)
                st.done(V.tensor_tensor(dv[:, t, :], dv[:, t, :], sv[:, t, :], ALU.add))


def phase_conformer(c, hT, w_in, dw_w, jobs, y, acc, gate, wblk, wslots, raw_taps):
    nc = c.nc
    NB = CCH // P
    PAD = CW - 1
    hv = hT.rearrange("p (k s) -> p k s", k=KC)
    yv = y.rearrange("p (b n) -> p b n", b=NB)
    accv = acc.rearrange("p (b n) -> p b n", b=NB)
    w = [wblk[:, s * D:(s + 1) * D].rearrange("p (k n) -> p k n", k=KC) for s in range(2)]
    taps = c.small[:, 1024:1024 + NB * CW]
    bias = c.small[:, 1160:1160 + NB]
    jw = [wslots[n % 2].rearrange("p (k n) -> p k n", k=KC) for n in range(len(jobs))]
    (dw_w, dw_b) = dw_w
    with ExitStack() as ctx:
        S = lambda n: c.sem(ctx, "cf_" + n)
        params, tap_turned, tap_placed = S("params"), S("tap_turned"), S("tap_placed")
        wload = [S("wload0"), S("wload1")]
        jload = [S("jload0"), S("jload1")]
        projected = S("projected")
        opened = S("opened")
        gated = S("gated")
        tapped = S("tapped")
        padded = S("padded")
        product, taken = S("product"), S("taken")
        block = ctx.enter_context(nc.Block())

        @block.sync
        def _(sp):
            sp.dma_start(raw_taps[0:CW, 0:CCH], dw_w).then_inc(params, 16)
            with nc.allow_non_contiguous_dma(reason="a bias vector by chunks"):
                sp.dma_start(bias, dw_b.rearrange("(b p) -> p b", p=P)).then_inc(params, 16)
            wv = cols(w_in)
            with sp.Fori(0, NB) as i:
                sp.wait_ge(projected, i * 2 + 1)
                sp.dma_start(w[0], wv[:, :, bass.ds(i * P, P)]).then_inc(wload[0], 16)
                sp.wait_ge(projected, i * 2 + 2)
                sp.dma_start(w[1], wv[:, :, bass.ds(i * P + CCH, P)]).then_inc(wload[1], 16)
            sp.wait_ge(tap_turned, 1)
            for n, job in enumerate(jobs):
                if n >= 2:
                    sp.wait_ge(product, TT * (n - 1))
                sp.dma_start(jw[n], job[1]).then_inc(jload[n % 2], 16)

        @block.tensor
        def _(pe):
            pe.wait_ge(params, 32)
            for b in range(NB):
                mm = nc.tensor.transpose(c.ps[:, 7, b * CW:(b + 1) * CW],
                                         raw_taps[0:CW, b * P:(b + 1) * P], c.ident[0:CW, 0:CW])
            mm.then_inc(tap_turned, 1)
            pe.sem_inc(projected, 2)
            with pe.Fori(0, NB) as i:
                for j in range(2):
                    pe.wait_ge(wload[j], i * 16 + 16)
                    pe.wait_ge(gated if j == 0 else opened, i + 1)
                    for k in range(KC):
                        for h in range(2):
                            mm = nc.tensor.matmul(c.ps[:, 2 * j + h, :], w[j][:, k, :],
                                                  hv[:, k, h * BANK:(h + 1) * BANK],
                                                  start=(k == 0), stop=(k == KC - 1))
                    mm.then_inc(projected, 1)
            pe.wait_ge(tap_placed, 1)
            for n, job in enumerate(jobs):
                pe.wait_ge(jload[n % 2], 16 * (n // 2 + 1))
                for t in range(TT):
                    m = n * TT + t
                    if m >= 4:
                        pe.wait_ge(taken, m - 3)
                    for k in range(KC):
                        mm = nc.tensor.matmul(c.ps[:, 4 + t % 4, :], job[0][:, k, t * P:(t + 1) * P],
                                              jw[n][:, k, :], start=(k == 0), stop=(k == KC - 1))
                    mm.then_inc(product, 1)

        @block.scalar
        def _(act):
            act.sem_inc(opened, 1)
            with act.Fori(0, NB) as i:
                act.wait_ge(projected, i * 2 + 4)
                act.wait_ge(gated, i + 1)
                nc.scalar.activation(gate, c.ps[:, 2:4, :].rearrange("p b n -> p (b n)"),
                                     ACT.Sigmoid).then_inc(opened, 1)
            for n, (_, _, _, dst, func) in enumerate(jobs):
                for t in range(TT):
                    act.wait_ge(product, n * TT + t + 1)
                    nc.scalar.activation(dst[:, t, :], c.ps[:, 4 + t % 4, :], func).then_inc(taken, 1)

        @block.vector
        def _(dve):
            V = nc.vector
            dve.wait_ge(tap_turned, 1)
            V.tensor_copy(taps, c.ps[:, 7, 0:NB * CW]).then_inc(tap_placed, 1)
            for b in range(NB):
                V.memset(yv[:, b, 0:PAD], 0.0).then_inc(padded, 1)
            dve.sem_inc(gated, 1)
            dve.wait_ge(tap_placed, 1)
            dve.wait_ge(padded, NB)
            dve.wait_ge(params, 32)
            with dve.Fori(0, NB) as i:
                dve.wait_ge(opened, i + 2)
                row = lambda j, n=SEQ: y[:, bass.ds(i * (SEQ + PAD) + j, n)]
                a_i = acc[:, bass.ds(i * SEQ, SEQ)]
                V.tensor_tensor(row(PAD), c.ps[:, 0:2, :].rearrange("p b n -> p (b n)"), gate,
                                ALU.mult).then_inc(gated, 1)
                dve.wait_ge(gated, i + 2)
                V.tensor_scalar(a_i, row(0), taps[:, bass.ds(i * CW, 1)], bias[:, bass.ds(i, 1)],
                                ALU.mult, ALU.add).then_inc(tapped, 1)
                for j in range(1, CW):
                    dve.wait_ge(tapped, i * CW + j)
                    V.scalar_tensor_tensor(out=a_i, in0=row(j), scalar=taps[:, bass.ds(i * CW + j, 1)],
                                           in1=a_i, op0=ALU.mult, op1=ALU.add).then_inc(tapped, 1)


def phase_channel_norm(c, acc, sq, rstd, g_dram, b_dram):
    nc = c.nc
    NB = CCH // P
    av = acc.rearrange("p (b n) -> p b n", b=NB)
    qv = sq.rearrange("p (b n) -> p b n", b=NB)
    g, b_ = c.small[:, 0:NB], c.small[:, 8:8 + NB]
    flat = lambda b: c.ps[:, b:b + 2, :].rearrange("p b n -> p (b n)")
    with ExitStack() as ctx:
        S = lambda n: c.sem(ctx, "cn_" + n)
        params, meaned, centred, squared = S("params"), S("meaned"), S("centred"), S("squared")
        spread, step, rooted, scaled, done = S("spread"), S("step"), S("rooted"), S("scaled"), S("done")
        block = ctx.enter_context(nc.Block())

        @block.sync
        def _(sp):
            with nc.allow_non_contiguous_dma(reason="per-channel vectors by chunks"):
                sp.dma_start(g, g_dram.rearrange("(b p) -> p b", p=P)).then_inc(params, 16)
                sp.dma_start(b_, b_dram.rearrange("(b p) -> p b", p=P)).then_inc(params, 16)

        @block.tensor
        def _(pe):
            def over_channels(src, bank, ready):
                for b in range(NB):
                    if ready is not None:
                        pe.wait_ge(ready, b + 1)
                    for h in range(2):
                        mm = nc.tensor.matmul(c.ps[:, bank + h, :], c.ones[:],
                                              src[:, b, h * BANK:(h + 1) * BANK],
                                              start=(b == 0), stop=(b == NB - 1))
                return mm
            over_channels(av, 0, None).then_inc(meaned, 1)
            over_channels(qv, 2, squared).then_inc(spread, 1)

        @block.scalar
        def _(act):
            for b in range(NB):
                act.wait_ge(centred, b + 1)
                nc.scalar.activation(qv[:, b, :], av[:, b, :], ACT.Square).then_inc(squared, 1)
            act.wait_ge(step, 1)
            nc.scalar.activation(rstd, rstd, ACT.Sqrt).then_inc(rooted, 1)
            act.wait_ge(params, 32)
            for b in range(NB):
                act.wait_ge(scaled, b + 1)
                nc.scalar.activation(av[:, b, :], av[:, b, :], ACT.Silu, scale=g[:, b:b + 1],
                                     bias=b_[:, b:b + 1]).then_inc(done, 1)

        @block.vector
        def _(dve):
            V = nc.vector
            dve.wait_ge(meaned, 1)
            for b in range(NB):
                V.scalar_tensor_tensor(out=av[:, b, :], in0=flat(0), scalar=-1.0 / CCH, in1=av[:, b, :],
                                       op0=ALU.mult, op1=ALU.add).then_inc(centred, 1)
            dve.wait_ge(spread, 1)
            V.tensor_scalar(rstd, flat(2), 1.0 / CCH, EPS, ALU.mult, ALU.add).then_inc(step, 1)
            dve.wait_ge(rooted, 1)
            V.reciprocal(rstd, rstd).then_inc(step, 1)
            dve.wait_ge(step, 2)
            dve.wait_ge(squared, NB)
            for b in range(NB):
                V.tensor_tensor(av[:, b, :], av[:, b, :], rstd, ALU.mult).then_inc(scaled, 1)


def phase_diff_attention(c, hT, w_in, q_g, k_g, lambdas, v, o, work, tmp):
    nc = c.nc
    hv = hT.rearrange("p (k s) -> p k s", k=KC)
    vv = v.rearrange("p (t n) -> p t n", t=TT)
    ov = o.rearrange("p (t n) -> p t n", t=TT)
    SCALE = float(DHD) ** -0.5
    take = lambda n: work[:, n * SEQ:(n + 1) * SEQ]
    qk = [take(0), take(1)]
    w = [take(2 + j).rearrange("p (k n) -> p k n", k=KC) for j in range(2)]
    prob = [take(4), take(5)]
    probT = [take(6), take(7)]
    sq, root = tmp[:, 0:SEQ], tmp[:, SEQ:2 * SEQ]
    sm = lambda a, n=2: c.small[:, 1400 + a:1400 + a + n]
    negmax, rowsum, rinv, gain, neglam = sm(0), sm(2), sm(4), sm(6), sm(8, 1)
    dots, halves_of = sm(10), c.small[:, 1160:1160 + P]
    lam_rows = tmp[:, 0:4 * DHD].rearrange("p (j n) -> p j n", j=4)
    lam_prod = tmp[:, SEQ:SEQ + 2 * DHD].rearrange("p (j n) -> p j n", j=2)
    GR = [(t, g) for t in range(TT) for g in range(t // 4 + 1)]
    NGR = len(GR)
    first = {t: n for n, (t, g) in reversed(list(enumerate(GR)))}
    flat = lambda b: c.ps[:, b:b + 2, :].rearrange("p b n -> p (b n)")
    with ExitStack() as ctx:
        S = lambda n: c.sem(ctx, "da_" + n)
        params, lam_step, filled = S("params"), S("lam_step"), S("filled")
        wload = [S("wload0"), S("wload1")]
        projected = S("projected")
        squared = S("squared")
        meaned = S("meaned")
        offset, rooted, inverted = S("offset"), S("rooted"), S("inverted")
        normed = S("normed")
        scored = S("scored")
        maxed, negated = S("maxed"), S("negated")
        exped = S("exped")
        weighed = S("weighed")
        combined = S("combined")
        turned, placed = S("turned"), S("placed")
        summed = S("summed")
        stored = S("stored")
        block = ctx.enter_context(nc.Block())

        @block.gpsimd
        def _(pool):
            nc.gpsimd.memset(halves_of, 0.0).then_inc(filled, 1)
            pool.wait_ge(filled, 1)
            for r in range(2):
                nc.gpsimd.memset(halves_of[r * DHD:(r + 1) * DHD, r * DHD:(r + 1) * DHD],
                                 1.0 / DHD).then_inc(filled, 1)

        @block.sync
        def _(sp):
            for j, l in enumerate(lambdas):
                sp.dma_start(lam_rows[:, j, :], bcast(l, DHD)).then_inc(params, 16)
            with nc.allow_non_contiguous_dma(reason="two gain vectors"):
                for j, g in enumerate((q_g, k_g)):
                    for r in range(2):
                        sp.dma_start(gain[r * DHD:(r + 1) * DHD, j:j + 1],
                                     g.rearrange("(p a) -> p a", a=1)).then_inc(params, 16)
            wv = cols(w_in)
            with sp.Fori(0, DH) as i:
                sp.wait_ge(normed, i * 2 + 2)
                sp.dma_start(w[0], wv[:, :, bass.ds(i * P + C2_Q, P)]).then_inc(wload[0], 16)
                sp.dma_start(w[1], wv[:, :, bass.ds(i * P + C2_K, P)]).then_inc(wload[1], 16)

        @block.tensor
        def _(pe):
            pe.sem_inc(summed, 2)
            pe.wait_ge(filled, 3)
            with pe.Fori(0, DH) as i:
                pe.wait_ge(stored, i * TT + 2)
                for j in range(2):
                    pe.wait_ge(wload[j], i * 16 + 16)
                    for k in range(KC):
                        for h in range(2):
                            mm = nc.tensor.matmul(c.ps[:, 2 * j + h, :], w[j][:, k, :],
                                                  hv[:, k, h * BANK:(h + 1) * BANK],
                                                  start=(k == 0), stop=(k == KC - 1))
                    mm.then_inc(projected, 1)
                for j in range(2):
                    pe.wait_ge(squared, i * 2 + (j + 1))
                    for h in range(2):
                        mm = nc.tensor.matmul(c.ps[:, 4 + 2 * j + h, :], halves_of,
                                              sq[:, h * BANK:(h + 1) * BANK], start=True, stop=True)
                    mm.then_inc(meaned, 1)
                pe.wait_ge(normed, i * 2 + 4)

                def score(t):
                    n = (t + 1) * P
                    for r in range(2):
                        pe.wait_ge(exped, i * (2 * TT) + (2 * t + r + 1))
                        rows = slice(r * DHD, (r + 1) * DHD)
                        for b in range((n + BANK - 1) // BANK):
                            width = min(BANK, n - b * BANK)
                            mm = nc.tensor.matmul(c.ps[:, 4 + 2 * r + b, 0:width],
                                                  qk[0][rows, t * P:(t + 1) * P],
                                                  qk[1][rows, b * BANK:b * BANK + width],
                                                  start=True, stop=False, skip_group_check=True)
                        nc.tensor.matmul(c.ps[:, 4 + 2 * r + b, width - P:width], c.identb[:],
                                         c.maskb[:], start=False, stop=True,
                                         skip_group_check=True).then_inc(scored, 1)

                def values(t):
                    pe.wait_ge(combined, i * TT + (t + 2))
                    for g in range(t // 4 + 1):
                        n = first[t] + g
                        pe.wait_ge(placed, i * NGR + (n + 1))
                        for b in range(min(4, t + 1 - 4 * g)):
                            mm = nc.tensor.transpose(c.ps[:, n % 2, b * P:(b + 1) * P],
                                                     prob[0][:, (4 * g + b) * P:(4 * g + b + 1) * P],
                                                     c.ident[:])
                        mm.then_inc(turned, 1)
                    pe.wait_ge(stored, i * TT + (t + 1))
                    pe.wait_ge(placed, i * NGR + (first[t] + t // 4 + 3))
                    for b in range(t + 1):
                        mm = nc.tensor.matmul(c.ps[:, 2 + t % 2, 0:DV],
                                              probT[t % 2][:, b * P:(b + 1) * P],
                                              vv[:, b, bass.ds(i * DV, DV)],
                                              start=(b == 0), stop=(b == t))
                    mm.then_inc(summed, 1)

                score(0)
                for t in range(TT):
                    if t + 1 < TT:
                        score(t + 1)
                    values(t)

        @block.scalar
        def _(act):
            act.wait_ge(lam_step, 2)
            nc.scalar.activation(dots, dots, ACT.Exp).then_inc(lam_step, 1)
            act.sem_inc(exped, 2)
            with act.Fori(0, DH) as i:
                for j in range(2):
                    act.wait_ge(projected, i * 2 + (j + 1))
                    if j:
                        act.wait_ge(meaned, i * 2 + 1)
                    nc.scalar.activation(sq, flat(2 * j), ACT.Square).then_inc(squared, 1)
                    act.wait_ge(offset, i * 2 + (j + 1))
                    nc.scalar.activation(root, root, ACT.Sqrt).then_inc(rooted, 1)
                for t in range(TT):
                    n = (t + 1) * P
                    for r in range(2):
                        act.wait_ge(negated, i * (2 * TT) + (2 * t + r + 1))
                        if r == 0 and t >= 1:
                            act.wait_ge(turned, i * NGR + (first[t - 1] + (t - 1) // 4 + 1))
                        act.wait_ge(combined, i * TT + (t + 1))
                        nc.scalar.activation(prob[r][:, 0:n], flat(4 + 2 * r)[:, 0:n], ACT.Exp,
                                             scale=SCALE, bias=negmax[:, r:r + 1],
                                             accum_out=rowsum[:, r:r + 1]).then_inc(exped, 1)

        @block.vector
        def _(dve):
            V = nc.vector
            dve.wait_ge(params, 16 * 8)
            V.tensor_tensor(lam_prod, lam_rows[:, 0:4:2, :], lam_rows[:, 1:4:2, :], ALU.mult)\
                .then_inc(lam_step, 1)
            dve.wait_ge(lam_step, 1)
            V.tensor_reduce(dots, lam_prod, AX.X, ALU.add).then_inc(lam_step, 1)
            dve.wait_ge(lam_step, 3)
            V.scalar_tensor_tensor(out=neglam, in0=dots[:, 1:2], scalar=-LAM_INIT, in1=dots[:, 0:1],
                                   op0=ALU.add, op1=ALU.subtract).then_inc(lam_step, 1)
            dve.wait_ge(lam_step, 4)
            dve.sem_inc(normed, 2)
            dve.sem_inc(combined, 1)
            dve.sem_inc(placed, 2)
            dve.sem_inc(stored, 2)
            with dve.Fori(0, DH) as i:
                for j in range(2):
                    dve.wait_ge(meaned, i * 2 + (j + 1))
                    V.tensor_scalar(root, flat(4 + 2 * j), 1.0, EPS, ALU.mult, ALU.add)\
                        .then_inc(offset, 1)
                    dve.wait_ge(rooted, i * 2 + (j + 1))
                    V.reciprocal(root, root).then_inc(inverted, 1)
                    dve.wait_ge(inverted, i * 2 + (j + 1))
                    V.scalar_tensor_tensor(out=qk[j], in0=flat(2 * j), scalar=gain[:, j:j + 1],
                                           in1=root, op0=ALU.mult, op1=ALU.mult).then_inc(normed, 1)
                    dve.wait_ge(normed, i * 2 + (j + 3))

                def maxima(t):
                    n = (t + 1) * P
                    for r in range(2):
                        m = 2 * t + r
                        dve.wait_ge(scored, i * (2 * TT) + (m + 1))
                        dve.wait_ge(exped, i * (2 * TT) + (m + 1))
                        V.tensor_reduce(negmax[:, r:r + 1], flat(4 + 2 * r)[:, 0:n], AX.X, ALU.max)\
                            .then_inc(maxed, 1)
                        dve.wait_ge(maxed, i * (2 * TT) + (m + 1))
                        V.tensor_scalar(negmax[:, r:r + 1], negmax[:, r:r + 1], -SCALE, None,
                                        ALU.mult).then_inc(negated, 1)

                def combine(t):
                    n = (t + 1) * P
                    dve.wait_ge(exped, i * (2 * TT) + (2 * t + 4))
                    V.reciprocal(rinv, rowsum).then_inc(weighed, 1)
                    dve.wait_ge(weighed, i * (3 * TT) + (3 * t + 1))
                    V.tensor_tensor(rinv[:, 1:2], rinv[:, 1:2], neglam, ALU.mult).then_inc(weighed, 1)
                    V.tensor_scalar(prob[0][:, 0:n], prob[0][:, 0:n], rinv[:, 0:1], None, ALU.mult)\
                        .then_inc(weighed, 1)
                    dve.wait_ge(weighed, i * (3 * TT) + (3 * t + 3))
                    V.scalar_tensor_tensor(out=prob[0][:, 0:n], in0=prob[1][:, 0:n],
                                           scalar=rinv[:, 1:2], in1=prob[0][:, 0:n], op0=ALU.mult,
                                           op1=ALU.add).then_inc(combined, 1)

                def take_T(t):
                    for g in range(t // 4 + 1):
                        n = first[t] + g
                        dve.wait_ge(turned, i * NGR + (n + 1))
                        dve.wait_ge(summed, i * TT + (t + 1))
                        width = min(4, t + 1 - 4 * g) * P
                        V.tensor_copy(probT[t % 2][:, 4 * g * P:4 * g * P + width],
                                      c.ps[:, n % 2, 0:width]).then_inc(placed, 1)

                maxima(0)
                for t in range(TT):
                    combine(t)
                    if t + 1 < TT:
                        maxima(t + 1)
                    take_T(t)
                    dve.wait_ge(summed, i * TT + (t + 3))
                    V.tensor_copy(ov[:, t, bass.ds(i * DV, DV)], c.ps[:, 2 + t % 2, 0:DV])\
                        .then_inc(stored, 1)


def phase_router(c, hT, w_group, w_expert, b_group, b_expert, gain_at, slot_dram, tmp):
    nc = c.nc
    hv = hT.rearrange("p (k s) -> p k s", k=KC)
    NL = NG + NE
    pos_ = [0]

    def take(n, parts=P):
        a = pos_[0]
        pos_[0] += n
        return tmp[0:parts, a:a + n]

    t3 = lambda ap, t=TT: ap.rearrange("p (t n) -> p t n", t=t)
    w = take(KC * NL).rearrange("p (k n) -> p k n", k=KC)
    bias = take(NL)
    grp = t3(take(TT * 8))
    exl = t3(take(TT * NE))
    top = t3(take(TT * 8))
    gtop = t3(take(TT * 8))
    gidx, eidx = t3(take(TT * 8)), t3(take(TT * 8))
    no, no_grp = take(NE), take(NE)
    sel = [t3(take(TT * NE)) for _ in range(2)]
    both, pos, dst_, one = (t3(take(TT * NE)) for _ in range(4))
    base = t3(take(TT * NE))
    count, over, blocks, upto, k2 = (take(NE) for _ in range(5))
    ones_e = take(NE)
    gexp = t3(take(TT * NG))
    gsum, e2, s2 = take(TT), take(TT), take(TT)
    dest_f = [take(TT) for _ in range(2)]
    cmp_ = take(EXTRA * NE).rearrange("p (b n) -> p b n", b=EXTRA)
    bno, bex, bcount = take(EXTRA), take(EXTRA), take(1)
    slot_f = take(P, SLOTS // P)
    bl = lambda ap, n: ap.unsqueeze(2).to_broadcast([P, ap.shape[1], n])
    bt = lambda ap, t=TT: ap.unsqueeze(1).to_broadcast([P, t, ap.shape[1]])
    with ExitStack() as ctx:
        S = lambda n: c.sem(ctx, "rt_" + n)
        loaded, numbered, logits, step = S("loaded"), S("numbered"), S("logits"), S("step")
        act_step, ranked, zeroed, scattered = S("act_step"), S("ranked"), S("zeroed"), S("scattered")
        read_back, turned = S("read_back"), S("turned")
        block = ctx.enter_context(nc.Block())

        @block.sync
        def _(sp):
            with nc.allow_non_contiguous_dma(reason="narrow router weights, once"):
                sp.dma_start(w[:, :, 0:NG], cols(w_group)).then_inc(loaded, 16)
                sp.dma_start(w[:, :, NG:NL], cols(w_expert)).then_inc(loaded, 16)
                sp.dma_start(bias[:, 0:NG], bcast(b_group, NG)).then_inc(loaded, 16)
                sp.dma_start(bias[:, NG:NL], bcast(b_expert, NE)).then_inc(loaded, 16)
            sp.wait_ge(numbered, 3)
            sp.dma_start(slot_dram.rearrange("(p b) a -> p (b a)", p=P), c.zeros_i)\
                .then_inc(zeroed, 16)
            sp.wait_ge(scattered, 16 * 2 * TT)
            sp.dma_start(c.slot_rows, slot_dram.rearrange("(b p) a -> b (p a)", p=P))\
                .then_inc(read_back, 16)

        @block.gpsimd
        def _(pool):
            pool.iota(c.expert_no, pattern=[[1, NE]], base=0, channel_multiplier=0)\
                .then_inc(numbered, 1)
            pool.iota(c.token_no, pattern=[[P, TT]], base=0, channel_multiplier=1)\
                .then_inc(numbered, 1)
            pool.memset(c.zeros_i, 0).then_inc(numbered, 1)
            pool.wait_ge(zeroed, 16)
            pool.wait_ge(numbered, 3)
            pool.wait_ge(step, DEST_DONE)
            for t in range(TT):
                for j in range(2):
                    if t or j:
                        pool.wait_ge(scattered, 16 * (2 * t + j))
                    pool.indirect_dma_start(
                        out=slot_dram, out_offset=bass.IndirectOffsetOnAxis(c.dest[j][:, t:t + 1], 0),
                        in_=c.token_no[:, t:t + 1], in_offset=None).then_inc(scattered, 16)
            pool.wait_ge(scattered, 16 * 2 * TT)

        @block.tensor
        def _(pe):
            pe.wait_ge(loaded, 64)
            for t in range(TT):
                for k in range(KC):
                    mm = nc.tensor.matmul(c.ps[:, 0, t * NL:(t + 1) * NL], hv[:, k, t * P:(t + 1) * P],
                                          w[:, k, :], start=(k == 0), stop=(k == KC - 1))
            mm.then_inc(logits, 1)
            pe.wait_ge(step, BOTH_DONE)
            flat = both.rearrange("p t n -> p (t n)")
            nc.tensor.matmul(c.ps[:, 1, 0:TT * NE], c.before[:], flat, start=True, stop=True)
            nc.tensor.matmul(c.ps[:, 2, 0:TT * NE], c.ones[:], flat, start=True, stop=True)\
                .then_inc(ranked, 1)
            pe.wait_ge(step, SLOTS_READ)
            nc.tensor.transpose(c.ps[:, 3, 0:SLOTS // P], slot_f, c.ident[0:SLOTS // P, 0:SLOTS // P])\
                .then_inc(turned, 1)

        @block.scalar
        def _(act):
            act.wait_ge(step, GEXP_ARG)
            nc.scalar.activation(gexp, gexp, ACT.Exp).then_inc(act_step, 1)
            act.wait_ge(step, E2_ARG)
            nc.scalar.activation(e2, e2, ACT.Exp).then_inc(act_step, 1)

        @block.vector
        def _(dve):
            V = nc.vector
            st = Steps(dve, step)
            W = st.then_wait
            tt = lambda o, a, b, op: W(V.tensor_tensor(o, a, b, op))
            ts = lambda o, a, x, y, op0, op1: W(V.tensor_scalar(o, a, x, y, op0, op1))
            dve.wait_ge(numbered, 3)
            W(V.tensor_copy(no, c.expert_no))
            W(V.memset(grp, NEG))
            W(V.memset(ones_e, 1.0))
            W(V.tensor_copy(c.expert_gain, gain_at))
            ts(no_grp, no, float(EPG), None, ALU.is_ge, ALU.bypass)
            for g in range(2, NG):
                W(V.scalar_tensor_tensor(out=no_grp, in0=no, scalar=float(EPG * g), in1=no_grp,
                                         op0=ALU.is_ge, op1=ALU.add))
            dve.wait_ge(logits, 1)
            ps = t3(c.ps[:, 0, 0:TT * NL])
            tt(grp[:, :, 0:NG], ps[:, :, 0:NG], bt(bias[:, 0:NG]), ALU.add)
            tt(exl, ps[:, :, NG:NL], bt(bias[:, NG:NL]), ALU.add)
            for t in range(TT):
                W(V.max(gtop[:, t, :], grp[:, t, :]))
                W(V.max_index(c.found[0][:, 8 * t:8 * t + 8].bitcast(U32), gtop[:, t, :], grp[:, t, :]))
            W(V.tensor_copy(gidx.rearrange("p t n -> p (t n)"), c.found[0]))
            tt(gexp, grp[:, :, 0:NG], gtop[:, :, 0:1].to_broadcast([P, TT, NG]), ALU.subtract)
            assert st.n == GEXP_ARG, st.n
            tt(one, bt(no_grp), gidx[:, :, 0:1].to_broadcast([P, TT, NE]), ALU.is_equal)
            ts(one, one, -NEG, NEG, ALU.mult, ALU.add)
            tt(exl, exl, one, ALU.add)
            for t in range(TT):
                W(V.max(top[:, t, :], exl[:, t, :]))
                W(V.max_index(c.found[1][:, 8 * t:8 * t + 8].bitcast(U32), top[:, t, :], exl[:, t, :]))
            W(V.tensor_copy(eidx.rearrange("p t n -> p (t n)"), c.found[1]))
            for j in range(2):
                tt(sel[j], bt(no), eidx[:, :, j:j + 1].to_broadcast([P, TT, NE]), ALU.is_equal)
            tt(both, sel[0], sel[1], ALU.add)
            assert st.n == BOTH_DONE, st.n
            tt(e2.unsqueeze(2), top[:, :, 1:2], top[:, :, 0:1], ALU.subtract)
            assert st.n == E2_ARG, st.n
            dve.wait_ge(act_step, 1)
            W(V.tensor_reduce(gsum, gexp, AX.X, ALU.add))
            dve.wait_ge(act_step, 2)
            ts(s2, e2, 1.0, None, ALU.add, ALU.bypass)
            tt(s2, s2, gsum, ALU.mult)
            W(V.reciprocal(c.weight[0], s2))
            tt(c.weight[1], c.weight[0], e2, ALU.mult)
            dve.wait_ge(ranked, 1)
            total = t3(c.ps[:, 2, 0:TT * NE])
            W(V.memset(base[:, 0, :], 0.0))
            for t in range(1, TT):
                tt(base[:, t, :], base[:, t - 1, :], total[:, t - 1, :], ALU.add)
            tt(count, base[:, TT - 1, :], total[:, TT - 1, :], ALU.add)
            tt(pos, t3(c.ps[:, 1, 0:TT * NE]), base, ALU.add)
            ts(blocks, count, float(P), None, ALU.is_gt, ALU.bypass)
            for n in range(2, SEQ // P):
                W(V.scalar_tensor_tensor(out=blocks, in0=count, scalar=float(P * n), in1=blocks,
                                         op0=ALU.is_gt, op1=ALU.add))
            W(V.tensor_tensor_scan(upto, ones_e, blocks, 0.0, ALU.mult, ALU.add))
            tt(k2, upto, blocks, ALU.subtract)
            tt(k2, k2, no, ALU.subtract)
            ts(k2, k2, float(P), float(P * (NE - 1)), ALU.mult, ALU.add)
            ts(one, pos, float(P), None, ALU.is_ge, ALU.bypass)
            tt(one, one, bt(k2), ALU.mult)
            tt(dst_, pos, one, ALU.add)
            W(V.scalar_tensor_tensor(out=dst_, in0=bt(no), scalar=float(P), in1=dst_, op0=ALU.mult,
                                     op1=ALU.add))
            for j in range(2):
                tt(sel[j], sel[j], dst_, ALU.mult)
                W(V.tensor_reduce(dest_f[j], sel[j], AX.X, ALU.add))
                W(V.tensor_copy(c.dest[j], dest_f[j]))
            assert st.n == DEST_DONE, st.n
            W(V.tensor_copy(bno, c.expert_no[:, 0:EXTRA]))
            tt(cmp_, bl(bno, NE), bt(upto, EXTRA), ALU.is_ge)
            W(V.tensor_reduce(bex, cmp_, AX.X, ALU.add))
            ts(bex, bex, float(NE - 1), None, ALU.min, ALU.bypass)
            W(V.tensor_copy(c.extra_expert, bex))
            W(V.tensor_copy(c.extra_count, upto[:, NE - 1:NE]))
            dve.wait_ge(read_back, 16)
            W(V.tensor_copy(slot_f, c.slot_rows))
            assert st.n == SLOTS_READ, st.n
            dve.wait_ge(turned, 1)
            W(V.tensor_copy(c.slot_token, c.ps[:, 3, 0:SLOTS // P]))


GEXP_ARG, BOTH_DONE, E2_ARG, DEST_DONE, SLOTS_READ = 27, 50, 51, 87, 94


def phase_experts(c, name, x_dram, y_dram, w_gate, w_up, w_down, slots, tmp, extra):
    nc = c.nc
    ns = 1 if extra else 2
    steps = EXTRA if extra else NE // 2
    first = NE if extra else 0
    FC = DE // P
    take = lambda a, n: tmp[:, a:a + n]
    x = [take(s * D, D) for s in range(2)]
    xT = [take(2048 + s * D, D).rearrange("p (k n) -> p k n", k=KC) for s in range(2)]
    hid = [take(4096 + s * DE, DE) for s in range(2)]
    hidT = [take(5120 + s * DE, DE).rearrange("p (k n) -> p k n", k=FC) for s in range(2)]
    y = [take(6144 + s * D, D) for s in range(2)]
    wg = [r[:, 0:4096].rearrange("p (k n) -> p k n", k=KC) for r in slots]
    wu = [r[:, 4096:8192].rearrange("p (k n) -> p k n", k=KC) for r in slots]
    wd = [r[:, 8192:12288].rearrange("p (k n) -> p k n", k=FC) for r in slots]
    with ExitStack() as ctx:
        S = lambda n: c.sem(ctx, f"{name}_{n}")
        in_load = [S("in_load0"), S("in_load1")]
        down_load = [S("down_load0"), S("down_load1")]
        gathered = [S("gathered0"), S("gathered1")]
        indexed = S("indexed")
        asked = S("asked")
        x_turned = S("x_turned")
        x_placed = S("x_placed")
        product = S("product")
        opened = S("opened")
        hidden = S("hidden")
        h_turned = S("h_turned")
        h_placed = S("h_placed")
        downed = S("downed")
        half0, half1 = S("half0"), S("half1")
        stored = [S("stored0"), S("stored1")]
        written = S("written")
        block = ctx.enter_context(nc.Block())

        def run(eng, body):
            if extra:
                count = eng.value_load(c.extra_count[0:1, 0:1], min_val=0, max_val=EXTRA)
                with eng.Fori(0, steps) as i:
                    with eng.If(i < count):
                        body(i, 0)
            else:
                with eng.Fori(0, steps) as i:
                    for s in range(ns):
                        body(i, s)

        @block.sync
        def _(sp):
            def load(i, s):
                if extra:
                    e = sp.value_load(c.extra_expert[0:1, bass.ds(i, 1)], min_val=0, max_val=NE - 1)
                else:
                    e = i * 2 + s
                rows = lambda m: m[bass.ds(e, 1)].rearrange("a (k p) n -> p (a k) n", p=P)
                sp.wait_ge(downed, i * ns + (s + 1))
                sp.dma_start(wg[s], rows(w_gate)).then_inc(in_load[s], 16)
                sp.dma_start(wu[s], rows(w_up)).then_inc(in_load[s], 16)
                sp.dma_start(wd[s], rows(w_down)).then_inc(down_load[s], 16)

            sp.sem_inc(stored[0], 16)
            sp.sem_inc(stored[1], 16)
            run(sp, load)

        @block.gpsimd
        def _(pool):
            def gather(i, s):
                b = i * ns + s
                pool.wait_ge(x_turned, b + 1)
                nc.gpsimd.tensor_copy(c.gather_at[s], c.slot_token[:, bass.ds(b + first, 1)])\
                    .then_inc(indexed, 1)
                pool.wait_ge(indexed, b + 1)
                pool.sem_inc(asked, 1)
                pool.indirect_dma_start(
                    out=x[s], out_offset=None, in_=x_dram,
                    in_offset=bass.IndirectOffsetOnAxis(c.gather_at[s], 0)).then_inc(gathered[s], 16)

            run(pool, gather)

        @block.tensor
        def _(pe):
            def turn_x(i, s):
                b = i * ns + s
                pe.wait_ge(gathered[s], i * 16 + 16)
                pe.wait_ge(x_placed, b + ns)
                for k in range(KC):
                    mm = nc.tensor.transpose(c.ps[:, k // 4, (k % 4) * P:(k % 4 + 1) * P],
                                             x[s][:, k * P:(k + 1) * P], c.ident[:])
                mm.then_inc(x_turned, 1)

            def gate_up(i, s):
                b = i * ns + s
                pe.wait_ge(in_load[s], i * 32 + 32)
                pe.wait_ge(x_placed, b + (ns + 1))
                pe.wait_ge(opened, b + ns)
                pe.wait_ge(hidden, b + ns)
                for k in range(KC):
                    for j, w in enumerate((wg, wu)):
                        mm = nc.tensor.matmul(c.ps[:, 2 + j, :], xT[s][:, k, :], w[s][:, k, :],
                                              start=(k == 0), stop=(k == KC - 1))
                mm.then_inc(product, 1)

            def turn_h(i, s):
                b = i * ns + s
                pe.wait_ge(hidden, b + (ns + 1))
                pe.wait_ge(h_placed, b + ns)
                for k in range(FC):
                    mm = nc.tensor.transpose(c.ps[:, 4, k * P:(k + 1) * P],
                                             hid[s][:, k * P:(k + 1) * P], c.ident[:])
                mm.then_inc(h_turned, 1)

            def down(i, s):
                b = i * ns + s
                pe.wait_ge(down_load[s], i * 16 + 16)
                pe.wait_ge(h_placed, b + (ns + 1))
                pe.wait_ge(half0, b + ns)
                pe.wait_ge(half1, b + ns)
                for k in range(FC):
                    for h in range(2):
                        mm = nc.tensor.matmul(c.ps[:, 5 + h, :], hidT[s][:, k, :],
                                              wd[s][:, k, h * BANK:(h + 1) * BANK],
                                              start=(k == 0), stop=(k == FC - 1))
                mm.then_inc(downed, 1)

            if extra:
                def whole(i, s):
                    for part in (turn_x, gate_up, turn_h, down):
                        part(i, s)
                pe.sem_inc(downed, ns)
                pe.sem_inc(x_turned, ns)
                run(pe, whole)
            else:
                pe.sem_inc(downed, ns)
                pe.sem_inc(x_turned, ns)
                turn_x(0, 0)

                def step(i, last):
                    gate_up(i, 0)
                    turn_x(i, 1)
                    turn_h(i, 0)
                    down(i, 0)
                    gate_up(i, 1)
                    if not last:
                        turn_x(i + 1, 0)
                    turn_h(i, 1)
                    down(i, 1)

                with pe.Fori(0, steps - 1) as i:
                    step(i, False)
                step(steps - 1, True)

        @block.scalar
        def _(act):
            def work(i, s):
                b = i * ns + s
                act.wait_ge(product, b + 1)
                nc.scalar.activation(hid[s], c.ps[:, 2, :], ACT.Silu).then_inc(opened, 1)
                act.wait_ge(h_turned, b + 1)
                nc.scalar.activation(hidT[s], c.ps[:, 4, :].rearrange("p (k n) -> p k n", k=FC),
                                     ACT.Identity).then_inc(h_placed, 1)
                act.wait_ge(downed, b + (ns + 1))
                act.wait_ge(stored[s], i * 16 + 16)
                nc.scalar.activation(y[s][:, 0:BANK], c.ps[:, 5, :], ACT.Identity).then_inc(half0, 1)
                act.wait_ge(half0, b + (ns + 1))
                act.wait_ge(half1, b + (ns + 1))
                act.dma_start(y_dram[bass.ds((b + first) * P, P), :], y[s]).then_inc(stored[s], 16)
                if extra:
                    act.wait_ge(stored[s], i * 16 + 32)
                    act.sem_inc(written, 1)

            act.sem_inc(opened, ns)
            act.sem_inc(h_placed, ns)
            act.sem_inc(half0, ns)
            run(act, work)
            if not extra:
                for s in range(ns):
                    act.wait_ge(stored[s], 16 * steps + 16)

        @block.vector
        def _(dve):
            V = nc.vector

            def place(i, s):
                b = i * ns + s
                dve.wait_ge(x_turned, b + (ns + 1))
                V.tensor_tensor(xT[s], c.ps[:, 0:2, :].rearrange("p b (k n) -> p (b k) n", k=4),
                                c.expert_gain.unsqueeze(2).to_broadcast([P, KC, P]), ALU.mult)\
                    .then_inc(x_placed, 1)

            def hide(i, s):
                b = i * ns + s
                dve.wait_ge(opened, b + (ns + 1))
                V.tensor_tensor(hid[s], hid[s], c.ps[:, 3, :], ALU.mult).then_inc(hidden, 1)

            def out(i, s):
                b = i * ns + s
                dve.wait_ge(downed, b + (ns + 1))
                dve.wait_ge(stored[s], i * 16 + 16)
                V.tensor_copy(y[s][:, BANK:D], c.ps[:, 6, :]).then_inc(half1, 1)

            dve.sem_inc(x_placed, ns)
            dve.sem_inc(hidden, ns)
            dve.sem_inc(half1, ns)
            if extra:
                def whole(i, s):
                    for part in (place, hide, out):
                        part(i, s)
                run(dve, whole)
            else:
                place(0, 0)

                def step(i, last):
                    hide(i, 0)
                    place(i, 1)
                    out(i, 0)
                    hide(i, 1)
                    if not last:
                        place(i + 1, 0)
                    out(i, 1)

                with dve.Fori(0, steps - 1) as i:
                    step(i, False)
                step(steps - 1, True)


def phase_combine(c, x2, y_dram, out_dram, tmp):
    nc = c.nc
    xv = x2.rearrange("p (t d) -> p t d", t=TT)
    rows = out_dram.rearrange("(t p) d -> p t d", p=P)
    NB = 8
    buf = [tmp[:, s * D:(s + 1) * D] for s in range(NB)]
    with ExitStack() as ctx:
        got = [c.sem(ctx, f"cb_got{s}") for s in range(NB)]
        added, stored = c.sem(ctx, "cb_added"), c.sem(ctx, "cb_stored")
        block = ctx.enter_context(nc.Block())

        @block.gpsimd
        def _(pool):
            for n in range(2 * TT):
                t, j = divmod(n, 2)
                if n >= NB:
                    pool.wait_ge(added, n - NB + 1)
                pool.indirect_dma_start(
                    out=buf[n % NB], out_offset=None, in_=y_dram,
                    in_offset=bass.IndirectOffsetOnAxis(c.dest[j][:, t:t + 1], 0))\
                    .then_inc(got[n % NB], 16)

        @block.vector
        def _(dve):
            for n in range(2 * TT):
                t, j = divmod(n, 2)
                dve.wait_ge(got[n % NB], 16 * (n // NB + 1))
                if j:
                    dve.wait_ge(added, n)
                nc.vector.scalar_tensor_tensor(out=xv[:, t, :], in0=buf[n % NB],
                                               scalar=c.weight[j][:, t:t + 1], in1=xv[:, t, :],
                                               op0=ALU.mult, op1=ALU.add).then_inc(added, 1)

        @block.sync
        def _(sp):
            for t in range(TT):
                sp.wait_ge(added, 2 * t + 2)
                sp.dma_start(rows[:, t, :], xv[:, t, :]).then_inc(stored, 16)
            sp.wait_ge(stored, 16 * TT)


def _build(nc, a, out, upto=99):
    with ExitStack() as ctx:
        c = Chip(nc, ctx)
        R = lambda r: c.at(r, 0, REGION)
        ys = nc.dram_tensor("expert_out", (SLOTS, D), F32).ap()
        zeroed = c.sem(ctx, "zeroed")
        phase_constants(c, c.at(5, 0, D), ys[NE * P:SLOTS, :], zeroed)
        phase_norm_T(c, "pre", R(1), R(0), R(2), a["pre_norm_g"][0], src_dram=a["x"][0],
                     also=(zeroed, 16 * EXTRA))
        phase_xbc(c, R(0), a["w_in"][0], a["conv_w"][0], a["conv_b"][0], c.at(1, 0, 2 * REGION), R(3),
                  R(4), R(5))
        fcum = nc.dram_tensor("forget_sums", (HEADS, SEQ), F32).ap()
        phase_decays(c, R(0), a["w_in"][0], a["dt_bias"][0], a["a_log"][0], a["d_skip"][0],
                     a["fgate_b"][0], fcum, R(5))
        if upto < 2:
            return c
        phase_ssd(c, c.at(1, 0, 2 * REGION), R(3), R(4), R(5))
        if upto < 3:
            return c
        T = lambda r, k=KC: r.rearrange("p (k s) -> p k s", k=k)
        half = lambda r, n: r.rearrange("p (t d) -> p t d", t=TT)[:, :, n * BANK:(n + 1) * BANK]
        wcol = lambda w, a0, n: cols(w)[:, :, a0 + n * BANK:a0 + (n + 1) * BANK]
        ws = [c.at(5, 0, REGION // 2), c.at(5, REGION // 2, REGION // 2)]
        w_in = a["w_in"][0]
        phase_dense(c, "z", [(T(R(0)), wcol(w_in, C_Z, n), "act", half(R(2), n), ACT.Silu)
                             for n in range(2)], ws)
        phase_turn(c, "y", R(4), R(1), gate=R(2), groups=GROUPS, gain_dram=a["ssm_norm_g"][0])
        if upto < 4:
            return c
        phase_dense(c, "bs", [(T(R(0)), wcol(w_in, C_GS, n), "act", half(R(4), n), ACT.Sigmoid)
                              for n in range(2)]
                    + [(T(R(1)), wcol(a["w_branch_ssm"][0], 0, n), "mul", half(R(2), n), half(R(4), n))
                       for n in range(2)]
                    + [(T(R(0)), wcol(w_in, C_V, n), "act", half(R(3), n), ACT.Identity)
                       for n in range(2)], ws)
        phase_forget_attention(c, R(0), w_in, fcum, R(3), R(4), c.at(1, 0, 4 * SEQ),
                               c.at(1, 4 * SEQ, 2 * D), c.at(5, 0, 4 * SEQ))
        if upto < 5:
            return c
        phase_dense(c, "za", [(T(R(0)), wcol(w_in, C_ZA, n), "act", half(R(3), n), ACT.Silu)
                              for n in range(2)], ws)
        phase_turn(c, "ya", R(4), R(1), gate=R(3))
        phase_dense(c, "ba", [(T(R(0)), wcol(w_in, C_GA, n), "act", half(R(4), n), ACT.Sigmoid)
                              for n in range(2)]
                    + [(T(R(1)), wcol(a["w_branch_att"][0], 0, n), "muladd", half(R(2), n),
                        half(R(4), n)) for n in range(2)], ws)
        phase_turn(c, "mg", R(2), R(1))
        phase_dense(c, "wo", [(T(R(1)), wcol(a["w_out"][0], 0, n), "act", half(R(3), n), ACT.Identity)
                              for n in range(2)], ws)
        phase_post(c, a["x"][0], a["post_norm_g"][0], R(3), R(4), R(2))
        if upto < 6:
            return c
        phase_norm_T(c, "n2", R(4), R(0), R(1), a["attn_norm_g_2"][0])
        w_in = a["w_in_2"][0]
        h2 = T(R(0))
        v2 = c.at(2, 4096, 4096)
        v2h = v2.rearrange("p (t d) -> p t d", t=TT)
        conv = c.at(2, 0, 4096)
        phase_conformer(c, R(0), w_in, (a["conv_dw_w_2"][0], a["conv_dw_b_2"][0]),
                        [(h2, wcol(w_in, C2_V, 0), "act", v2h, ACT.Identity)]
                        + [(h2, wcol(w_in, C2_G, n), "act", half(R(3), n), ACT.Sigmoid)
                           for n in range(2)],
                        c.at(1, 0, 4 * (SEQ + CW - 1)), conv, c.at(1, 4224, SEQ),
                        c.at(1, 5248, 2 * D), ws, c.at(5, REGION // 2, CCH))
        phase_channel_norm(c, conv, c.at(1, 0, 4096), c.at(1, 4096, SEQ), a["conv_ln_g_2"][0],
                           a["conv_ln_b_2"][0])
        if upto < 7:
            return c
        o2 = c.at(1, 0, 4096)
        phase_diff_attention(c, R(0), w_in, a["q_norm_g_2"][0], a["k_norm_g_2"][0],
                             [a[f"lambda_{n}_2"][0] for n in ("q1", "k1", "q2", "k2")], v2, o2, R(5),
                             c.at(1, 4096, 2 * SEQ))
        phase_turn(c, "o2", o2, v2, groups=DH, gain_dram=a["subln_g_2"][0], gain_times=1.0 - LAM_INIT,
                   width=DH * DV)
        if upto < 8:
            return c
        phase_dense(c, "b2", [(h2, wcol(w_in, C2_G, 2 + n), "act", half(R(1), n), ACT.Sigmoid)
                              for n in range(2)]
                    + [(T(conv, 4), wcol(a["w_conv_out_2"][0], 0, n), "mul", half(R(3), n),
                        half(R(3), n)) for n in range(2)]
                    + [(T(v2, 4), wcol(a["w_attn_out_2"][0], 0, n), "muladd", half(R(3), n),
                        half(R(1), n)) for n in range(2)], ws)
        phase_turn(c, "m2", R(3), R(1))
        phase_dense(c, "wo2", [(T(R(1)), wcol(a["w_out_2"][0], 0, n), "add", half(R(4), n), None)
                               for n in range(2)], ws)
        if upto < 9:
            return c
        xn = nc.dram_tensor("expert_in", (SEQ, D), F32).ap()
        slot_dram = nc.dram_tensor("slot_tokens", (SLOTS, 1), I32).ap()
        phase_norm_T(c, "n3", R(4), R(0), R(1), a["ffn_norm_g_2"][0], xn_dram=xn)
        phase_router(c, R(0), a["w_router_group_2"][0], a["w_router_expert_2"][0],
                     a["b_router_group_2"][0], a["b_router_expert_2"][0], c.small[:, 16:24],
                     slot_dram, R(2))
        if upto < 10:
            return c
        slots = [c.at(1, 0, 12288), c.at(1, 12288, 12288)]
        for extra in (False, True):
            phase_experts(c, "xe" if extra else "ex", xn, ys, a["w_gate_e_2"][0], a["w_up_e_2"][0],
                          a["w_down_e_2"][0], slots, R(5), extra)
        phase_combine(c, R(4), ys, out[0], R(1))
        return c


_INS = ['x', 'pre_norm_g', 'w_in', 'conv_w', 'conv_b', 'dt_bias', 'a_log', 'd_skip', 'ssm_norm_g',
        'fgate_b', 'w_branch_ssm', 'w_branch_att', 'w_out', 'post_norm_g', 'attn_norm_g_2',
        'w_in_2', 'conv_dw_w_2', 'conv_dw_b_2', 'conv_ln_g_2', 'conv_ln_b_2', 'w_conv_out_2',
        'q_norm_g_2', 'k_norm_g_2', 'lambda_q1_2', 'lambda_k1_2', 'lambda_q2_2', 'lambda_k2_2',
        'subln_g_2', 'w_attn_out_2', 'w_out_2', 'ffn_norm_g_2', 'w_router_group_2',
        'b_router_group_2', 'w_router_expert_2', 'b_router_expert_2', 'w_gate_e_2', 'w_up_e_2',
        'w_down_e_2']


def kernel(**inputs):
    import numpy as _np
    import concourse.bacc as _bacc
    from concourse import mybir as _mybir
    from concourse.bass_utils import run_bass_kernel_spmd as _run

    nc = _bacc.Bacc("TRN2", target_bir_lowering=False, num_devices=1)
    arrays, args = {}, {}
    for name in _INS:
        v = _np.ascontiguousarray(inputs[name])
        arrays[f"in_{name}"] = v
        args[name] = nc.dram_tensor(f"in_{name}", v.shape, _mybir.dt.from_np(v.dtype),
                                    kind="ExternalInput").ap()
    out = nc.dram_tensor("out_0", (1, SEQ, D), _mybir.dt.float32, kind="ExternalOutput").ap()
    _build(nc, args, out)
    r = _run(nc, [arrays], core_ids=[0])
    return r.results[0]["out_0"]
```

```python
from contextlib import ExitStack

import concourse.bass as bass
from concourse import mybir

F32 = mybir.dt.float32
F32R = mybir.dt.float32r
BF16 = mybir.dt.bfloat16
I32 = mybir.dt.int32
U32 = mybir.dt.uint32
ACT = mybir.ActivationFunctionType
ALU = mybir.AluOpType
AX = mybir.AxisListType

P = 128
SEQ = 1024
D = 1024
TT = SEQ // P
KC = D // P
BANK = 512
EPS = 1e-6

HEADS, HD = 16, 64
GROUPS, STATE, CONV = 4, 128, 4
HPG = HEADS // GROUPS
XBC = D + 2 * GROUPS * STATE
C_Z, C_XBC = 0, D
C_DT = C_XBC + XBC
C_Q = C_DT + HEADS
C_K, C_V = C_Q + D, C_Q + 2 * D
C_F = C_Q + 3 * D
C_ZA = C_F + HEADS
C_GS, C_GA = C_ZA + D, C_ZA + 2 * D

CCH, CW = D // 2, 31
DH, DHD = 4, 64
DV = 2 * DHD
C2_Q = 2 * CCH
C2_K = C2_Q + DH * DV
C2_V = C2_K + DH * DV
C2_G = C2_V + DH * DV
LAM_INIT = 0.8 - 0.6
NG, EPG = 4, 8
NE = NG * EPG
DE = D // 2
ASSIGN = 2 * SEQ
EXTRA = ASSIGN // P
SLOTS = (NE + EXTRA) * P

NEG = -1e30
REGION = 8192


class Steps:

    def __init__(self, eng, sem, base=0):
        self.eng, self.sem, self.base, self.n = eng, sem, base, 0

    def done(self, ins):
        ins.then_inc(self.sem, 1)
        self.n += 1
        return self.n

    def then_wait(self, ins):
        self.done(ins)
        self.eng.wait_ge(self.sem, self.base + self.n)


class Chip:

    def __init__(self, nc, ctx):
        self.nc, self.ctx = nc, ctx
        sb = lambda name, shape, dt=F32: ctx.enter_context(nc.sbuf_tensor(name, shape, dt))
        self.arena = sb("arena", [P, 6 * REGION])
        self.arena_at = nc.sbuf_base - 4 * 6 * REGION
        self.ps = ctx.enter_context(nc.psum_tensor("ps", [P, 8, BANK], F32))
        self.ident = sb("ident", [P, P])
        self.ones = sb("ones", [P, P])
        self.upto = sb("upto", [P, P])
        self.before = sb("before", [P, P])
        self.identb = sb("identb", [P, P], BF16)
        self.maskb = sb("maskb", [P, P], BF16)
        self.maskTb = sb("maskTb", [P, 4, P], BF16)
        self.small = sb("small", [P, 1600])
        ints = sb("ints", [P, 512], I32)
        self.dest = [ints[:, 8 * j:8 * j + 8] for j in range(2)]
        self.slot_token = ints[:, 16:16 + SLOTS // P]
        self.gather_at = [ints[:, 64 + j:65 + j] for j in range(2)]
        self.found = [ints[:, 66 + 64 * j:130 + 64 * j] for j in range(2)]
        self.expert_no = ints[:, 194:194 + NE]
        self.token_no = ints[:, 226:226 + TT]
        self.extra_expert = ints[:, 234:234 + EXTRA]
        self.extra_count = ints[:, 250:251]
        self.zeros_i = ints[:, 256:256 + SLOTS // P]
        self.slot_rows = ints[0:SLOTS // P, 320:320 + P]
        self.weight = [self.small[:, 1408 + 32 + 8 * j:1408 + 40 + 8 * j] for j in range(2)]

    def at(self, region, offset, size):
        a = region * REGION + offset
        return self.arena[:, a:a + size]

    def named(self, name, region, offset, size, dtype=F32, parts=1):
        t = self.nc.alloc_sbuf_tensor_at(name, [P, parts, size], dtype,
                                         offset=self.arena_at + 4 * (region * REGION + offset))
        return t[:, 0, :] if parts == 1 else [t[:, n, :] for n in range(parts)]

    def rounded(self, name, region, offset, size):
        return self.named(name, region, offset, size, F32R, 2)

    def sem(self, ctx, name):
        s = ctx.enter_context(self.nc.semaphore(name))
        ctx.callback(lambda: self.nc.gpsimd.sem_clear(s))
        return s


def cols(ap):
    return ap.rearrange("(k p) n -> p k n", p=P)


def phase_constants(c, zero, extra_dram, zeroed):
    nc = c.nc
    with ExitStack() as ctx:
        filled, shaped = c.sem(ctx, "const_filled"), c.sem(ctx, "const_shaped")
        zero_set = c.sem(ctx, "zero_set")
        block = ctx.enter_context(nc.Block())

        @block.vector
        def _(dve):
            nc.vector.memset(zero, 0.0).then_inc(zero_set, 1)

        @block.sync
        def _(sp):
            sp.wait_ge(zero_set, 1)
            for b in range(EXTRA):
                sp.dma_start(extra_dram[b * P:(b + 1) * P, :], zero).then_inc(zeroed, 16)

        @block.gpsimd
        def _(pool):
            for m, v in ((c.ident, 0.0), (c.ones, 1.0), (c.upto, 1.0), (c.before, 1.0),
                         (c.identb, 0.0), (c.maskb, 0.0), (c.maskTb, 0.0)):
                pool.memset(m[:], v).then_inc(filled, 1)
            pool.wait_ge(filled, 7)
            one = [[-1, P]]
            up = [[1, P]]
            for m in (c.ident, c.identb):
                pool.affine_select(out=m[:], in_=m[:], compare_op=ALU.not_equal, fill=1.0, base=0,
                                   pattern=one, channel_multiplier=1).then_inc(shaped, 1)
            pool.affine_select(out=c.upto[:], in_=c.upto[:], compare_op=ALU.is_ge, fill=0.0, base=0,
                               pattern=up, channel_multiplier=-1).then_inc(shaped, 1)
            pool.affine_select(out=c.before[:], in_=c.before[:], compare_op=ALU.is_gt, fill=0.0,
                               base=0, pattern=up, channel_multiplier=-1).then_inc(shaped, 1)
            pool.affine_select(out=c.maskb[:], in_=c.maskb[:], compare_op=ALU.is_ge, fill=NEG,
                               base=0, pattern=one, channel_multiplier=1).then_inc(shaped, 1)
            pool.affine_select(out=c.maskTb[:], in_=c.maskTb[:], compare_op=ALU.is_ge, fill=NEG,
                               base=0, pattern=[[0, 4], [1, P]], channel_multiplier=-1)\
                .then_inc(shaped, 1)
            pool.wait_ge(shaped, 6)


def phase_norm_T(c, name, src, dst, xn, gain_dram, src_dram=None, xn_dram=None, also=None,
                 row_gain=None, keep_dram=None):
    nc = c.nc
    with ExitStack() as ctx:
        loaded = [c.sem(ctx, f"{name}_loaded{t}") for t in range(2)]
        squared, rooted = c.sem(ctx, f"{name}_squared"), c.sem(ctx, f"{name}_rooted")
        step = c.sem(ctx, f"{name}_step")
        turned, placed = c.sem(ctx, f"{name}_turned"), c.sem(ctx, f"{name}_placed")
        stored, kept = c.sem(ctx, f"{name}_stored"), c.sem(ctx, f"{name}_kept")
        ss, rstd, gain = c.small[:, 0:8], c.small[:, 8:16], c.small[:, 16:24]
        block = ctx.enter_context(nc.Block())
        srcv = src.rearrange("p (t d) -> p t d", t=TT)
        xnv = xn.rearrange("p (t d) -> p t d", t=TT)
        dstv = dst.rearrange("p (k s) -> p k s", k=KC)

        @block.sync
        def _(sp):
            if row_gain is None:
                with nc.allow_non_contiguous_dma(reason="a gain vector by chunks"):
                    sp.dma_start(gain, gain_dram.rearrange("(k p) -> p k", p=P))\
                        .then_inc(loaded[0], 16)
            else:
                sp.dma_start(row_gain, bcast(gain_dram, D)).then_inc(loaded[0], 16)
                sp.dma_start(keep_dram.rearrange("(t p) d -> p t d", p=P), srcv).then_inc(kept, 16)
            if src_dram is not None:
                rows = src_dram.rearrange("(t p) d -> p t d", p=P)
                for t in range(2):
                    sp.dma_start(srcv[:, 4 * t:4 * t + 4, :], rows[:, 4 * t:4 * t + 4, :])\
                        .then_inc(loaded[t], 16)
            if xn_dram is not None:
                rows = xn_dram.rearrange("(t p) d -> p t d", p=P)
                for t in range(TT):
                    sp.wait_ge(step, 3 + t)
                    sp.dma_start(rows[:, t, :], xnv[:, t, :]).then_inc(stored, 16)
                sp.wait_ge(stored, 16 * TT)
                sp.wait_ge(kept, 16)
            if also is not None:
                sp.wait_ge(*also)

        @block.scalar
        def _(act):
            for t in range(TT):
                if src_dram is not None and t % 4 == 0:
                    act.wait_ge(loaded[t // 4], 32 if t == 0 else 16)
                nc.scalar.activation(xnv[:, t, :], srcv[:, t, :], ACT.Square,
                                     accum_out=ss[:, t:t + 1]).then_inc(squared, 1)
            act.wait_ge(step, 1)
            nc.scalar.activation(rstd, rstd, ACT.Sqrt).then_inc(rooted, 1)

        @block.vector
        def _(dve):
            st = Steps(dve, step)
            dve.wait_ge(squared, TT)
            st.done(nc.vector.tensor_scalar(rstd, ss, 1.0 / D, EPS, ALU.mult, ALU.add))
            dve.wait_ge(rooted, 1)
            st.then_wait(nc.vector.reciprocal(rstd, rstd))
            dve.wait_ge(loaded[0], 16 if src_dram is None else 32)
            for t in range(TT):
                if row_gain is None:
                    x = nc.vector.tensor_scalar(xnv[:, t, :], srcv[:, t, :], rstd[:, t:t + 1], None,
                                                ALU.mult)
                else:
                    x = nc.vector.scalar_tensor_tensor(out=xnv[:, t, :], in0=srcv[:, t, :],
                                                       scalar=rstd[:, t:t + 1], in1=row_gain,
                                                       op0=ALU.mult, op1=ALU.mult)
                st.done(x)
            for n in range(2 * TT):
                t, h = divmod(n, 2)
                dve.wait_ge(turned, n + 1)
                out = dstv[:, 4 * h:4 * h + 4, t * P:(t + 1) * P]
                ps = c.ps[:, n % 8, :].rearrange("p (k s) -> p k s", k=4)
                if row_gain is None:
                    x = nc.vector.tensor_tensor(
                        out, ps, gain[:, 4 * h:4 * h + 4].unsqueeze(2).to_broadcast([P, 4, P]),
                        ALU.mult)
                else:
                    x = nc.vector.tensor_copy(out, ps)
                x.then_inc(placed, 1)

        @block.tensor
        def _(pe):
            for n in range(2 * TT):
                t, h = divmod(n, 2)
                pe.wait_ge(step, 3 + t)
                if n >= 8:
                    pe.wait_ge(placed, n - 7)
                for k in range(4):
                    kk = 4 * h + k
                    mm = nc.tensor.transpose(c.ps[:, n % 8, k * P:(k + 1) * P],
                                             xnv[:, t, kk * P:(kk + 1) * P], c.ident[:])
                mm.then_inc(turned, 1)


def phase_xbc(c, hT, w_in, conv_w, conv_b, tok, bcT, temps, wslots):
    nc = c.nc
    NB = XBC // P
    hv = hT.rearrange("p (k s) -> p k s", k=KC)
    tokv = tok.rearrange("p (t n) -> p t n", t=TT)
    u = [temps[:, s * 1028:s * 1028 + CONV - 1 + SEQ] for s in range(2)]
    acc = [temps[:, 2056 + s * SEQ:2056 + (s + 1) * SEQ] for s in range(2)]
    act_out = [temps[:, 4104 + s * SEQ:4104 + (s + 1) * SEQ] for s in range(2)]
    w = [wslots[:, s * D:(s + 1) * D].rearrange("p (k n) -> p k n", k=KC) for s in range(2)]
    taps = c.small[:, 0:NB * CONV].rearrange("p (j b) -> p j b", j=CONV)
    bias = c.small[:, 64:64 + NB]
    wv = cols(w_in)
    with ExitStack() as ctx:
        params = c.sem(ctx, "xbc_params")
        wload = [c.sem(ctx, f"xbc_wload{s}") for s in range(2)]
        projected = c.sem(ctx, "xbc_projected")
        evacuated = c.sem(ctx, "xbc_evacuated")
        convolved = c.sem(ctx, "xbc_convolved")
        silued = c.sem(ctx, "xbc_silued")
        turned = c.sem(ctx, "xbc_turned")
        placed = c.sem(ctx, "xbc_placed")
        kept = c.sem(ctx, "xbc_kept")
        tapped = c.sem(ctx, "xbc_tapped")
        block = ctx.enter_context(nc.Block())

        @block.sync
        def _(sp):
            with nc.allow_non_contiguous_dma(reason="per-channel vectors by chunks"):
                for j in range(CONV):
                    sp.dma_start(taps[:, j, :], conv_w[j].rearrange("(b p) -> p b", p=P))\
                        .then_inc(params, 16)
                sp.dma_start(bias, conv_b.rearrange("(b p) -> p b", p=P)).then_inc(params, 16)
            for s in range(2):
                sp.dma_start(w[s], wv[:, :, C_XBC + s * P:C_XBC + (s + 1) * P]).then_inc(wload[s], 16)
            with sp.Fori(1, NB // 2) as i:
                for s in range(2):
                    sp.wait_ge(projected, i * 2 + (s - 1))
                    sp.dma_start(w[s], wv[:, :, bass.ds(i * (2 * P) + (C_XBC + s * P), P)])\
                        .then_inc(wload[s], 16)

        @block.tensor
        def _(pe):
            def transposes(i, s):
                pe.wait_ge(silued, i * 2 + (s + 3))
                pe.wait_ge(placed, i * 2 + (s + 1))
                for t in range(TT):
                    mm = nc.tensor.transpose(
                        c.ps[:, 4 + 2 * s + t // 4, (t % 4) * P:(t % 4 + 1) * P],
                        act_out[s][:, t * P:(t + 1) * P], c.ident[:])
                mm.then_inc(turned, 1)

            def project(i, s):
                pe.wait_ge(wload[s], i * 16 + 16)
                pe.wait_ge(evacuated, i * 2 + (s + 1))
                for k in range(KC):
                    for h in range(2):
                        mm = nc.tensor.matmul(c.ps[:, 2 * s + h, :], w[s][:, k, :],
                                              hv[:, k, h * BANK:(h + 1) * BANK],
                                              start=(k == 0), stop=(k == KC - 1))
                mm.then_inc(projected, 1)

            pe.sem_inc(turned, 2)
            project(0, 0)
            with pe.Fori(0, NB // 2 - 1) as i:
                project(i, 1)
                transposes(i, 0)
                project(i + 1, 0)
                transposes(i, 1)
            project(NB // 2 - 1, 1)
            transposes(NB // 2 - 1, 0)
            transposes(NB // 2 - 1, 1)

        @block.scalar
        def _(act):
            def evacuate(i, s):
                act.wait_ge(projected, i * 2 + (s + 1))
                act.wait_ge(convolved, i * 2 + (s + 1))
                nc.scalar.activation(u[s][:, CONV - 1:],
                                     c.ps[:, 2 * s:2 * s + 2, :].rearrange("p b n -> p (b n)"),
                                     ACT.Identity).then_inc(evacuated, 1)

            def silu(i, s):
                act.wait_ge(convolved, i * 2 + (s + 3))
                act.wait_ge(turned, i * 2 + (s + 1))
                act.wait_ge(kept, i * 2 + (s + 1))
                nc.scalar.activation(act_out[s], acc[s], ACT.Silu).then_inc(silued, 1)

            act.sem_inc(evacuated, 2)
            evacuate(0, 0)
            with act.Fori(0, NB // 2 - 1) as i:
                evacuate(i, 1)
                silu(i, 0)
                evacuate(i + 1, 0)
                silu(i, 1)
            evacuate(NB // 2 - 1, 1)
            silu(NB // 2 - 1, 0)
            silu(NB // 2 - 1, 1)

        @block.vector
        def _(dve):
            def convolve(i, s):
                dve.wait_ge(evacuated, i * 2 + (s + 3))
                dve.wait_ge(silued, i * 2 + (s + 1))
                tap = lambda j: taps[:, j, bass.ds(i * 2 + s, 1)]
                base = 3 * s
                nc.vector.tensor_scalar(acc[s], u[s][:, 3:3 + SEQ], tap(3),
                                        bias[:, bass.ds(i * 2 + s, 1)], ALU.mult, ALU.add)\
                    .then_inc(tapped, 1)
                for j in (2, 1, 0):
                    dve.wait_ge(tapped, i * 6 + (base + 3 - j))
                    x = nc.vector.scalar_tensor_tensor(out=acc[s], in0=u[s][:, j:j + SEQ],
                                                       scalar=tap(j), in1=acc[s], op0=ALU.mult,
                                                       op1=ALU.add)
                    x.then_inc(tapped if j else convolved, 1)

            def place(i, s):
                dve.wait_ge(turned, i * 2 + (s + 3))
                nc.vector.tensor_copy(tokv[:, :, bass.ds(i * (2 * P) + s * P, P)],
                                      c.ps[:, 4 + 2 * s:6 + 2 * s, :]
                                      .rearrange("p b (t n) -> p (b t) n", t=4)).then_inc(placed, 1)

            dve.sem_inc(silued, 2)
            dve.sem_inc(placed, 2)
            for s in range(2):
                nc.vector.memset(u[s][:, 0:CONV - 1], 0.0).then_inc(convolved, 1)
            dve.wait_ge(convolved, 2)
            dve.wait_ge(params, 16 * (CONV + 1))
            convolve(0, 0)
            with dve.Fori(0, NB // 2 - 1) as i:
                convolve(i, 1)
                place(i, 0)
                convolve(i + 1, 0)
                place(i, 1)
            convolve(NB // 2 - 1, 1)
            place(NB // 2 - 1, 0)
            place(NB // 2 - 1, 1)

        @block.gpsimd
        def _(pool):
            pool.sem_inc(kept, 2)
            pool.sem_inc(kept, D // P)
            first = D // P // 2
            with pool.Fori(first, NB // 2) as i:
                for s in range(2):
                    pool.wait_ge(silued, i * 2 + (s + 3))
                    nc.gpsimd.tensor_copy(bcT[:, bass.ds((i - first) * (2 * SEQ) + s * SEQ, SEQ)],
                                          act_out[s]).then_inc(kept, 1)


def bcast(row, n):
    return row.rearrange("(a n) -> a n", a=1).to_broadcast([P, n])


class Decays:

    def __init__(self, c):
        take = lambda n: c.small[:, P * (n + 1):P * (n + 2)]
        self.dt, self.ncs, self.ecs, self.dte, self.cdec, self.dta = (take(n) for n in range(6))
        self.skip = c.small[:, 7 * P:7 * P + HEADS]


def phase_decays(c, hT, w_in, dt_bias, a_log, d_skip, fgate_b, fcum_dram, tmp):
    nc = c.nc
    n2 = 2 * HEADS
    W = TT * n2
    d = Decays(c)
    hv = hT.rearrange("p (k s) -> p k s", k=KC)
    w = tmp[:, 0:KC * n2].rearrange("p (k n) -> p k n", k=KC)
    wide = lambda j: tmp[:, 256 + j * W:256 + (j + 1) * W]
    v3 = lambda ap: ap.rearrange("p (t n) -> p t n", t=TT)
    x, ax, e, u1, ln, eq, res = (wide(j) for j in range(7))
    bias = tmp[:, 2048:2048 + n2]
    a_neg = tmp[:, 2080:2080 + HEADS]
    run = tmp[0:HEADS, 4096:4096 + SEQ]
    one_row = tmp[0:HEADS, 5120:5120 + SEQ]
    fT = tmp[0:HEADS, 6144:6144 + SEQ]
    heads = lambda t, lo: v3(t)[:, :, lo:lo + HEADS]
    with ExitStack() as ctx:
        loaded, logits = c.sem(ctx, "dec_loaded"), c.sem(ctx, "dec_logits")
        step, act_step = c.sem(ctx, "dec_step"), c.sem(ctx, "dec_act")
        summed, turned = c.sem(ctx, "dec_summed"), c.sem(ctx, "dec_turned")
        stored = c.sem(ctx, "dec_stored")
        block = ctx.enter_context(nc.Block())

        @block.sync
        def _(sp):
            wv = cols(w_in)
            with nc.allow_non_contiguous_dma(reason="narrow columns and broadcasts, once"):
                sp.dma_start(w[:, :, 0:HEADS], wv[:, :, C_DT:C_DT + HEADS]).then_inc(loaded, 16)
                sp.dma_start(w[:, :, HEADS:n2], wv[:, :, C_F:C_F + HEADS]).then_inc(loaded, 16)
                sp.dma_start(bias[:, 0:HEADS], bcast(dt_bias, HEADS)).then_inc(loaded, 16)
                sp.dma_start(bias[:, HEADS:n2], bcast(fgate_b, HEADS)).then_inc(loaded, 16)
                sp.dma_start(a_neg, bcast(a_log, HEADS)).then_inc(loaded, 16)
                sp.dma_start(d.skip, bcast(d_skip, HEADS)).then_inc(loaded, 16)
            sp.wait_ge(step, RUN_DONE)
            sp.dma_start(fcum_dram, run).then_inc(stored, 16)
            sp.wait_ge(stored, 16)

        @block.tensor
        def _(pe):
            pe.wait_ge(loaded, 96)
            for t in range(TT):
                for k in range(KC):
                    mm = nc.tensor.matmul(c.ps[:, 0, t * n2:(t + 1) * n2], hv[:, k, t * P:(t + 1) * P],
                                          w[:, k, :], start=(k == 0), stop=(k == KC - 1))
            mm.then_inc(logits, 1)
            pe.wait_ge(step, DTA_DONE)
            nc.tensor.matmul(c.ps[:, 1, 0:P], c.upto[:], d.dta, start=True, stop=True)
            nc.tensor.matmul(c.ps[:, 2, 0:P], c.ones[:], d.dta, start=True, stop=True)\
                .then_inc(summed, 1)
            for t in range(TT):
                mm = nc.tensor.transpose(c.ps[0:HEADS, 3 + t // 4, (t % 4) * P:(t % 4 + 1) * P],
                                         heads(res, HEADS)[:, t, :], c.ident[:])
            mm.then_inc(turned, 1)

        @block.scalar
        def _(act):
            act.wait_ge(loaded, 96)
            nc.scalar.activation(a_neg, a_neg, ACT.Exp).then_inc(act_step, 1)
            act.wait_ge(step, 3)
            nc.scalar.activation(e, ax, ACT.Exp, scale=-1.0).then_inc(act_step, 1)
            act.wait_ge(step, 4)
            nc.scalar.activation(ln, u1, ACT.Ln).then_inc(act_step, 1)
            act.wait_ge(step, DECAY_ARGS)
            nc.scalar.activation(d.ecs, d.ncs, ACT.Exp, scale=-1.0).then_inc(act_step, 1)
            nc.scalar.activation(d.dte, d.dte, ACT.Exp).then_inc(act_step, 1)
            nc.scalar.activation(d.cdec, d.cdec, ACT.Exp).then_inc(act_step, 1)

        @block.vector
        def _(dve):
            st = Steps(dve, step)
            V = nc.vector
            dve.wait_ge(logits, 1)
            psv = c.ps[:, 0, 0:W]
            b = lambda t, n: t.unsqueeze(1).to_broadcast([P, TT, n])
            st.then_wait(V.tensor_tensor(v3(x), v3(psv), b(bias, n2), ALU.add))
            st.then_wait(V.tensor_scalar(heads(x, HEADS), heads(x, HEADS), -1.0, None, ALU.mult))
            st.then_wait(V.scalar_tensor_tensor(out=ax, in0=x, scalar=-1.0, in1=x, op0=ALU.mult,
                                                op1=ALU.max))
            dve.wait_ge(act_step, 2)
            st.then_wait(V.tensor_scalar(u1, e, 1.0, None, ALU.add))
            st.then_wait(V.tensor_scalar(eq, u1, 1.0, None, ALU.is_equal))
            st.then_wait(V.scalar_tensor_tensor(out=ax, in0=u1, scalar=-1.0, in1=eq, op0=ALU.add,
                                                op1=ALU.add))
            st.then_wait(V.reciprocal(ax, ax))
            dve.wait_ge(act_step, 3)
            st.then_wait(V.tensor_tensor(ln, ln, eq, ALU.add))
            st.then_wait(V.tensor_tensor(ln, ln, ax, ALU.mult))
            st.then_wait(V.tensor_tensor(ln, ln, e, ALU.mult))
            st.then_wait(V.scalar_tensor_tensor(out=res, in0=x, scalar=0.0, in1=ln, op0=ALU.max,
                                                op1=ALU.add))
            st.then_wait(V.tensor_scalar(a_neg, a_neg, -1.0, None, ALU.mult))
            st.done(V.tensor_copy(v3(d.dt), heads(res, 0)))
            st.done(V.tensor_tensor(v3(d.dta), heads(res, 0), b(a_neg, HEADS), ALU.mult))
            assert st.n == DTA_DONE
            st.done(V.memset(one_row, 1.0))
            dve.wait_ge(summed, 1)
            st.then_wait(V.tensor_scalar(d.ncs, c.ps[:, 1, 0:P], -1.0, None, ALU.mult))
            st.done(V.tensor_tensor(d.dte, c.ps[:, 2, 0:P], d.ncs, ALU.add))
            st.done(V.tensor_copy(d.cdec, c.ps[:, 2, 0:P]))
            assert st.n == DECAY_ARGS
            dve.wait_ge(turned, 1)
            st.then_wait(V.tensor_scalar(fT, c.ps[0:HEADS, 3:5, :].rearrange("p b n -> p (b n)"),
                                         float(HD) ** 0.5, None, ALU.mult))
            st.done(V.tensor_tensor_scan(run, one_row, fT, 0.0, ALU.mult, ALU.add))
            assert st.n == RUN_DONE
            dve.wait_ge(act_step, 5)
            st.then_wait(V.tensor_tensor(d.dte, d.dte, d.dt, ALU.mult))


DTA_DONE, DECAY_ARGS, RUN_DONE = 14, 18, 20


def phase_ssd(c, tok, bcT, y, tmp):
    nc = c.nc
    d = Decays(c)
    tokv = tok.rearrange("p (t n) -> p t n", t=TT)
    bcv = bcT.rearrange("p (b s) -> p b s", b=2 * GROUPS)
    N = HPG * P
    take = lambda a, n=512: tmp[:, a:a + n]
    decayed_in = [take(0), take(512)]
    dec = [take(1024), take(1536)]
    bTc, cTc, btok = take(2048), take(2560), take(3072)
    xdt, xde = take(3584, 1024), take(4608, 1024)
    prev, skipped = take(5632, 1024), take(6656, 1024)
    hv = lambda ap: ap.rearrange("p (h n) -> p h n", n=HD)
    with ExitStack() as ctx:
        S = lambda n: c.sem(ctx, "ssd_" + n)
        staged = S("staged")
        laid = S("laid")
        cb = S("cb")
        spread = S("spread")
        decayed = S("decayed")
        weighted = S("weighted")
        scaled = S("scaled")
        y_off, y_diag = S("y_off"), S("y_diag")
        state = S("state")
        skip = S("skip")
        part = S("part")
        carried = S("carried")
        summed = S("summed")
        block = ctx.enter_context(nc.Block())

        @block.scalar
        def _(act):
            act.sem_inc(y_diag, 4)
            act.sem_inc(state, 1)
            act.sem_inc(y_off, 1)
            with act.Fori(0, TT) as i:
                act.wait_ge(state, i + 1)
                for dst, src in ((bTc.rearrange("p (g s) -> p g s", g=4), bcv[:, 0:4, bass.ds(i * P, P)]),
                                 (cTc.rearrange("p (g s) -> p g s", g=4), bcv[:, 4:8, bass.ds(i * P, P)]),
                                 (btok, tokv[:, bass.ds(i, 1), D:D + 512].rearrange("p a n -> p (a n)"))):
                    nc.scalar.activation(dst, src, ACT.Identity).then_inc(staged, 1)
                for g in range(GROUPS):
                    act.wait_ge(spread, i * 4 + (g + 5))
                    act.wait_ge(y_diag, i * 4 + (g + 3))
                    for r in range(HPG):
                        h = g * HPG + r
                        x = nc.scalar.activation(dec[g % 2][:, r * P:(r + 1) * P],
                                                 c.ps[:, 1 + g % 2, r * P:(r + 1) * P], ACT.Exp,
                                                 bias=d.ncs[:, bass.ds(i * HEADS + h, 1)])
                    x.then_inc(decayed, 1)

        @block.gpsimd
        def _(pool):
            pool.sem_inc(spread, 4)
            with pool.Fori(0, TT) as i:
                for g in range(GROUPS):
                    pool.wait_ge(spread, i * 4 + (g + 3))
                    nc.gpsimd.tensor_tensor(
                        decayed_in[g % 2].rearrange("p (r l) -> p r l", r=HPG),
                        c.upto[:].unsqueeze(1).to_broadcast([P, HPG, P]),
                        d.dta[:, bass.ds(i * HEADS + g * HPG, HPG)].unsqueeze(2)
                        .to_broadcast([P, HPG, P]), ALU.mult).then_inc(laid, 1)
                pool.wait_ge(summed, i + 1)
                nc.gpsimd.tensor_tensor(
                    hv(skipped), hv(tokv[:, bass.ds(i, 1), 0:D].rearrange("p a n -> p (a n)")),
                    d.skip.unsqueeze(2).to_broadcast([P, HEADS, HD]), ALU.mult).then_inc(skip, 1)

        @block.tensor
        def _(pe):
            with pe.Fori(0, TT) as i:
                pe.wait_ge(staged, i * 3 + 3)
                pe.wait_ge(weighted, i * 4 + 4)
                pe.wait_ge(carried, i + 1)
                for g in range(GROUPS):
                    mm = nc.tensor.matmul(c.ps[:, 0, g * P:(g + 1) * P], bTc[:, g * P:(g + 1) * P],
                                          cTc[:, g * P:(g + 1) * P], start=True, stop=True)
                mm.then_inc(cb, 1)

                def running(g):
                    pe.wait_ge(laid, i * 4 + (g + 1))
                    pe.wait_ge(decayed, i * 4 + (g + 3))
                    bank = c.ps[:, 1 + g % 2, :]
                    nc.tensor.matmul(bank, c.identb[:], c.maskTb[:].rearrange("p r l -> p (r l)"),
                                     start=True, stop=False, skip_group_check=True)
                    nc.tensor.matmul(bank, c.ones[:], decayed_in[g % 2], start=False, stop=True,
                                     skip_group_check=True).then_inc(spread, 1)

                def diagonal(g):
                    pe.wait_ge(weighted, i * 4 + (g + 5))
                    for r in range(HPG):
                        h = g * HPG + r
                        mm = nc.tensor.matmul(c.ps[:, 3 + h // 8, (h % 8) * HD:(h % 8 + 1) * HD],
                                              dec[g % 2][:, r * P:(r + 1) * P],
                                              xdt[:, h * HD:(h + 1) * HD], start=True, stop=True)
                    mm.then_inc(y_diag, 1)

                running(0)
                running(1)
                pe.wait_ge(summed, i + 1)
                for g in range(GROUPS):
                    mm = nc.tensor.matmul(c.ps[:, 5 + g // 2, (g % 2) * 256:(g % 2 + 1) * 256],
                                          cTc[:, g * P:(g + 1) * P],
                                          prev[:, g * 256:(g + 1) * 256], start=True, stop=True)
                mm.then_inc(y_off, 1)
                running(2)
                pe.wait_ge(scaled, i * 2 + 2)
                diagonal(0)
                running(3)
                for g in range(1, GROUPS):
                    diagonal(g)
                for g in range(GROUPS):
                    mm = nc.tensor.matmul(c.ps[:, (7, 0)[g // 2], (g % 2) * 256:(g % 2 + 1) * 256],
                                          btok[:, g * P:(g + 1) * P],
                                          xde[:, g * 256:(g + 1) * 256], start=True, stop=True)
                mm.then_inc(state, 1)

        @block.vector
        def _(dve):
            V = nc.vector
            dve.sem_inc(decayed, 4)
            dve.sem_inc(weighted, 4)
            dve.sem_inc(summed, 1)
            dve.sem_inc(part, 1)
            V.memset(prev, 0.0).then_inc(carried, 1)
            with dve.Fori(0, TT) as i:
                xs = hv(tokv[:, bass.ds(i, 1), 0:D].rearrange("p a n -> p (a n)"))
                col = lambda t: t[:, bass.ds(i * HEADS, HEADS)].unsqueeze(2)\
                    .to_broadcast([P, HEADS, HD])
                dve.wait_ge(state, i + 1)
                V.tensor_tensor(hv(xdt), xs, col(d.dt), ALU.mult).then_inc(scaled, 1)
                V.tensor_tensor(hv(xde), xs, col(d.dte), ALU.mult).then_inc(scaled, 1)
                dve.wait_ge(cb, i + 1)
                for g in range(GROUPS):
                    dve.wait_ge(decayed, i * 4 + (g + 5))
                    m = dec[g % 2].rearrange("p (r l) -> p r l", r=HPG)
                    V.tensor_tensor(m, m, c.ps[:, 0, g * P:(g + 1) * P].unsqueeze(1)
                                    .to_broadcast([P, HPG, P]), ALU.mult).then_inc(weighted, 1)
                dve.wait_ge(y_off, i + 2)
                yc = y[:, bass.ds(i * D, D)]
                flat = lambda b: c.ps[:, b:b + 2, :].rearrange("p b n -> p (b n)")
                V.tensor_tensor(hv(yc), hv(flat(5)), col(d.ecs), ALU.mult).then_inc(part, 1)
                dve.wait_ge(carried, i + 1)
                V.tensor_tensor(hv(prev), hv(prev), col(d.cdec), ALU.mult).then_inc(part, 1)
                dve.wait_ge(part, i * 4 + 3)
                dve.wait_ge(y_diag, i * 4 + 8)
                V.tensor_tensor(yc, yc, flat(3), ALU.add).then_inc(part, 1)
                dve.wait_ge(state, i + 2)
                V.tensor_tensor(prev[:, 0:512], prev[:, 0:512], c.ps[:, 7, :], ALU.add)\
                    .then_inc(part, 1)
                V.tensor_tensor(prev[:, 512:1024], prev[:, 512:1024], c.ps[:, 0, :], ALU.add)\
                    .then_inc(carried, 1)
                dve.wait_ge(part, i * 4 + 5)
                dve.wait_ge(skip, i + 1)
                V.tensor_tensor(yc, yc, skipped, ALU.add).then_inc(summed, 1)


def phase_dense(c, name, jobs, region):
    nc = c.nc
    raw = [c.at(region, u * 2 * BANK, 2 * BANK).rearrange("p (k n) -> p k n", k=2) for u in range(2)]
    wp = [c.rounded(f"{name}_w{s}", region, 4 * BANK + s * 2 * BANK, BANK) for s in range(2)]
    tp = [c.rounded(f"{name}_t{s}", region, 8 * BANK + s * 2 * SEQ, SEQ) for s in range(2)]
    steps = [(j, k) for j, job in enumerate(jobs) for k in range(job[1].shape[1])]
    NS = len(steps)
    last = [sum(j[1].shape[1] for j in jobs[:n + 1]) - 1 for n in range(len(jobs))]
    on_act = [j[2] == "act" for j in jobs]
    before = lambda n, act: TT * sum(1 for x in on_act[:n] if x == act)
    with ExitStack() as ctx:
        wload = [c.sem(ctx, f"{name}_wload{s}") for s in range(2)]
        w_high, w_low = c.sem(ctx, f"{name}_w_high"), c.sem(ctx, f"{name}_w_low")
        t_high, t_low = c.sem(ctx, f"{name}_t_high"), c.sem(ctx, f"{name}_t_low")
        stepped = c.sem(ctx, f"{name}_stepped")
        product = c.sem(ctx, f"{name}_product")
        by_act = c.sem(ctx, f"{name}_by_act")
        by_vec = c.sem(ctx, f"{name}_by_vec")
        multiplied = c.sem(ctx, f"{name}_multiplied")
        block = ctx.enter_context(nc.Block())

        @block.sync
        def _(sp):
            for u in range(NS // 2):
                j, k = steps[2 * u]
                if u >= 2:
                    sp.wait_ge(w_low, 2 * (u - 1))
                sp.dma_start(raw[u % 2], jobs[j][1][:, k:k + 2, :]).then_inc(wload[u % 2], 16)

        @block.tensor
        def _(pe):
            for n, (j, k) in enumerate(steps):
                s = n % 2
                pe.wait_ge(w_low, n + 1)
                pe.wait_ge(t_low, n + 1)
                for t in range(TT):
                    if k == 0 and j >= 1:
                        pe.wait_ge(by_act if on_act[j - 1] else by_vec,
                                   before(j - 1, on_act[j - 1]) + t + 1)
                    tile = slice(t * P, (t + 1) * P)
                    nc.tensor.matmul(c.ps[:, t, :], tp[s][0][:, tile], wp[s][0], start=(k == 0),
                                     stop=False)
                    nc.tensor.matmul(c.ps[:, t, :], tp[s][0][:, tile], wp[s][1], start=False,
                                     stop=False)
                    mm = nc.tensor.matmul(c.ps[:, t, :], tp[s][1][:, tile], wp[s][0], start=False,
                                          stop=(n == last[j]))
                    if n == last[j]:
                        mm.then_inc(product, 1)
                if n != last[j]:
                    mm.then_inc(stepped, 1)
                else:
                    pe.wait_ge(product, TT * (j + 1))
                    pe.sem_inc(stepped, 1)

        @block.scalar
        def _(act):
            def high_parts(n):
                j, k = steps[n]
                s = n % 2
                if n >= 2:
                    act.wait_ge(stepped, n - 1)
                nc.scalar.activation(tp[s][0], jobs[j][0][:, k, :], ACT.Identity).then_inc(t_high, 1)
                act.wait_ge(wload[n // 2 % 2], 16 * (n // 4 + 1))
                nc.scalar.activation(wp[s][0], raw[n // 2 % 2][:, n % 2, :], ACT.Identity)\
                    .then_inc(w_high, 1)

            for n in range(NS + 1):
                if n < NS:
                    high_parts(n)
                j = steps[n - 1][0]
                if n >= 1 and n - 1 == last[j] and on_act[j]:
                    for t in range(TT):
                        act.wait_ge(product, TT * j + t + 1)
                        nc.scalar.activation(jobs[j][3][:, t, :], c.ps[:, t, :], jobs[j][4])\
                            .then_inc(by_act, 1)

        @block.vector
        def _(dve):
            V = nc.vector

            def low_parts(n):
                j, k = steps[n]
                s = n % 2
                dve.wait_ge(t_high, n + 1)
                V.tensor_tensor(tp[s][1], jobs[j][0][:, k, :], tp[s][0].bitcast(F32), ALU.subtract)\
                    .then_inc(t_low, 1)
                dve.wait_ge(w_high, n + 1)
                V.tensor_tensor(wp[s][1], raw[n // 2 % 2][:, n % 2, :], wp[s][0].bitcast(F32),
                                ALU.subtract).then_inc(w_low, 1)

            pairs = 0
            for n in range(NS + 1):
                if n < NS:
                    low_parts(n)
                if n == 0 or n - 1 != last[steps[n - 1][0]]:
                    continue
                j = steps[n - 1][0]
                _, _, kind, dst, other = jobs[j]
                if kind == "act":
                    continue
                if before(j, True):
                    dve.wait_ge(by_act, before(j, True))
                for t in range(TT):
                    dve.wait_ge(product, TT * j + t + 1)
                    src = c.ps[:, t, :]
                    if kind == "mul":
                        x = V.tensor_tensor(dst[:, t, :], src, other[:, t, :], ALU.mult)
                    elif kind == "add":
                        x = V.tensor_tensor(dst[:, t, :], src, dst[:, t, :], ALU.add)
                    else:
                        V.tensor_tensor(other[:, t, :], src, other[:, t, :], ALU.mult)\
                            .then_inc(multiplied, 1)
                        pairs += 1
                        dve.wait_ge(multiplied, pairs)
                        x = V.tensor_tensor(dst[:, t, :], other[:, t, :], dst[:, t, :], ALU.add)
                    x.then_inc(by_vec, 1)


def phase_turn(c, name, src, dst, gate=None, groups=0, gain_dram=None, gain_times=1.0, width=D):
    nc = c.nc
    n_k = width // P
    gw = width // max(groups, 1)
    sv = src.rearrange("p (t d) -> p t d", t=TT)
    gv = gate.rearrange("p (t d) -> p t d", t=TT) if gate is not None else None
    dv = dst.rearrange("p (k s) -> p k s", k=n_k)
    ng = max(groups, 1)
    ss = c.small[:, 0:TT * ng]
    rstd, gain = c.small[:, 32:32 + TT * ng], c.small[:, 64:64 + n_k]
    with ExitStack() as ctx:
        loaded, squared = c.sem(ctx, f"{name}_loaded"), c.sem(ctx, f"{name}_squared")
        gated, rooted = c.sem(ctx, f"{name}_gated"), c.sem(ctx, f"{name}_rooted")
        step, ready = c.sem(ctx, f"{name}_step"), c.sem(ctx, f"{name}_ready")
        turned, placed = c.sem(ctx, f"{name}_turned"), c.sem(ctx, f"{name}_placed")
        block = ctx.enter_context(nc.Block())
        halves = n_k // 4

        @block.sync
        def _(sp):
            if gain_dram is not None:
                with nc.allow_non_contiguous_dma(reason="a gain vector by chunks"):
                    g = gain_dram.rearrange("(k p) -> p k", p=P)
                    if g.shape[1] == 1 and n_k > 1:
                        for k in range(n_k):
                            sp.dma_start(gain[:, k:k + 1], g).then_inc(loaded, 16)
                    else:
                        sp.dma_start(gain, g).then_inc(loaded, 16)

        loads = 0 if gain_dram is None else (16 * n_k if gain_dram.shape[0] == P else 16)

        @block.scalar
        def _(act):
            if groups:
                for t in range(TT):
                    if gate is not None:
                        act.wait_ge(gated, t + 1)
                    for g in range(groups):
                        nc.scalar.activation(dst[:, t * width + g * gw:t * width + (g + 1) * gw],
                                             sv[:, t, g * gw:(g + 1) * gw], ACT.Square,
                                             accum_out=ss[:, t * ng + g:t * ng + g + 1])\
                            .then_inc(squared, 1)
                act.wait_ge(step, 1)
                nc.scalar.activation(rstd, rstd, ACT.Sqrt).then_inc(rooted, 1)

        @block.vector
        def _(dve):
            V = nc.vector
            if gate is not None:
                for t in range(TT):
                    V.tensor_tensor(sv[:, t, :], sv[:, t, :], gv[:, t, :], ALU.mult).then_inc(gated, 1)
            if groups:
                st = Steps(dve, step)
                dve.wait_ge(squared, TT * groups)
                st.done(V.tensor_scalar(rstd, ss, 1.0 / gw, EPS, ALU.mult, ALU.add))
                dve.wait_ge(rooted, 1)
                st.then_wait(V.reciprocal(rstd, rstd))
                for t in range(TT):
                    row = sv[:, t, :].rearrange("p (g n) -> p g n", g=groups)
                    V.tensor_tensor(row, row, rstd[:, t * ng:(t + 1) * ng].unsqueeze(2)
                                    .to_broadcast([P, groups, gw]), ALU.mult).then_inc(ready, 1)
            if gain_dram is not None:
                dve.wait_ge(loaded, loads)
                if gain_times != 1.0:
                    V.tensor_scalar(gain, gain, gain_times, None, ALU.mult).then_inc(loaded, 16)
                    dve.wait_ge(loaded, loads + 16)
            for n in range(halves * TT):
                t, h = divmod(n, halves)
                dve.wait_ge(turned, n + 1)
                out = dv[:, 4 * h:4 * h + 4, t * P:(t + 1) * P]
                ps = c.ps[:, n % 8, :].rearrange("p (k s) -> p k s", k=4)
                if gain_dram is None:
                    x = V.tensor_copy(out, ps)
                else:
                    x = V.tensor_tensor(out, ps, gain[:, 4 * h:4 * h + 4].unsqueeze(2)
                                        .to_broadcast([P, 4, P]), ALU.mult)
                x.then_inc(placed, 1)

        @block.tensor
        def _(pe):
            for n in range(halves * TT):
                t, h = divmod(n, halves)
                if groups:
                    pe.wait_ge(ready, t + 1)
                elif gate is not None:
                    pe.wait_ge(gated, t + 1)
                if n >= 8:
                    pe.wait_ge(placed, n - 7)
                for k in range(4):
                    mm = nc.tensor.transpose(c.ps[:, n % 8, k * P:(k + 1) * P],
                                             sv[:, t, (4 * h + k) * P:(4 * h + k + 1) * P],
                                             c.ident[:])
                mm.then_inc(turned, 1)


def phase_forget_attention(c, hT, w_in, fcum_dram, v, yT, qk, wslots, probs, tmp):
    nc = c.nc
    hv = hT.rearrange("p (k s) -> p k s", k=KC)
    vv = v.rearrange("p (t n) -> p t n", t=TT)
    SCALE = float(HD) ** -0.5
    q = [qk[:, r * SEQ:(r + 1) * SEQ] for r in range(2)]
    k_ = [qk[:, (2 + r) * SEQ:(3 + r) * SEQ] for r in range(2)]
    w = [wslots[:, s * D:(s + 1) * D].rearrange("p (k n) -> p k n", k=KC) for s in range(3)]
    prob = [probs[:, r * SEQ:(r + 1) * SEQ] for r in range(2)]
    probT = [probs[:, (2 + r) * SEQ:(3 + r) * SEQ] for r in range(2)]
    v_pair = probs[:, 4 * SEQ:5 * SEQ].rearrange("p (t n) -> p t n", t=TT)
    gate = tmp[:, 0:SEQ]
    negmax, rowsum, rinv = c.small[:, 1400:1402], c.small[:, 1402:1404], c.small[:, 1404:1406]
    PAIRS = HEADS // 2
    UNITS = [(r, t) for t in range(TT) for r in range(2)]
    NU = len(UNITS)
    GR = [(u, g) for u, (r, t) in enumerate(UNITS) for g in range(t // 4 + 1)]
    NGR = len(GR)
    first_group = {u: n for n, (u, g) in reversed(list(enumerate(GR)))}
    S_BANK, T_BANK, O_BANK = (4, 6), (0, 1), (2, 3)
    flat = lambda b: c.ps[:, b:b + 2, :].rearrange("p b n -> p (b n)")
    with ExitStack() as ctx:
        S = lambda n: c.sem(ctx, "fa_" + n)
        wload = [S("wload0"), S("wload1"), S("wload2")]
        sums = S("sums")
        padded = S("padded")
        projected = S("projected")
        split = S("split")
        opened = S("opened")
        staged = S("staged")
        scored = S("scored")
        maxed = S("maxed")
        negated = S("negated")
        exped = S("exped")
        inverted = S("inverted")
        normed = S("normed")
        turned = S("turned")
        placed = S("placed")
        summed = S("summed")
        stored = S("stored")
        block = ctx.enter_context(nc.Block())

        @block.sync
        def _(sp):
            wv = cols(w_in)
            with sp.Fori(0, PAIRS) as i:
                sp.wait_ge(split, i * 4 + 4)
                sp.dma_start(w[0], wv[:, :, bass.ds(i * P + C_Q, P)]).then_inc(wload[0], 16)
                sp.dma_start(w[1], wv[:, :, bass.ds(i * P + C_K, P)]).then_inc(wload[1], 16)
                sp.wait_ge(opened, i + 1)
                sp.dma_start(w[2], wv[:, :, bass.ds(i * P + C_ZA, P)]).then_inc(wload[2], 16)
                sp.wait_ge(padded, 4)
                sp.wait_ge(summed, i * NU + 2)
                for r in range(2):
                    sp.dma_start(k_[r][HD:HD + 1, :], fcum_dram[bass.ds(i * 2 + r, 1), :])\
                        .then_inc(sums, 16)

        @block.tensor
        def _(pe):
            pe.sem_inc(summed, 2)
            pe.sem_inc(turned, 1)
            pe.wait_ge(padded, 6)
            with pe.Fori(0, PAIRS) as i:
                pe.wait_ge(exped, i * NU + 2)
                pe.wait_ge(stored, i * NU + 2)
                for j, bank in enumerate((4, 6, 0)):
                    pe.wait_ge(wload[j], i * 16 + 16)
                    for k in range(KC):
                        for h in range(2):
                            mm = nc.tensor.matmul(c.ps[:, bank + h, :], w[j][:, k, :],
                                                  hv[:, k, h * BANK:(h + 1) * BANK],
                                                  start=(k == 0), stop=(k == KC - 1))
                    mm.then_inc(projected, 1)
                pe.wait_ge(split, i * 4 + 8)
                pe.wait_ge(sums, i * 32 + 32)

                def score(u):
                    r, t = UNITS[u]
                    n = (t + 1) * P
                    pe.wait_ge(exped, i * NU + (u + 1))
                    for b in range((n + BANK - 1) // BANK):
                        width = min(BANK, n - b * BANK)
                        has_diag = (b + 1) * BANK >= n
                        nc.tensor.matmul(c.ps[:, S_BANK[u % 2] + b, 0:width],
                                         q[r][:, t * P:(t + 1) * P],
                                         k_[r][:, b * BANK:b * BANK + width],
                                         start=True, stop=not has_diag, skip_group_check=True)
                    nc.tensor.matmul(c.ps[:, S_BANK[u % 2] + b, width - P:width],
                                     c.identb[:], c.maskb[:], start=False, stop=True,
                                     skip_group_check=True).then_inc(scored, 1)

                def turn(u):
                    r, t = UNITS[u]
                    pe.wait_ge(normed, i * NU + (u + 3))
                    for g in range(t // 4 + 1):
                        n = first_group[u] + g
                        pe.wait_ge(placed, i * NGR + (n + 1))
                        for b in range(min(4, t + 1 - 4 * g)):
                            mm = nc.tensor.transpose(
                                c.ps[:, T_BANK[n % 2], b * P:(b + 1) * P],
                                prob[u % 2][:, (4 * g + b) * P:(4 * g + b + 1) * P], c.ident[:])
                        mm.then_inc(turned, 1)

                def values(u):
                    r, t = UNITS[u]
                    pe.wait_ge(stored, i * NU + (u + 1))
                    pe.wait_ge(placed, i * NGR + (first_group[u] + t // 4 + 3))
                    if u == 0:
                        pe.wait_ge(staged, i + 2)
                    for b in range(t + 1):
                        mm = nc.tensor.matmul(c.ps[r * HD:(r + 1) * HD, O_BANK[u % 2], 0:P],
                                              v_pair[:, b, r * HD:(r + 1) * HD],
                                              probT[u % 2][:, b * P:(b + 1) * P],
                                              start=(b == 0), stop=(b == t))
                    mm.then_inc(summed, 1)

                score(0)
                score(1)
                pe.wait_ge(opened, i + 2)
                for u in range(NU):
                    turn(u)
                    if u + 2 < NU:
                        score(u + 2)
                    values(u)

        @block.scalar
        def _(act):
            act.sem_inc(exped, 2)
            act.sem_inc(opened, 1)
            act.sem_inc(staged, 1)
            with act.Fori(0, PAIRS) as i:
                act.wait_ge(projected, i * 3 + 1)
                for r in range(2):
                    nc.scalar.activation(
                        q[r][0:HD, :], c.ps[r * HD:(r + 1) * HD, 4:6, :].rearrange("p b n -> p (b n)"),
                        ACT.Identity).then_inc(split, 1)
                act.wait_ge(summed, i * NU + 2)
                nc.scalar.activation(v_pair, vv[:, :, bass.ds(i * P, P)], ACT.Identity)\
                    .then_inc(staged, 1)
                act.wait_ge(projected, i * 3 + 3)
                act.wait_ge(stored, i * NU + 2)
                nc.scalar.activation(gate, flat(0), ACT.Silu).then_inc(opened, 1)
                for u, (r, t) in enumerate(UNITS):
                    n = (t + 1) * P
                    act.wait_ge(negated, i * NU + (u + 3))
                    last = (first_group[u - 2] + UNITS[u - 2][1] // 4 + 2 if u >= 2 else 1)
                    act.wait_ge(turned, i * NGR + last)
                    nc.scalar.activation(prob[u % 2][:, 0:n], flat(S_BANK[u % 2])[:, 0:n], ACT.Exp,
                                         scale=SCALE, bias=negmax[:, u % 2:u % 2 + 1],
                                         accum_out=rowsum[:, u % 2:u % 2 + 1]).then_inc(exped, 1)

        @block.gpsimd
        def _(pool):
            for r in range(2):
                for m in (q[r], k_[r]):
                    nc.gpsimd.memset(m[HD:P, :], 0.0).then_inc(padded, 1)
            pool.wait_ge(padded, 4)
            for r in range(2):
                nc.gpsimd.memset(q[r][HD:HD + 1, :], 1.0).then_inc(padded, 1)

        @block.vector
        def _(dve):
            V = nc.vector
            dve.sem_inc(split, 4)
            dve.sem_inc(negated, 2)
            dve.sem_inc(placed, 2)
            dve.sem_inc(normed, 2)
            dve.sem_inc(stored, 2)
            with dve.Fori(0, PAIRS) as i:
                dve.wait_ge(projected, i * 3 + 2)
                for r in range(2):
                    V.tensor_copy(k_[r][0:HD, :], c.ps[r * HD:(r + 1) * HD, 6:8, :]
                                  .rearrange("p b n -> p (b n)")).then_inc(split, 1)

                def maxima(u):
                    r, t = UNITS[u]
                    n = (t + 1) * P
                    m = negmax[:, u % 2:u % 2 + 1]
                    dve.wait_ge(scored, i * NU + (u + 1))
                    dve.wait_ge(exped, i * NU + (u + 1))
                    V.tensor_reduce(m, flat(S_BANK[u % 2])[:, 0:n], AX.X, ALU.max).then_inc(maxed, 1)
                    dve.wait_ge(maxed, i * NU + (u + 1))
                    V.tensor_scalar(m, m, -SCALE, None, ALU.mult).then_inc(negated, 1)

                def norm(u):
                    r, t = UNITS[u]
                    n = (t + 1) * P
                    dve.wait_ge(exped, i * NU + (u + 3))
                    V.reciprocal(rinv[:, u % 2:u % 2 + 1], rowsum[:, u % 2:u % 2 + 1])\
                        .then_inc(inverted, 1)
                    dve.wait_ge(inverted, i * NU + (u + 1))
                    V.tensor_scalar(prob[u % 2][:, 0:n], prob[u % 2][:, 0:n],
                                    rinv[:, u % 2:u % 2 + 1], None, ALU.mult).then_inc(normed, 1)

                def take(u):
                    r, t = UNITS[u]
                    for g in range(t // 4 + 1):
                        n = first_group[u] + g
                        dve.wait_ge(turned, i * NGR + (n + 2))
                        width = min(4, t + 1 - 4 * g) * P
                        if g == 0:
                            dve.wait_ge(summed, i * NU + (u + 1))
                        V.tensor_copy(probT[u % 2][:, 4 * g * P:4 * g * P + width],
                                      c.ps[:, T_BANK[n % 2], 0:width]).then_inc(placed, 1)

                def store(u):
                    r, t = UNITS[u]
                    dve.wait_ge(summed, i * NU + (u + 3))
                    rows = slice(r * HD, (r + 1) * HD)
                    V.tensor_tensor(yT[rows, bass.ds(i * SEQ + t * P, P)],
                                    c.ps[rows, O_BANK[u % 2], 0:P], gate[rows, t * P:(t + 1) * P],
                                    ALU.mult).then_inc(stored, 1)

                maxima(0)
                maxima(1)
                norm(0)
                dve.wait_ge(opened, i + 2)
                for u in range(NU):
                    take(u)
                    if u + 1 < NU:
                        norm(u + 1)
                    if u + 2 < NU:
                        maxima(u + 2)
                    store(u)


def phase_post(c, x_dram, gain_dram, src, dst, tmp):
    nc = c.nc
    v = lambda r: r.rearrange("p (t d) -> p t d", t=TT)
    sv, dv = v(src), v(dst)
    gain = tmp[:, 0:D]
    sq = tmp[:, D:2 * D]
    ss, rstd = c.small[:, 0:8], c.small[:, 8:16]
    with ExitStack() as ctx:
        loaded = [c.sem(ctx, f"post_loaded{t}") for t in range(3)]
        squared, rooted = c.sem(ctx, "post_squared"), c.sem(ctx, "post_rooted")
        step = c.sem(ctx, "post_step")
        block = ctx.enter_context(nc.Block())

        @block.sync
        def _(sp):
            sp.dma_start(gain, bcast(gain_dram, D)).then_inc(loaded[2], 16)
            rows = x_dram.rearrange("(t p) d -> p t d", p=P)
            for t in range(2):
                sp.dma_start(dv[:, 4 * t:4 * t + 4, :], rows[:, 4 * t:4 * t + 4, :])\
                    .then_inc(loaded[t], 16)

        @block.scalar
        def _(act):
            for t in range(TT):
                if t:
                    act.wait_ge(squared, t)
                nc.scalar.activation(sq, sv[:, t, :], ACT.Square, accum_out=ss[:, t:t + 1])\
                    .then_inc(squared, 1)
            act.wait_ge(step, 1)
            nc.scalar.activation(rstd, rstd, ACT.Sqrt).then_inc(rooted, 1)

        @block.vector
        def _(dve):
            V = nc.vector
            st = Steps(dve, step)
            dve.wait_ge(squared, TT)
            st.done(V.tensor_scalar(rstd, ss, 1.0 / D, EPS, ALU.mult, ALU.add))
            dve.wait_ge(rooted, 1)
            st.then_wait(V.reciprocal(rstd, rstd))
            dve.wait_ge(loaded[2], 16)
            for t in range(TT):
                st.then_wait(V.scalar_tensor_tensor(out=sv[:, t, :], in0=sv[:, t, :],
                                                    scalar=rstd[:, t:t + 1], in1=gain,
                                                    op0=ALU.mult, op1=ALU.mult))
                if t % 4 == 0:
                    dve.wait_ge(loaded[t // 4], 16)
                st.done(V.tensor_tensor(dv[:, t, :], dv[:, t, :], sv[:, t, :], ALU.add))


def phase_conformer(c, hT, w_in, dw_w, jobs, y, acc, gate, wblk, wslots, raw_taps):
    nc = c.nc
    NB = CCH // P
    PAD = CW - 1
    hv = hT.rearrange("p (k s) -> p k s", k=KC)
    yv = y.rearrange("p (b n) -> p b n", b=NB)
    accv = acc.rearrange("p (b n) -> p b n", b=NB)
    w = [wblk[:, s * D:(s + 1) * D].rearrange("p (k n) -> p k n", k=KC) for s in range(2)]
    taps = c.small[:, 1024:1024 + NB * CW]
    bias = c.small[:, 1160:1160 + NB]
    jw = [wslots[n % 2].rearrange("p (k n) -> p k n", k=KC) for n in range(len(jobs))]
    (dw_w, dw_b) = dw_w
    with ExitStack() as ctx:
        S = lambda n: c.sem(ctx, "cf_" + n)
        params, tap_turned, tap_placed = S("params"), S("tap_turned"), S("tap_placed")
        wload = [S("wload0"), S("wload1")]
        jload = [S("jload0"), S("jload1")]
        projected = S("projected")
        opened = S("opened")
        gated = S("gated")
        tapped = S("tapped")
        padded = S("padded")
        product, taken = S("product"), S("taken")
        block = ctx.enter_context(nc.Block())

        @block.sync
        def _(sp):
            sp.dma_start(raw_taps[0:CW, 0:CCH], dw_w).then_inc(params, 16)
            with nc.allow_non_contiguous_dma(reason="a bias vector by chunks"):
                sp.dma_start(bias, dw_b.rearrange("(b p) -> p b", p=P)).then_inc(params, 16)
            wv = cols(w_in)
            with sp.Fori(0, NB) as i:
                sp.wait_ge(projected, i * 2 + 1)
                sp.dma_start(w[0], wv[:, :, bass.ds(i * P, P)]).then_inc(wload[0], 16)
                sp.wait_ge(projected, i * 2 + 2)
                sp.dma_start(w[1], wv[:, :, bass.ds(i * P + CCH, P)]).then_inc(wload[1], 16)
            sp.wait_ge(tap_turned, 1)
            for n, job in enumerate(jobs):
                if n >= 2:
                    sp.wait_ge(product, TT * (n - 1))
                sp.dma_start(jw[n], job[1]).then_inc(jload[n % 2], 16)

        @block.tensor
        def _(pe):
            pe.wait_ge(params, 32)
            for b in range(NB):
                mm = nc.tensor.transpose(c.ps[:, 7, b * CW:(b + 1) * CW],
                                         raw_taps[0:CW, b * P:(b + 1) * P], c.ident[0:CW, 0:CW])
            mm.then_inc(tap_turned, 1)
            pe.sem_inc(projected, 2)
            with pe.Fori(0, NB) as i:
                for j in range(2):
                    pe.wait_ge(wload[j], i * 16 + 16)
                    pe.wait_ge(gated if j == 0 else opened, i + 1)
                    for k in range(KC):
                        for h in range(2):
                            mm = nc.tensor.matmul(c.ps[:, 2 * j + h, :], w[j][:, k, :],
                                                  hv[:, k, h * BANK:(h + 1) * BANK],
                                                  start=(k == 0), stop=(k == KC - 1))
                    mm.then_inc(projected, 1)
            pe.wait_ge(tap_placed, 1)
            for n, job in enumerate(jobs):
                pe.wait_ge(jload[n % 2], 16 * (n // 2 + 1))
                for t in range(TT):
                    m = n * TT + t
                    if m >= 4:
                        pe.wait_ge(taken, m - 3)
                    for k in range(KC):
                        mm = nc.tensor.matmul(c.ps[:, 4 + t % 4, :], job[0][:, k, t * P:(t + 1) * P],
                                              jw[n][:, k, :], start=(k == 0), stop=(k == KC - 1))
                    mm.then_inc(product, 1)

        @block.scalar
        def _(act):
            act.sem_inc(opened, 1)
            with act.Fori(0, NB) as i:
                act.wait_ge(projected, i * 2 + 4)
                act.wait_ge(gated, i + 1)
                nc.scalar.activation(gate, c.ps[:, 2:4, :].rearrange("p b n -> p (b n)"),
                                     ACT.Sigmoid).then_inc(opened, 1)
            for n, (_, _, _, dst, func) in enumerate(jobs):
                for t in range(TT):
                    act.wait_ge(product, n * TT + t + 1)
                    nc.scalar.activation(dst[:, t, :], c.ps[:, 4 + t % 4, :], func).then_inc(taken, 1)

        @block.vector
        def _(dve):
            V = nc.vector
            dve.wait_ge(tap_turned, 1)
            V.tensor_copy(taps, c.ps[:, 7, 0:NB * CW]).then_inc(tap_placed, 1)
            for b in range(NB):
                V.memset(yv[:, b, 0:PAD], 0.0).then_inc(padded, 1)
            dve.sem_inc(gated, 1)
            dve.wait_ge(tap_placed, 1)
            dve.wait_ge(padded, NB)
            dve.wait_ge(params, 32)
            with dve.Fori(0, NB) as i:
                dve.wait_ge(opened, i + 2)
                row = lambda j, n=SEQ: y[:, bass.ds(i * (SEQ + PAD) + j, n)]
                a_i = acc[:, bass.ds(i * SEQ, SEQ)]
                V.tensor_tensor(row(PAD), c.ps[:, 0:2, :].rearrange("p b n -> p (b n)"), gate,
                                ALU.mult).then_inc(gated, 1)
                dve.wait_ge(gated, i + 2)
                V.tensor_scalar(a_i, row(0), taps[:, bass.ds(i * CW, 1)], bias[:, bass.ds(i, 1)],
                                ALU.mult, ALU.add).then_inc(tapped, 1)
                for j in range(1, CW):
                    dve.wait_ge(tapped, i * CW + j)
                    V.scalar_tensor_tensor(out=a_i, in0=row(j), scalar=taps[:, bass.ds(i * CW + j, 1)],
                                           in1=a_i, op0=ALU.mult, op1=ALU.add).then_inc(tapped, 1)


def phase_channel_norm(c, acc, sq, rstd, g_dram, b_dram):
    nc = c.nc
    NB = CCH // P
    av = acc.rearrange("p (b n) -> p b n", b=NB)
    qv = sq.rearrange("p (b n) -> p b n", b=NB)
    g, b_ = c.small[:, 0:NB], c.small[:, 8:8 + NB]
    flat = lambda b: c.ps[:, b:b + 2, :].rearrange("p b n -> p (b n)")
    with ExitStack() as ctx:
        S = lambda n: c.sem(ctx, "cn_" + n)
        params, meaned, centred, squared = S("params"), S("meaned"), S("centred"), S("squared")
        spread, step, rooted, scaled, done = S("spread"), S("step"), S("rooted"), S("scaled"), S("done")
        block = ctx.enter_context(nc.Block())

        @block.sync
        def _(sp):
            with nc.allow_non_contiguous_dma(reason="per-channel vectors by chunks"):
                sp.dma_start(g, g_dram.rearrange("(b p) -> p b", p=P)).then_inc(params, 16)
                sp.dma_start(b_, b_dram.rearrange("(b p) -> p b", p=P)).then_inc(params, 16)

        @block.tensor
        def _(pe):
            def over_channels(src, bank, ready):
                for b in range(NB):
                    if ready is not None:
                        pe.wait_ge(ready, b + 1)
                    for h in range(2):
                        mm = nc.tensor.matmul(c.ps[:, bank + h, :], c.ones[:],
                                              src[:, b, h * BANK:(h + 1) * BANK],
                                              start=(b == 0), stop=(b == NB - 1))
                return mm
            over_channels(av, 0, None).then_inc(meaned, 1)
            over_channels(qv, 2, squared).then_inc(spread, 1)

        @block.scalar
        def _(act):
            for b in range(NB):
                act.wait_ge(centred, b + 1)
                nc.scalar.activation(qv[:, b, :], av[:, b, :], ACT.Square).then_inc(squared, 1)
            act.wait_ge(step, 1)
            nc.scalar.activation(rstd, rstd, ACT.Sqrt).then_inc(rooted, 1)
            act.wait_ge(params, 32)
            for b in range(NB):
                act.wait_ge(scaled, b + 1)
                nc.scalar.activation(av[:, b, :], av[:, b, :], ACT.Silu, scale=g[:, b:b + 1],
                                     bias=b_[:, b:b + 1]).then_inc(done, 1)

        @block.vector
        def _(dve):
            V = nc.vector
            dve.wait_ge(meaned, 1)
            for b in range(NB):
                V.scalar_tensor_tensor(out=av[:, b, :], in0=flat(0), scalar=-1.0 / CCH, in1=av[:, b, :],
                                       op0=ALU.mult, op1=ALU.add).then_inc(centred, 1)
            dve.wait_ge(spread, 1)
            V.tensor_scalar(rstd, flat(2), 1.0 / CCH, EPS, ALU.mult, ALU.add).then_inc(step, 1)
            dve.wait_ge(rooted, 1)
            V.reciprocal(rstd, rstd).then_inc(step, 1)
            dve.wait_ge(step, 2)
            dve.wait_ge(squared, NB)
            for b in range(NB):
                V.tensor_tensor(av[:, b, :], av[:, b, :], rstd, ALU.mult).then_inc(scaled, 1)


def phase_diff_attention(c, hT, w_in, q_g, k_g, lambdas, v, o, work, tmp):
    nc = c.nc
    hv = hT.rearrange("p (k s) -> p k s", k=KC)
    vv = v.rearrange("p (t n) -> p t n", t=TT)
    ov = o.rearrange("p (t n) -> p t n", t=TT)
    SCALE = float(DHD) ** -0.5
    take = lambda n: work[:, n * SEQ:(n + 1) * SEQ]
    q_of = [take(0), tmp[:, 2 * SEQ:3 * SEQ]]
    k_all = take(1)
    w = [take(2 + j).rearrange("p (k n) -> p k n", k=KC) for j in range(2)]
    prob = [take(4), take(5)]
    probT = [take(6), take(7)]
    sq, root = tmp[:, 0:SEQ], tmp[:, SEQ:2 * SEQ]
    sm = lambda a, n=2: c.small[:, 1400 + a:1400 + a + n]
    negmax, rowsum, rinv, gain, neglam = sm(0), sm(2), sm(4), sm(6), sm(8, 1)
    dots, halves_of = sm(10), c.small[:, 1160:1160 + P]
    lam_rows = tmp[:, 0:4 * DHD].rearrange("p (j n) -> p j n", j=4)
    lam_prod = tmp[:, SEQ:SEQ + 2 * DHD].rearrange("p (j n) -> p j n", j=2)
    GR = [(t, g) for t in range(TT) for g in range(t // 4 + 1)]
    NGR = len(GR)
    first = {t: n for n, (t, g) in reversed(list(enumerate(GR)))}
    flat = lambda b: c.ps[:, b:b + 2, :].rearrange("p b n -> p (b n)")
    with ExitStack() as ctx:
        S = lambda n: c.sem(ctx, "da_" + n)
        params, lam_step, filled = S("params"), S("lam_step"), S("filled")
        wload = [S("wload0"), S("wload1")]
        projected = S("projected")
        squared = S("squared")
        meaned = S("meaned")
        offset, rooted, inverted = S("offset"), S("rooted"), S("inverted")
        normed = S("normed")
        scored = S("scored")
        maxed, negated = S("maxed"), S("negated")
        exped = S("exped")
        weighed = S("weighed")
        combined = S("combined")
        turned, placed = S("turned"), S("placed")
        summed = S("summed")
        stored = S("stored")
        block = ctx.enter_context(nc.Block())

        @block.gpsimd
        def _(pool):
            nc.gpsimd.memset(halves_of, 0.0).then_inc(filled, 1)
            pool.wait_ge(filled, 1)
            for r in range(2):
                nc.gpsimd.memset(halves_of[r * DHD:(r + 1) * DHD, r * DHD:(r + 1) * DHD],
                                 1.0 / DHD).then_inc(filled, 1)
                nc.gpsimd.memset(q_of[r][(1 - r) * DHD:(2 - r) * DHD, :], 0.0).then_inc(filled, 1)

        @block.sync
        def _(sp):
            for j, l in enumerate(lambdas):
                sp.dma_start(lam_rows[:, j, :], bcast(l, DHD)).then_inc(params, 16)
            with nc.allow_non_contiguous_dma(reason="two gain vectors"):
                for j, g in enumerate((q_g, k_g)):
                    for r in range(2):
                        sp.dma_start(gain[r * DHD:(r + 1) * DHD, j:j + 1],
                                     g.rearrange("(p a) -> p a", a=1)).then_inc(params, 16)
            wv = cols(w_in)
            with sp.Fori(0, DH) as i:
                sp.wait_ge(normed, i * 4 + 4)
                sp.dma_start(w[0], wv[:, :, bass.ds(i * P + C2_Q, P)]).then_inc(wload[0], 16)
                sp.dma_start(w[1], wv[:, :, bass.ds(i * P + C2_K, P)]).then_inc(wload[1], 16)

        @block.tensor
        def _(pe):
            pe.sem_inc(summed, 2)
            pe.wait_ge(filled, 5)
            with pe.Fori(0, DH) as i:
                pe.wait_ge(stored, i * TT + 2)
                for j in range(2):
                    pe.wait_ge(wload[j], i * 16 + 16)
                    for k in range(KC):
                        for h in range(2):
                            mm = nc.tensor.matmul(c.ps[:, 2 * j + h, :], w[j][:, k, :],
                                                  hv[:, k, h * BANK:(h + 1) * BANK],
                                                  start=(k == 0), stop=(k == KC - 1))
                    mm.then_inc(projected, 1)
                for j in range(2):
                    pe.wait_ge(squared, i * 2 + (j + 1))
                    for h in range(2):
                        mm = nc.tensor.matmul(c.ps[:, 4 + 2 * j + h, :], halves_of,
                                              sq[:, h * BANK:(h + 1) * BANK], start=True, stop=True)
                    mm.then_inc(meaned, 1)
                pe.wait_ge(normed, i * 4 + 8)

                def score(t):
                    n = (t + 1) * P
                    for r in range(2):
                        pe.wait_ge(exped, i * (2 * TT) + (2 * t + r + 1))
                        for b in range((n + BANK - 1) // BANK):
                            width = min(BANK, n - b * BANK)
                            mm = nc.tensor.matmul(c.ps[:, 4 + 2 * r + b, 0:width],
                                                  q_of[r][:, t * P:(t + 1) * P],
                                                  k_all[:, b * BANK:b * BANK + width],
                                                  start=True, stop=False, skip_group_check=True)
                        nc.tensor.matmul(c.ps[:, 4 + 2 * r + b, width - P:width], c.identb[:],
                                         c.maskb[:], start=False, stop=True,
                                         skip_group_check=True).then_inc(scored, 1)

                def values(t):
                    pe.wait_ge(combined, i * TT + (t + 2))
                    for g in range(t // 4 + 1):
                        n = first[t] + g
                        pe.wait_ge(placed, i * NGR + (n + 1))
                        for b in range(min(4, t + 1 - 4 * g)):
                            mm = nc.tensor.transpose(c.ps[:, n % 2, b * P:(b + 1) * P],
                                                     prob[0][:, (4 * g + b) * P:(4 * g + b + 1) * P],
                                                     c.ident[:])
                        mm.then_inc(turned, 1)
                    pe.wait_ge(stored, i * TT + (t + 1))
                    pe.wait_ge(placed, i * NGR + (first[t] + t // 4 + 3))
                    for b in range(t + 1):
                        mm = nc.tensor.matmul(c.ps[:, 2 + t % 2, 0:DV],
                                              probT[t % 2][:, b * P:(b + 1) * P],
                                              vv[:, b, bass.ds(i * DV, DV)],
                                              start=(b == 0), stop=(b == t))
                    mm.then_inc(summed, 1)

                score(0)
                for t in range(TT):
                    if t + 1 < TT:
                        score(t + 1)
                    values(t)

        @block.scalar
        def _(act):
            act.wait_ge(lam_step, 2)
            nc.scalar.activation(dots, dots, ACT.Exp).then_inc(lam_step, 1)
            act.sem_inc(exped, 2)
            with act.Fori(0, DH) as i:
                for j in range(2):
                    act.wait_ge(projected, i * 2 + (j + 1))
                    if j:
                        act.wait_ge(meaned, i * 2 + 1)
                    nc.scalar.activation(sq, flat(2 * j), ACT.Square).then_inc(squared, 1)
                    act.wait_ge(offset, i * 2 + (j + 1))
                    nc.scalar.activation(root, root, ACT.Sqrt).then_inc(rooted, 1)
                for t in range(TT):
                    n = (t + 1) * P
                    for r in range(2):
                        act.wait_ge(negated, i * (2 * TT) + (2 * t + r + 1))
                        if r == 0 and t >= 1:
                            act.wait_ge(turned, i * NGR + (first[t - 1] + (t - 1) // 4 + 1))
                        act.wait_ge(combined, i * TT + (t + 1))
                        nc.scalar.activation(prob[r][:, 0:n], flat(4 + 2 * r)[:, 0:n], ACT.Exp,
                                             scale=SCALE, bias=negmax[:, r:r + 1],
                                             accum_out=rowsum[:, r:r + 1]).then_inc(exped, 1)

        @block.vector
        def _(dve):
            V = nc.vector
            dve.wait_ge(params, 16 * 8)
            V.tensor_tensor(lam_prod, lam_rows[:, 0:4:2, :], lam_rows[:, 1:4:2, :], ALU.mult)\
                .then_inc(lam_step, 1)
            dve.wait_ge(lam_step, 1)
            V.tensor_reduce(dots, lam_prod, AX.X, ALU.add).then_inc(lam_step, 1)
            dve.wait_ge(lam_step, 3)
            V.scalar_tensor_tensor(out=neglam, in0=dots[:, 1:2], scalar=-LAM_INIT, in1=dots[:, 0:1],
                                   op0=ALU.add, op1=ALU.subtract).then_inc(lam_step, 1)
            dve.wait_ge(lam_step, 4)
            dve.sem_inc(normed, 4)
            dve.sem_inc(combined, 1)
            dve.sem_inc(placed, 2)
            dve.sem_inc(stored, 2)
            with dve.Fori(0, DH) as i:
                for j in range(2):
                    dve.wait_ge(meaned, i * 2 + (j + 1))
                    V.tensor_scalar(root, flat(4 + 2 * j), 1.0, EPS, ALU.mult, ALU.add)\
                        .then_inc(offset, 1)
                    dve.wait_ge(rooted, i * 2 + (j + 1))
                    V.reciprocal(root, root).then_inc(inverted, 1)
                    dve.wait_ge(inverted, i * 2 + (j + 1))
                    for r in range(2):
                        rows = slice(r * DHD, (r + 1) * DHD)
                        V.scalar_tensor_tensor(out=(k_all if j else q_of[r])[rows, :],
                                               in0=c.ps[rows, 2 * j:2 * j + 2, :]
                                               .rearrange("p b n -> p (b n)"),
                                               scalar=gain[rows, j:j + 1], in1=root[rows, :],
                                               op0=ALU.mult, op1=ALU.mult).then_inc(normed, 1)
                    dve.wait_ge(normed, i * 4 + (2 * j + 6))

                def maxima(t):
                    n = (t + 1) * P
                    for r in range(2):
                        m = 2 * t + r
                        dve.wait_ge(scored, i * (2 * TT) + (m + 1))
                        dve.wait_ge(exped, i * (2 * TT) + (m + 1))
                        V.tensor_reduce(negmax[:, r:r + 1], flat(4 + 2 * r)[:, 0:n], AX.X, ALU.max)\
                            .then_inc(maxed, 1)
                        dve.wait_ge(maxed, i * (2 * TT) + (m + 1))
                        V.tensor_scalar(negmax[:, r:r + 1], negmax[:, r:r + 1], -SCALE, None,
                                        ALU.mult).then_inc(negated, 1)

                def combine(t):
                    n = (t + 1) * P
                    dve.wait_ge(exped, i * (2 * TT) + (2 * t + 4))
                    V.reciprocal(rinv, rowsum).then_inc(weighed, 1)
                    dve.wait_ge(weighed, i * (3 * TT) + (3 * t + 1))
                    V.tensor_tensor(rinv[:, 1:2], rinv[:, 1:2], neglam, ALU.mult).then_inc(weighed, 1)
                    V.tensor_scalar(prob[0][:, 0:n], prob[0][:, 0:n], rinv[:, 0:1], None, ALU.mult)\
                        .then_inc(weighed, 1)
                    dve.wait_ge(weighed, i * (3 * TT) + (3 * t + 3))
                    V.scalar_tensor_tensor(out=prob[0][:, 0:n], in0=prob[1][:, 0:n],
                                           scalar=rinv[:, 1:2], in1=prob[0][:, 0:n], op0=ALU.mult,
                                           op1=ALU.add).then_inc(combined, 1)

                def take_T(t):
                    for g in range(t // 4 + 1):
                        n = first[t] + g
                        dve.wait_ge(turned, i * NGR + (n + 1))
                        dve.wait_ge(summed, i * TT + (t + 1))
                        width = min(4, t + 1 - 4 * g) * P
                        V.tensor_copy(probT[t % 2][:, 4 * g * P:4 * g * P + width],
                                      c.ps[:, n % 2, 0:width]).then_inc(placed, 1)

                maxima(0)
                for t in range(TT):
                    combine(t)
                    if t + 1 < TT:
                        maxima(t + 1)
                    take_T(t)
                    dve.wait_ge(summed, i * TT + (t + 3))
                    V.tensor_copy(ov[:, t, bass.ds(i * DV, DV)], c.ps[:, 2 + t % 2, 0:DV])\
                        .then_inc(stored, 1)


def phase_router(c, hT, w_group, w_expert, b_group, b_expert, slot_dram, tmp):
    nc = c.nc
    hv = hT.rearrange("p (k s) -> p k s", k=KC)
    NL = NG + NE
    pos_ = [0]

    def take(n, parts=P):
        a = pos_[0]
        pos_[0] += n
        return tmp[0:parts, a:a + n]

    t3 = lambda ap, t=TT: ap.rearrange("p (t n) -> p t n", t=t)
    w = take(KC * NL).rearrange("p (k n) -> p k n", k=KC)
    bias = take(NL)
    grp = t3(take(TT * 8))
    exl = t3(take(TT * NE))
    top = t3(take(TT * 8))
    gtop = t3(take(TT * 8))
    gidx, eidx = t3(take(TT * 8)), t3(take(TT * 8))
    no, no_grp = take(NE), take(NE)
    sel = [t3(take(TT * NE)) for _ in range(2)]
    both, pos, dst_, one = (t3(take(TT * NE)) for _ in range(4))
    base = t3(take(TT * NE))
    count, over, blocks, upto, k2 = (take(NE) for _ in range(5))
    ones_e = take(NE)
    gexp = t3(take(TT * NG))
    gsum, e2, s2 = take(TT), take(TT), take(TT)
    dest_f = [take(TT) for _ in range(2)]
    cmp_ = take(EXTRA * NE).rearrange("p (b n) -> p b n", b=EXTRA)
    bno, bex, bcount = take(EXTRA), take(EXTRA), take(1)
    slot_f = take(P, SLOTS // P)
    bl = lambda ap, n: ap.unsqueeze(2).to_broadcast([P, ap.shape[1], n])
    bt = lambda ap, t=TT: ap.unsqueeze(1).to_broadcast([P, t, ap.shape[1]])
    with ExitStack() as ctx:
        S = lambda n: c.sem(ctx, "rt_" + n)
        loaded, numbered, logits, step = S("loaded"), S("numbered"), S("logits"), S("step")
        act_step, ranked, zeroed, scattered = S("act_step"), S("ranked"), S("zeroed"), S("scattered")
        read_back, turned = S("read_back"), S("turned")
        block = ctx.enter_context(nc.Block())

        @block.sync
        def _(sp):
            with nc.allow_non_contiguous_dma(reason="narrow router weights, once"):
                sp.dma_start(w[:, :, 0:NG], cols(w_group)).then_inc(loaded, 16)
                sp.dma_start(w[:, :, NG:NL], cols(w_expert)).then_inc(loaded, 16)
                sp.dma_start(bias[:, 0:NG], bcast(b_group, NG)).then_inc(loaded, 16)
                sp.dma_start(bias[:, NG:NL], bcast(b_expert, NE)).then_inc(loaded, 16)
            sp.wait_ge(numbered, 3)
            sp.dma_start(slot_dram.rearrange("(p b) a -> p (b a)", p=P), c.zeros_i)\
                .then_inc(zeroed, 16)
            sp.wait_ge(scattered, 16 * 2 * TT)
            sp.dma_start(c.slot_rows, slot_dram.rearrange("(b p) a -> b (p a)", p=P))\
                .then_inc(read_back, 16)

        @block.gpsimd
        def _(pool):
            pool.iota(c.expert_no, pattern=[[1, NE]], base=0, channel_multiplier=0)\
                .then_inc(numbered, 1)
            pool.iota(c.token_no, pattern=[[P, TT]], base=0, channel_multiplier=1)\
                .then_inc(numbered, 1)
            pool.memset(c.zeros_i, 0).then_inc(numbered, 1)
            pool.wait_ge(zeroed, 16)
            pool.wait_ge(numbered, 3)
            pool.wait_ge(step, DEST_DONE)
            for t in range(TT):
                for j in range(2):
                    if t or j:
                        pool.wait_ge(scattered, 16 * (2 * t + j))
                    pool.indirect_dma_start(
                        out=slot_dram, out_offset=bass.IndirectOffsetOnAxis(c.dest[j][:, t:t + 1], 0),
                        in_=c.token_no[:, t:t + 1], in_offset=None).then_inc(scattered, 16)
            pool.wait_ge(scattered, 16 * 2 * TT)

        @block.tensor
        def _(pe):
            pe.wait_ge(loaded, 64)
            for t in range(TT):
                for k in range(KC):
                    mm = nc.tensor.matmul(c.ps[:, 0, t * NL:(t + 1) * NL], hv[:, k, t * P:(t + 1) * P],
                                          w[:, k, :], start=(k == 0), stop=(k == KC - 1))
            mm.then_inc(logits, 1)
            pe.wait_ge(step, BOTH_DONE)
            flat = both.rearrange("p t n -> p (t n)")
            nc.tensor.matmul(c.ps[:, 1, 0:TT * NE], c.before[:], flat, start=True, stop=True)
            nc.tensor.matmul(c.ps[:, 2, 0:TT * NE], c.ones[:], flat, start=True, stop=True)\
                .then_inc(ranked, 1)
            pe.wait_ge(step, SLOTS_READ)
            nc.tensor.transpose(c.ps[:, 3, 0:SLOTS // P], slot_f, c.ident[0:SLOTS // P, 0:SLOTS // P])\
                .then_inc(turned, 1)

        @block.scalar
        def _(act):
            act.wait_ge(step, GEXP_ARG)
            nc.scalar.activation(gexp, gexp, ACT.Exp).then_inc(act_step, 1)
            act.wait_ge(step, E2_ARG)
            nc.scalar.activation(e2, e2, ACT.Exp).then_inc(act_step, 1)

        @block.vector
        def _(dve):
            V = nc.vector
            st = Steps(dve, step)
            W = st.then_wait
            tt = lambda o, a, b, op: W(V.tensor_tensor(o, a, b, op))
            ts = lambda o, a, x, y, op0, op1: W(V.tensor_scalar(o, a, x, y, op0, op1))
            dve.wait_ge(numbered, 3)
            W(V.tensor_copy(no, c.expert_no))
            W(V.memset(grp, NEG))
            W(V.memset(ones_e, 1.0))
            ts(no_grp, no, float(EPG), None, ALU.is_ge, ALU.bypass)
            for g in range(2, NG):
                W(V.scalar_tensor_tensor(out=no_grp, in0=no, scalar=float(EPG * g), in1=no_grp,
                                         op0=ALU.is_ge, op1=ALU.add))
            dve.wait_ge(logits, 1)
            ps = t3(c.ps[:, 0, 0:TT * NL])
            tt(grp[:, :, 0:NG], ps[:, :, 0:NG], bt(bias[:, 0:NG]), ALU.add)
            tt(exl, ps[:, :, NG:NL], bt(bias[:, NG:NL]), ALU.add)
            for t in range(TT):
                W(V.max(gtop[:, t, :], grp[:, t, :]))
                W(V.max_index(c.found[0][:, 8 * t:8 * t + 8].bitcast(U32), gtop[:, t, :], grp[:, t, :]))
            W(V.tensor_copy(gidx.rearrange("p t n -> p (t n)"), c.found[0]))
            tt(gexp, grp[:, :, 0:NG], gtop[:, :, 0:1].to_broadcast([P, TT, NG]), ALU.subtract)
            assert st.n == GEXP_ARG, st.n
            tt(one, bt(no_grp), gidx[:, :, 0:1].to_broadcast([P, TT, NE]), ALU.is_equal)
            ts(one, one, -NEG, NEG, ALU.mult, ALU.add)
            tt(exl, exl, one, ALU.add)
            for t in range(TT):
                W(V.max(top[:, t, :], exl[:, t, :]))
                W(V.max_index(c.found[1][:, 8 * t:8 * t + 8].bitcast(U32), top[:, t, :], exl[:, t, :]))
            W(V.tensor_copy(eidx.rearrange("p t n -> p (t n)"), c.found[1]))
            for j in range(2):
                tt(sel[j], bt(no), eidx[:, :, j:j + 1].to_broadcast([P, TT, NE]), ALU.is_equal)
            tt(both, sel[0], sel[1], ALU.add)
            assert st.n == BOTH_DONE, st.n
            tt(e2.unsqueeze(2), top[:, :, 1:2], top[:, :, 0:1], ALU.subtract)
            assert st.n == E2_ARG, st.n
            dve.wait_ge(act_step, 1)
            W(V.tensor_reduce(gsum, gexp, AX.X, ALU.add))
            dve.wait_ge(act_step, 2)
            ts(s2, e2, 1.0, None, ALU.add, ALU.bypass)
            tt(s2, s2, gsum, ALU.mult)
            W(V.reciprocal(c.weight[0], s2))
            tt(c.weight[1], c.weight[0], e2, ALU.mult)
            dve.wait_ge(ranked, 1)
            total = t3(c.ps[:, 2, 0:TT * NE])
            W(V.memset(base[:, 0, :], 0.0))
            for t in range(1, TT):
                tt(base[:, t, :], base[:, t - 1, :], total[:, t - 1, :], ALU.add)
            tt(count, base[:, TT - 1, :], total[:, TT - 1, :], ALU.add)
            tt(pos, t3(c.ps[:, 1, 0:TT * NE]), base, ALU.add)
            ts(blocks, count, float(P), None, ALU.is_gt, ALU.bypass)
            for n in range(2, SEQ // P):
                W(V.scalar_tensor_tensor(out=blocks, in0=count, scalar=float(P * n), in1=blocks,
                                         op0=ALU.is_gt, op1=ALU.add))
            W(V.tensor_tensor_scan(upto, ones_e, blocks, 0.0, ALU.mult, ALU.add))
            tt(k2, upto, blocks, ALU.subtract)
            tt(k2, k2, no, ALU.subtract)
            ts(k2, k2, float(P), float(P * (NE - 1)), ALU.mult, ALU.add)
            ts(one, pos, float(P), None, ALU.is_ge, ALU.bypass)
            tt(one, one, bt(k2), ALU.mult)
            tt(dst_, pos, one, ALU.add)
            W(V.scalar_tensor_tensor(out=dst_, in0=bt(no), scalar=float(P), in1=dst_, op0=ALU.mult,
                                     op1=ALU.add))
            for j in range(2):
                tt(sel[j], sel[j], dst_, ALU.mult)
                W(V.tensor_reduce(dest_f[j], sel[j], AX.X, ALU.add))
                W(V.tensor_copy(c.dest[j], dest_f[j]))
            assert st.n == DEST_DONE, st.n
            W(V.tensor_copy(bno, c.expert_no[:, 0:EXTRA]))
            tt(cmp_, bl(bno, NE), bt(upto, EXTRA), ALU.is_ge)
            W(V.tensor_reduce(bex, cmp_, AX.X, ALU.add))
            ts(bex, bex, float(NE - 1), None, ALU.min, ALU.bypass)
            W(V.tensor_copy(c.extra_expert, bex))
            W(V.tensor_copy(c.extra_count, upto[:, NE - 1:NE]))
            dve.wait_ge(read_back, 16)
            W(V.tensor_copy(slot_f, c.slot_rows))
            assert st.n == SLOTS_READ, st.n
            dve.wait_ge(turned, 1)
            W(V.tensor_copy(c.slot_token, c.ps[:, 3, 0:SLOTS // P]))


GEXP_ARG, BOTH_DONE, E2_ARG, DEST_DONE, SLOTS_READ = 26, 49, 50, 86, 93


def phase_experts(c, name, x_dram, y_dram, w_gate, w_up, w_down, extra):
    nc = c.nc
    ns = 1 if extra else 2
    steps = EXTRA if extra else NE // 2
    first = NE if extra else 0
    FC = DE // P
    W = KC * DE
    GATE, UP, DOWN = range(3)
    raw = [c.named(f"{name}_raw{m}", 0, m * W, W) for m in range(3)]
    part = [[p.rearrange("p (k n) -> p k n", k=(KC, KC, FC)[m])
             for p in c.rounded(f"{name}_w{m}", 0, (3 + 2 * m) * W, W)] for m in range(3)]
    at = 9 * W
    x = [c.at(0, at + s * D, D) for s in range(2)]
    at += 2 * D
    xT = [c.rounded(f"{name}_xT{s}", 0, at + 2 * s * D, D) for s in range(2)]
    at += 4 * D
    hid = [c.at(0, at + s * DE, DE) for s in range(2)]
    at += 2 * DE
    hidT = [c.rounded(f"{name}_hT{s}", 0, at + 2 * s * DE, DE) for s in range(2)]
    at += 4 * DE
    y = [c.at(0, at + s * D, D) for s in range(2)]
    assert at + 2 * D <= 6 * REGION
    flat = lambda b, n: c.ps[:, b:b + n, :].rearrange("p b n -> p (b n)")
    as_f32 = lambda r: r.bitcast(F32)
    with ExitStack() as ctx:
        S = lambda n: c.sem(ctx, f"{name}_{n}")
        loaded = [S(f"loaded{m}") for m in range(3)]
        high = [S(f"high{m}") for m in range(3)]
        low = [S(f"low{m}") for m in range(3)]
        used = [S(f"used{m}") for m in range(3)]
        gathered = [S("gathered0"), S("gathered1")]
        indexed, asked = S("indexed"), S("asked")
        x_turned = S("x_turned")
        x_high, x_low = S("x_high"), S("x_low")
        opened = S("opened")
        hidden = S("hidden")
        h_turned = S("h_turned")
        h_high, h_low = S("h_high"), S("h_low")
        half0, half1 = S("half0"), S("half1")
        stored = [S("stored0"), S("stored1")]
        written = S("written")
        block = ctx.enter_context(nc.Block())

        def run(eng, body):
            if extra:
                count = eng.value_load(c.extra_count[0:1, 0:1], min_val=0, max_val=EXTRA)
                with eng.Fori(0, steps) as i:
                    with eng.If(i < count):
                        body(i, 0)
            else:
                with eng.Fori(0, steps) as i:
                    for s in range(ns):
                        body(i, s)

        def overlapped(eng, ahead, rest):
            if extra:
                def body(i, s):
                    for part_of in ahead:
                        part_of(i, s)
                    rest(i, s, [lambda: None] * len(ahead))
                run(eng, body)
                return
            for part_of in ahead:
                part_of(0, 0)
            with eng.Fori(0, steps - 1) as i:
                rest(i, 0, [lambda f=f: f(i, 1) for f in ahead])
                rest(i, 1, [lambda f=f: f(i + 1, 0) for f in ahead])
            rest(steps - 1, 0, [lambda f=f: f(steps - 1, 1) for f in ahead])
            rest(steps - 1, 1, [lambda: None] * len(ahead))

        @block.sync
        def _(sp):
            def load(i, s):
                b = i * ns + s
                if extra:
                    e = sp.value_load(c.extra_expert[0:1, bass.ds(i, 1)], min_val=0, max_val=NE - 1)
                else:
                    e = b
                for m, w in enumerate((w_gate, w_up, w_down)):
                    sp.wait_ge(low[m], b + 1)
                    sp.dma_start(raw[m].rearrange("p (k n) -> p k n", k=(KC, KC, FC)[m]),
                                 w[bass.ds(e, 1)].rearrange("a (k p) n -> p (a k) n", p=P))\
                        .then_inc(loaded[m], 16)

            sp.sem_inc(stored[0], 16)
            sp.sem_inc(stored[1], 16)
            run(sp, load)

        @block.gpsimd
        def _(pool):
            def gather(i, s):
                b = i * ns + s
                pool.wait_ge(x_turned, b + 1)
                nc.gpsimd.tensor_copy(c.gather_at[s], c.slot_token[:, bass.ds(b + first, 1)])\
                    .then_inc(indexed, 1)
                pool.wait_ge(indexed, b + 1)
                pool.sem_inc(asked, 1)
                pool.indirect_dma_start(
                    out=x[s], out_offset=None, in_=x_dram,
                    in_offset=bass.IndirectOffsetOnAxis(c.gather_at[s], 0)).then_inc(gathered[s], 16)

            run(pool, gather)

        @block.tensor
        def _(pe):
            def three(out, a, b, k, kc):
                for n, (l, r) in enumerate(((a[0], b[0]), (a[0], b[1]), (a[1], b[0]))):
                    mm = nc.tensor.matmul(out, l, r, start=(k == 0 and n == 0),
                                          stop=(k == kc - 1 and n == 2))
                return mm

            def turn_x(i, s):
                b = i * ns + s
                pe.wait_ge(gathered[s], i * 16 + 16)
                pe.wait_ge(x_low, b + 1)
                for k in range(KC):
                    mm = nc.tensor.transpose(c.ps[:, k // 4, (k % 4) * P:(k % 4 + 1) * P],
                                             x[s][:, k * P:(k + 1) * P], c.ident[:])
                mm.then_inc(x_turned, 1)

            def product(i, s, m, bank_free):
                b = i * ns + s
                pe.wait_ge(x_low, b + 2)
                pe.wait_ge(low[m], b + 2)
                pe.wait_ge(bank_free, b + 1)
                for k in range(KC):
                    mm = three(c.ps[:, 2 + m, :], [p[:, k * P:(k + 1) * P] for p in xT[s]],
                               [p[:, k, :] for p in part[m]], k, KC)
                mm.then_inc(used[m], 1)

            def turn_h(i, s):
                b = i * ns + s
                pe.wait_ge(hidden, b + 2)
                pe.wait_ge(h_low, b + 1)
                for k in range(FC):
                    mm = nc.tensor.transpose(c.ps[:, 4, k * P:(k + 1) * P],
                                             hid[s][:, k * P:(k + 1) * P], c.ident[:])
                mm.then_inc(h_turned, 1)

            def down(i, s):
                b = i * ns + s
                pe.wait_ge(low[DOWN], b + 2)
                pe.wait_ge(h_low, b + 2)
                pe.wait_ge(half0, b + 1)
                pe.wait_ge(half1, b + 1)
                for h in range(2):
                    for k in range(FC):
                        mm = three(c.ps[:, 5 + h, :], [p[:, k * P:(k + 1) * P] for p in hidT[s]],
                                   [p[:, k, h * BANK:(h + 1) * BANK] for p in part[DOWN]], k, FC)
                mm.then_inc(used[DOWN], 1)

            def rest(i, s, ahead):
                product(i, s, GATE, opened)
                product(i, s, UP, hidden)
                ahead[0]()
                turn_h(i, s)
                down(i, s)

            for m in range(3):
                pe.sem_inc(used[m], 1)
            pe.sem_inc(x_turned, ns)
            overlapped(pe, [turn_x], rest)

        @block.scalar
        def _(act):
            def hi(m):
                def f(i, s):
                    b = i * ns + s
                    act.wait_ge(loaded[m], b * 16 + 16)
                    act.wait_ge(used[m], b + 1)
                    nc.scalar.activation(part[m][0].rearrange("p k n -> p (k n)"), raw[m],
                                         ACT.Identity).then_inc(high[m], 1)
                return f

            def hi_x(i, s):
                b = i * ns + s
                act.wait_ge(x_turned, b + (ns + 1))
                act.wait_ge(used[UP], b + 1)
                nc.scalar.activation(xT[s][0], flat(0, 2), ACT.Identity).then_inc(x_high, 1)

            def rest(i, s, ahead):
                b = i * ns + s
                act.wait_ge(used[GATE], b + 2)
                nc.scalar.activation(hid[s], c.ps[:, 2 + GATE, :], ACT.Silu).then_inc(opened, 1)
                ahead[0]()
                ahead[1]()
                act.wait_ge(h_turned, b + 1)
                nc.scalar.activation(hidT[s][0], c.ps[:, 4, :], ACT.Identity).then_inc(h_high, 1)
                ahead[2]()
                act.wait_ge(used[DOWN], b + 2)
                act.wait_ge(stored[s], i * 16 + 16)
                nc.scalar.activation(y[s][:, 0:BANK], c.ps[:, 5, :], ACT.Identity).then_inc(half0, 1)
                ahead[3]()
                act.wait_ge(half0, b + 2)
                act.wait_ge(half1, b + 2)
                act.dma_start(y_dram[bass.ds((b + first) * P, P), :], y[s]).then_inc(stored[s], 16)
                if extra:
                    act.wait_ge(stored[s], i * 16 + 32)
                    act.sem_inc(written, 1)

            act.sem_inc(opened, 1)
            act.sem_inc(half0, 1)
            overlapped(act, [hi(GATE), hi_x, hi(UP), hi(DOWN)], rest)
            if not extra:
                for s in range(ns):
                    act.wait_ge(stored[s], 16 * steps + 16)

        @block.vector
        def _(dve):
            V = nc.vector

            def lo(m):
                def f(i, s):
                    b = i * ns + s
                    dve.wait_ge(high[m], b + 1)
                    V.tensor_tensor(part[m][1].rearrange("p k n -> p (k n)"), raw[m],
                                    as_f32(part[m][0]).rearrange("p k n -> p (k n)"),
                                    ALU.subtract).then_inc(low[m], 1)
                return f

            def lo_x(i, s):
                b = i * ns + s
                dve.wait_ge(x_high, b + 1)
                V.tensor_tensor(xT[s][1], flat(0, 2), as_f32(xT[s][0]), ALU.subtract)\
                    .then_inc(x_low, 1)

            def rest(i, s, ahead):
                b = i * ns + s
                dve.wait_ge(opened, b + 2)
                dve.wait_ge(used[UP], b + 2)
                V.tensor_tensor(hid[s], hid[s], c.ps[:, 2 + UP, :], ALU.mult).then_inc(hidden, 1)
                ahead[0]()
                dve.wait_ge(h_high, b + 1)
                V.tensor_tensor(hidT[s][1], c.ps[:, 4, :], as_f32(hidT[s][0]), ALU.subtract)\
                    .then_inc(h_low, 1)
                ahead[1]()
                ahead[2]()
                dve.wait_ge(used[DOWN], b + 2)
                dve.wait_ge(stored[s], i * 16 + 16)
                V.tensor_copy(y[s][:, BANK:D], c.ps[:, 6, :]).then_inc(half1, 1)
                ahead[3]()

            for m in range(3):
                dve.sem_inc(low[m], 1)
            dve.sem_inc(x_low, 1)
            dve.sem_inc(hidden, 1)
            dve.sem_inc(h_low, 1)
            dve.sem_inc(half1, 1)
            overlapped(dve, [lo_x, lo(GATE), lo(UP), lo(DOWN)], rest)


def phase_combine(c, x2_dram, x2, y_dram, out_dram, tmp):
    nc = c.nc
    xv = x2.rearrange("p (t d) -> p t d", t=TT)
    rows = out_dram.rearrange("(t p) d -> p t d", p=P)
    NB = 8
    buf = [tmp[:, s * D:(s + 1) * D] for s in range(NB)]
    with ExitStack() as ctx:
        got = [c.sem(ctx, f"cb_got{s}") for s in range(NB)]
        back = [c.sem(ctx, f"cb_back{t}") for t in range(TT)]
        added, stored = c.sem(ctx, "cb_added"), c.sem(ctx, "cb_stored")
        block = ctx.enter_context(nc.Block())

        @block.gpsimd
        def _(pool):
            for n in range(2 * TT):
                t, j = divmod(n, 2)
                if n >= NB:
                    pool.wait_ge(added, n - NB + 1)
                pool.indirect_dma_start(
                    out=buf[n % NB], out_offset=None, in_=y_dram,
                    in_offset=bass.IndirectOffsetOnAxis(c.dest[j][:, t:t + 1], 0))\
                    .then_inc(got[n % NB], 16)

        @block.vector
        def _(dve):
            for n in range(2 * TT):
                t, j = divmod(n, 2)
                dve.wait_ge(got[n % NB], 16 * (n // NB + 1))
                if j:
                    dve.wait_ge(added, n)
                else:
                    dve.wait_ge(back[t], 16)
                nc.vector.scalar_tensor_tensor(out=xv[:, t, :], in0=buf[n % NB],
                                               scalar=c.weight[j][:, t:t + 1], in1=xv[:, t, :],
                                               op0=ALU.mult, op1=ALU.add).then_inc(added, 1)

        @block.sync
        def _(sp):
            kept = x2_dram.rearrange("(t p) d -> p t d", p=P)
            for t in range(TT):
                sp.dma_start(xv[:, t, :], kept[:, t, :]).then_inc(back[t], 16)
            for t in range(TT):
                sp.wait_ge(added, 2 * t + 2)
                sp.dma_start(rows[:, t, :], xv[:, t, :]).then_inc(stored, 16)
            sp.wait_ge(stored, 16 * TT)


def _build(nc, a, out, upto=99):
    with ExitStack() as ctx:
        c = Chip(nc, ctx)
        R = lambda r: c.at(r, 0, REGION)
        ys = nc.dram_tensor("expert_out", (SLOTS, D), F32).ap()
        zeroed = c.sem(ctx, "zeroed")
        phase_constants(c, c.at(5, 0, D), ys[NE * P:SLOTS, :], zeroed)
        phase_norm_T(c, "pre", R(1), R(0), R(2), a["pre_norm_g"][0], src_dram=a["x"][0],
                     also=(zeroed, 16 * EXTRA))
        phase_xbc(c, R(0), a["w_in"][0], a["conv_w"][0], a["conv_b"][0], c.at(1, 0, 2 * REGION), R(3),
                  R(4), R(5))
        fcum = nc.dram_tensor("forget_sums", (HEADS, SEQ), F32).ap()
        phase_decays(c, R(0), a["w_in"][0], a["dt_bias"][0], a["a_log"][0], a["d_skip"][0],
                     a["fgate_b"][0], fcum, R(5))
        if upto < 2:
            return c
        phase_ssd(c, c.at(1, 0, 2 * REGION), R(3), R(4), R(5))
        if upto < 3:
            return c
        T = lambda r, k=KC: r.rearrange("p (k s) -> p k s", k=k)
        half = lambda r, n: r.rearrange("p (t d) -> p t d", t=TT)[:, :, n * BANK:(n + 1) * BANK]
        wcol = lambda w, a0, n: cols(w)[:, :, a0 + n * BANK:a0 + (n + 1) * BANK]
        ws = [c.at(5, 0, REGION // 2), c.at(5, REGION // 2, REGION // 2)]
        w_in = a["w_in"][0]
        phase_dense(c, "z", [(T(R(0)), wcol(w_in, C_Z, n), "act", half(R(2), n), ACT.Silu)
                             for n in range(2)], 5)
        phase_turn(c, "y", R(4), R(1), gate=R(2), groups=GROUPS, gain_dram=a["ssm_norm_g"][0])
        if upto < 4:
            return c
        phase_dense(c, "bs", [(T(R(0)), wcol(w_in, C_GS, n), "act", half(R(4), n), ACT.Sigmoid)
                              for n in range(2)]
                    + [(T(R(1)), wcol(a["w_branch_ssm"][0], 0, n), "mul", half(R(2), n), half(R(4), n))
                       for n in range(2)]
                    + [(T(R(0)), wcol(w_in, C_V, n), "act", half(R(3), n), ACT.Identity)
                       for n in range(2)], 5)
        phase_forget_attention(c, R(0), w_in, fcum, R(3), R(4), c.at(1, 0, 4 * SEQ),
                               c.at(1, 4 * SEQ, 3 * D), c.at(5, 0, 5 * SEQ), c.at(5, 5 * SEQ, SEQ))
        if upto < 5:
            return c
        phase_dense(c, "ba", [(T(R(0)), wcol(w_in, C_GA, n), "act", half(R(3), n), ACT.Sigmoid)
                              for n in range(2)]
                    + [(T(R(4)), wcol(a["w_branch_att"][0], 0, n), "muladd", half(R(2), n),
                        half(R(3), n)) for n in range(2)], 5)
        phase_turn(c, "mg", R(2), R(1))
        phase_dense(c, "wo", [(T(R(1)), wcol(a["w_out"][0], 0, n), "act", half(R(3), n), ACT.Identity)
                              for n in range(2)], 5)
        phase_post(c, a["x"][0], a["post_norm_g"][0], R(3), R(4), R(2))
        if upto < 6:
            return c
        phase_norm_T(c, "n2", R(4), R(0), R(1), a["attn_norm_g_2"][0])
        w_in = a["w_in_2"][0]
        h2 = T(R(0))
        v2 = c.at(2, 4096, 4096)
        v2h = v2.rearrange("p (t d) -> p t d", t=TT)
        conv = c.at(2, 0, 4096)
        phase_conformer(c, R(0), w_in, (a["conv_dw_w_2"][0], a["conv_dw_b_2"][0]),
                        [(h2, wcol(w_in, C2_V, 0), "act", v2h, ACT.Identity)]
                        + [(h2, wcol(w_in, C2_G, n), "act", half(R(3), n), ACT.Sigmoid)
                           for n in range(2)],
                        c.at(1, 0, 4 * (SEQ + CW - 1)), conv, c.at(1, 4224, SEQ),
                        c.at(1, 5248, 2 * D), ws, c.at(5, REGION // 2, CCH))
        phase_channel_norm(c, conv, c.at(1, 0, 4096), c.at(1, 4096, SEQ), a["conv_ln_g_2"][0],
                           a["conv_ln_b_2"][0])
        if upto < 7:
            return c
        o2 = c.at(1, 0, 4096)
        phase_diff_attention(c, R(0), w_in, a["q_norm_g_2"][0], a["k_norm_g_2"][0],
                             [a[f"lambda_{n}_2"][0] for n in ("q1", "k1", "q2", "k2")], v2, o2, R(5),
                             c.at(1, 4096, 3 * SEQ))
        phase_turn(c, "o2", o2, v2, groups=DH, gain_dram=a["subln_g_2"][0], gain_times=1.0 - LAM_INIT,
                   width=DH * DV)
        if upto < 8:
            return c
        phase_dense(c, "b2", [(h2, wcol(w_in, C2_G, 2 + n), "act", half(R(1), n), ACT.Sigmoid)
                              for n in range(2)]
                    + [(T(conv, 4), wcol(a["w_conv_out_2"][0], 0, n), "mul", half(R(3), n),
                        half(R(3), n)) for n in range(2)]
                    + [(T(v2, 4), wcol(a["w_attn_out_2"][0], 0, n), "muladd", half(R(3), n),
                        half(R(1), n)) for n in range(2)], 5)
        phase_turn(c, "m2", R(3), R(1))
        phase_dense(c, "wo2", [(T(R(1)), wcol(a["w_out_2"][0], 0, n), "add", half(R(4), n), None)
                               for n in range(2)], 5)
        if upto < 9:
            return c
        xn = nc.dram_tensor("expert_in", (SEQ, D), F32).ap()
        slot_dram = nc.dram_tensor("slot_tokens", (SLOTS, 1), I32).ap()
        x2_dram = nc.dram_tensor("x2_kept", (SEQ, D), F32).ap()
        phase_norm_T(c, "n3", R(4), R(0), R(1), a["ffn_norm_g_2"][0], xn_dram=xn,
                     row_gain=c.at(5, 0, D), keep_dram=x2_dram)
        phase_router(c, R(0), a["w_router_group_2"][0], a["w_router_expert_2"][0],
                     a["b_router_group_2"][0], a["b_router_expert_2"][0], slot_dram, R(2))
        if upto < 10:
            return c
        for extra in (False, True):
            phase_experts(c, "xe" if extra else "ex", xn, ys, a["w_gate_e_2"][0], a["w_up_e_2"][0],
                          a["w_down_e_2"][0], extra)
        phase_combine(c, x2_dram, R(4), ys, out[0], R(1))
        return c


_INS = ['x', 'pre_norm_g', 'w_in', 'conv_w', 'conv_b', 'dt_bias', 'a_log', 'd_skip', 'ssm_norm_g',
        'fgate_b', 'w_branch_ssm', 'w_branch_att', 'w_out', 'post_norm_g', 'attn_norm_g_2',
        'w_in_2', 'conv_dw_w_2', 'conv_dw_b_2', 'conv_ln_g_2', 'conv_ln_b_2', 'w_conv_out_2',
        'q_norm_g_2', 'k_norm_g_2', 'lambda_q1_2', 'lambda_k1_2', 'lambda_q2_2', 'lambda_k2_2',
        'subln_g_2', 'w_attn_out_2', 'w_out_2', 'ffn_norm_g_2', 'w_router_group_2',
        'b_router_group_2', 'w_router_expert_2', 'b_router_expert_2', 'w_gate_e_2', 'w_up_e_2',
        'w_down_e_2']


def kernel(**inputs):
    import numpy as _np
    import concourse.bacc as _bacc
    from concourse import mybir as _mybir
    from concourse.bass_utils import run_bass_kernel_spmd as _run

    nc = _bacc.Bacc("TRN2", target_bir_lowering=False, num_devices=1)
    arrays, args = {}, {}
    for name in _INS:
        v = _np.ascontiguousarray(inputs[name])
        arrays[f"in_{name}"] = v
        args[name] = nc.dram_tensor(f"in_{name}", v.shape, _mybir.dt.from_np(v.dtype),
                                    kind="ExternalInput").ap()
    out = nc.dram_tensor("out_0", (1, SEQ, D), _mybir.dt.float32, kind="ExternalOutput").ap()
    _build(nc, args, out)
    r = _run(nc, [arrays], core_ids=[0])
    return r.results[0]["out_0"]
```

```python
from contextlib import ExitStack

import concourse.bass as bass
from concourse import mybir

F32 = mybir.dt.float32
F32R = mybir.dt.float32r
BF16 = mybir.dt.bfloat16
I32 = mybir.dt.int32
U32 = mybir.dt.uint32
ACT = mybir.ActivationFunctionType
ALU = mybir.AluOpType
AX = mybir.AxisListType

P = 128
SEQ = 1024
D = 1024
TT = SEQ // P
KC = D // P
BANK = 512
EPS = 1e-6

HEADS, HD = 16, 64
GROUPS, STATE, CONV = 4, 128, 4
HPG = HEADS // GROUPS
XBC = D + 2 * GROUPS * STATE
C_Z, C_XBC = 0, D
C_DT = C_XBC + XBC
C_Q = C_DT + HEADS
C_K, C_V = C_Q + D, C_Q + 2 * D
C_F = C_Q + 3 * D
C_ZA = C_F + HEADS
C_GS, C_GA = C_ZA + D, C_ZA + 2 * D

CCH, CW = D // 2, 31
DH, DHD = 4, 64
DV = 2 * DHD
C2_Q = 2 * CCH
C2_K = C2_Q + DH * DV
C2_V = C2_K + DH * DV
C2_G = C2_V + DH * DV
LAM_INIT = 0.8 - 0.6
NG, EPG = 4, 8
NE = NG * EPG
DE = D // 2
ASSIGN = 2 * SEQ
EXTRA = ASSIGN // P
SLOTS = (NE + EXTRA) * P

NEG = -1e30
REGION = 8192


class Steps:

    def __init__(self, eng, sem, base=0):
        self.eng, self.sem, self.base, self.n = eng, sem, base, 0

    def done(self, ins):
        ins.then_inc(self.sem, 1)
        self.n += 1
        return self.n

    def then_wait(self, ins):
        self.done(ins)
        self.eng.wait_ge(self.sem, self.base + self.n)


class Chip:

    def __init__(self, nc, ctx):
        self.nc, self.ctx = nc, ctx
        sb = lambda name, shape, dt=F32: ctx.enter_context(nc.sbuf_tensor(name, shape, dt))
        self.arena = sb("arena", [P, 6 * REGION])
        self.arena_at = nc.sbuf_base - 4 * 6 * REGION
        self.ps = ctx.enter_context(nc.psum_tensor("ps", [P, 8, BANK], F32))
        self.ident = sb("ident", [P, P])
        self.ones = sb("ones", [P, P])
        self.upto = sb("upto", [P, P])
        self.before = sb("before", [P, P])
        self.identb = sb("identb", [P, P], BF16)
        self.maskb = sb("maskb", [P, P], BF16)
        self.maskTb = sb("maskTb", [P, 4, P], BF16)
        self.small = sb("small", [P, 1600])
        ints = sb("ints", [P, 512], I32)
        self.dest = [ints[:, 8 * j:8 * j + 8] for j in range(2)]
        self.slot_token = ints[:, 16:16 + SLOTS // P]
        self.gather_at = [ints[:, 64 + j:65 + j] for j in range(2)]
        self.found = [ints[:, 66 + 64 * j:130 + 64 * j] for j in range(2)]
        self.expert_no = ints[:, 194:194 + NE]
        self.token_no = ints[:, 226:226 + TT]
        self.extra_expert = ints[:, 234:234 + EXTRA]
        self.extra_count = ints[:, 250:251]
        self.taps = self.small[:, 1024:1024 + XBC // P * CONV].rearrange("p (b j) -> p b j", j=CONV)
        self.tap_bias = self.small[:, 1092:1092 + XBC // P]
        self.taps2 = self.small[:, 1024:1024 + CCH // P * CW].rearrange("p (b j) -> p b j", j=CW)
        self.tap_bias2 = self.small[:, 1150:1150 + CCH // P]
        self.weight = [self.small[:, 1408 + 32 + 8 * j:1408 + 40 + 8 * j] for j in range(2)]

    def at(self, region, offset, size):
        a = region * REGION + offset
        return self.arena[:, a:a + size]

    def named(self, name, region, offset, size, dtype=F32, parts=1):
        t = self.nc.alloc_sbuf_tensor_at(name, [P, parts, size], dtype,
                                         offset=self.arena_at + 4 * (region * REGION + offset))
        return t[:, 0, :] if parts == 1 else [t[:, n, :] for n in range(parts)]

    def rounded(self, name, region, offset, size):
        return self.named(name, region, offset, size, F32R, 2)

    def sem(self, ctx, name):
        s = ctx.enter_context(self.nc.semaphore(name))
        ctx.callback(lambda: self.nc.gpsimd.sem_clear(s))
        return s


def cols(ap):
    return ap.rearrange("(k p) n -> p k n", p=P)


def phase_constants(c, zero):
    nc = c.nc
    with ExitStack() as ctx:
        filled, shaped = c.sem(ctx, "const_filled"), c.sem(ctx, "const_shaped")
        block = ctx.enter_context(nc.Block())

        @block.vector
        def _(dve):
            nc.vector.memset(zero, 0.0)

        @block.gpsimd
        def _(pool):
            for m, v in ((c.ident, 0.0), (c.ones, 1.0), (c.upto, 1.0), (c.before, 1.0),
                         (c.identb, 0.0), (c.maskb, 0.0), (c.maskTb, 0.0)):
                pool.memset(m[:], v).then_inc(filled, 1)
            pool.wait_ge(filled, 7)
            one = [[-1, P]]
            up = [[1, P]]
            for m in (c.ident, c.identb):
                pool.affine_select(out=m[:], in_=m[:], compare_op=ALU.not_equal, fill=1.0, base=0,
                                   pattern=one, channel_multiplier=1).then_inc(shaped, 1)
            pool.affine_select(out=c.upto[:], in_=c.upto[:], compare_op=ALU.is_ge, fill=0.0, base=0,
                               pattern=up, channel_multiplier=-1).then_inc(shaped, 1)
            pool.affine_select(out=c.before[:], in_=c.before[:], compare_op=ALU.is_gt, fill=0.0,
                               base=0, pattern=up, channel_multiplier=-1).then_inc(shaped, 1)
            pool.affine_select(out=c.maskb[:], in_=c.maskb[:], compare_op=ALU.is_ge, fill=NEG,
                               base=0, pattern=one, channel_multiplier=1).then_inc(shaped, 1)
            pool.affine_select(out=c.maskTb[:], in_=c.maskTb[:], compare_op=ALU.is_ge, fill=NEG,
                               base=0, pattern=[[0, 4], [1, P]], channel_multiplier=-1)\
                .then_inc(shaped, 1)
            pool.wait_ge(shaped, 6)


def phase_norm_T(c, name, src, dst, xn, gain_dram, src_dram=None, xn_dram=None, background=None,
                 row_gain=None, keep_dram=None):
    nc = c.nc
    NG2 = TT // 2
    two = lambda ap, g: ap[:, 2 * g:2 * g + 2]
    with ExitStack() as ctx:
        loaded = [c.sem(ctx, f"{name}_loaded{t}") for t in range(2)]
        squared, rooted = c.sem(ctx, f"{name}_squared"), c.sem(ctx, f"{name}_rooted")
        meaned, inverted = c.sem(ctx, f"{name}_meaned"), c.sem(ctx, f"{name}_inverted")
        ready = c.sem(ctx, f"{name}_ready")
        turned, placed = c.sem(ctx, f"{name}_turned"), c.sem(ctx, f"{name}_placed")
        stored, kept = c.sem(ctx, f"{name}_stored"), c.sem(ctx, f"{name}_kept")
        ss, rstd, gain = c.small[:, 0:8], c.small[:, 8:16], c.small[:, 16:24]
        block = ctx.enter_context(nc.Block())
        srcv = src.rearrange("p (t d) -> p t d", t=TT)
        xnv = xn.rearrange("p (t d) -> p t d", t=TT)
        dstv = dst.rearrange("p (k s) -> p k s", k=KC)

        @block.sync
        def _(sp):
            if row_gain is None:
                with nc.allow_non_contiguous_dma(reason="a gain vector by chunks"):
                    sp.dma_start(gain, gain_dram.rearrange("(k p) -> p k", p=P))\
                        .then_inc(loaded[0], 16)
            else:
                sp.dma_start(row_gain, bcast(gain_dram, D)).then_inc(loaded[0], 16)
                sp.dma_start(keep_dram.rearrange("(t p) d -> p t d", p=P), srcv).then_inc(kept, 16)
            if src_dram is not None:
                rows = src_dram.rearrange("(t p) d -> p t d", p=P)
                for t in range(2):
                    sp.dma_start(srcv[:, 4 * t:4 * t + 4, :], rows[:, 4 * t:4 * t + 4, :])\
                        .then_inc(loaded[t], 16)
            if xn_dram is not None:
                rows = xn_dram.rearrange("(t p) d -> p t d", p=P)
                for t in range(TT):
                    sp.wait_ge(ready, t + 1)
                    sp.dma_start(rows[:, t, :], xnv[:, t, :]).then_inc(stored, 16)
                sp.wait_ge(stored, 16 * TT)
                sp.wait_ge(kept, 16)
            if background is not None:
                background(sp)

        @block.scalar
        def _(act):
            for g in range(NG2 + 1):
                for t in range(2 * g, 2 * g + 2) if g < NG2 else ():
                    if src_dram is not None and t % 4 == 0:
                        act.wait_ge(loaded[t // 4], 32 if t == 0 else 16)
                    nc.scalar.activation(xnv[:, t, :], srcv[:, t, :], ACT.Square,
                                         accum_out=ss[:, t:t + 1]).then_inc(squared, 1)
                if g:
                    act.wait_ge(meaned, g)
                    nc.scalar.activation(two(rstd, g - 1), two(rstd, g - 1), ACT.Sqrt)\
                        .then_inc(rooted, 1)

        @block.vector
        def _(dve):
            def place(t):
                for h in range(2):
                    n = 2 * t + h
                    dve.wait_ge(turned, n + 1)
                    out = dstv[:, 4 * h:4 * h + 4, t * P:(t + 1) * P]
                    ps = c.ps[:, n % 8, :].rearrange("p (k s) -> p k s", k=4)
                    if row_gain is None:
                        x = nc.vector.tensor_tensor(
                            out, ps, gain[:, 4 * h:4 * h + 4].unsqueeze(2).to_broadcast([P, 4, P]),
                            ALU.mult)
                    else:
                        x = nc.vector.tensor_copy(out, ps)
                    x.then_inc(placed, 1)

            dve.wait_ge(loaded[0], 16 if src_dram is None else 32)
            for g in range(NG2):
                dve.wait_ge(squared, 2 * g + 2)
                nc.vector.tensor_scalar(two(rstd, g), two(ss, g), 1.0 / D, EPS, ALU.mult, ALU.add)\
                    .then_inc(meaned, 1)
                if g:
                    place(2 * g - 2)
                dve.wait_ge(rooted, g + 1)
                nc.vector.reciprocal(two(rstd, g), two(rstd, g)).then_inc(inverted, 1)
                dve.wait_ge(inverted, g + 1)
                for t in (2 * g, 2 * g + 1):
                    if row_gain is None:
                        x = nc.vector.tensor_scalar(xnv[:, t, :], srcv[:, t, :], rstd[:, t:t + 1],
                                                    None, ALU.mult)
                    else:
                        x = nc.vector.scalar_tensor_tensor(out=xnv[:, t, :], in0=srcv[:, t, :],
                                                           scalar=rstd[:, t:t + 1], in1=row_gain,
                                                           op0=ALU.mult, op1=ALU.mult)
                    x.then_inc(ready, 1)
                if g:
                    place(2 * g - 1)
            place(TT - 2)
            place(TT - 1)

        @block.tensor
        def _(pe):
            for n in range(2 * TT):
                t, h = divmod(n, 2)
                pe.wait_ge(ready, t + 1)
                if n >= 8:
                    pe.wait_ge(placed, n - 7)
                for k in range(4):
                    kk = 4 * h + k
                    mm = nc.tensor.transpose(c.ps[:, n % 8, k * P:(k + 1) * P],
                                             xnv[:, t, kk * P:(kk + 1) * P], c.ident[:])
                mm.then_inc(turned, 1)


def phase_xbc_turn(c, acc, tok):
    nc = c.nc
    NB = XBC // P
    tokv = tok.rearrange("p (t n) -> p t n", t=TT)
    av = acc.rearrange("p (b s) -> p b s", b=NB)
    with ExitStack() as ctx:
        silued, turned = c.sem(ctx, "xt_silued"), c.sem(ctx, "xt_turned")
        placed = c.sem(ctx, "xt_placed")
        block = ctx.enter_context(nc.Block())

        @block.scalar
        def _(act):
            for b in range(NB):
                nc.scalar.activation(av[:, b, :], av[:, b, :], ACT.Silu).then_inc(silued, 1)

        @block.tensor
        def _(pe):
            for b in range(NB):
                pe.wait_ge(silued, b + 1)
                if b >= 4:
                    pe.wait_ge(placed, b - 3)
                for t in range(TT):
                    mm = nc.tensor.transpose(
                        c.ps[:, 2 * (b % 4) + t // 4, (t % 4) * P:(t % 4 + 1) * P],
                        av[:, b, t * P:(t + 1) * P], c.ident[:])
                mm.then_inc(turned, 1)

        @block.vector
        def _(dve):
            for b in range(NB):
                dve.wait_ge(turned, b + 1)
                nc.vector.tensor_copy(tokv[:, :, b * P:(b + 1) * P],
                                      c.ps[:, 2 * (b % 4):2 * (b % 4) + 2, :]
                                      .rearrange("p b (t n) -> p (b t) n", t=4)).then_inc(placed, 1)


def bcast(row, n):
    return row.rearrange("(a n) -> a n", a=1).to_broadcast([P, n])


class Decays:

    def __init__(self, c):
        take = lambda n: c.small[:, P * (n + 1):P * (n + 2)]
        self.dt, self.ncs, self.ecs, self.dte, self.cdec, self.dta = (take(n) for n in range(6))
        self.skip = c.small[:, 7 * P:7 * P + HEADS]


def phase_decays(c, hT, w_in, dt_bias, a_log, d_skip, fgate_b, fcum_dram, tmp):
    nc = c.nc
    n2 = 2 * HEADS
    W = TT * n2
    d = Decays(c)
    hv = hT.rearrange("p (k s) -> p k s", k=KC)
    w = tmp[:, 0:KC * n2].rearrange("p (k n) -> p k n", k=KC)
    wide = lambda j: tmp[:, 256 + j * W:256 + (j + 1) * W]
    v3 = lambda ap: ap.rearrange("p (t n) -> p t n", t=TT)
    x, ax, e, u1, ln, eq, res = (wide(j) for j in range(7))
    bias = tmp[:, 2048:2048 + n2]
    a_neg = tmp[:, 2080:2080 + HEADS]
    run = tmp[0:HEADS, 4096:4096 + SEQ]
    one_row = tmp[0:HEADS, 5120:5120 + SEQ]
    fT = tmp[0:HEADS, 6144:6144 + SEQ]
    heads = lambda t, lo: v3(t)[:, :, lo:lo + HEADS]
    with ExitStack() as ctx:
        loaded, logits = c.sem(ctx, "dec_loaded"), c.sem(ctx, "dec_logits")
        step, act_step = c.sem(ctx, "dec_step"), c.sem(ctx, "dec_act")
        summed, turned = c.sem(ctx, "dec_summed"), c.sem(ctx, "dec_turned")
        stored = c.sem(ctx, "dec_stored")
        block = ctx.enter_context(nc.Block())

        @block.sync
        def _(sp):
            wv = cols(w_in)
            with nc.allow_non_contiguous_dma(reason="narrow columns and broadcasts, once"):
                sp.dma_start(w[:, :, 0:HEADS], wv[:, :, C_DT:C_DT + HEADS]).then_inc(loaded, 16)
                sp.dma_start(w[:, :, HEADS:n2], wv[:, :, C_F:C_F + HEADS]).then_inc(loaded, 16)
                sp.dma_start(bias[:, 0:HEADS], bcast(dt_bias, HEADS)).then_inc(loaded, 16)
                sp.dma_start(bias[:, HEADS:n2], bcast(fgate_b, HEADS)).then_inc(loaded, 16)
                sp.dma_start(a_neg, bcast(a_log, HEADS)).then_inc(loaded, 16)
                sp.dma_start(d.skip, bcast(d_skip, HEADS)).then_inc(loaded, 16)
            sp.wait_ge(step, RUN_DONE)
            sp.dma_start(fcum_dram, run).then_inc(stored, 16)
            sp.wait_ge(stored, 16)

        @block.tensor
        def _(pe):
            pe.wait_ge(loaded, 96)
            for t in range(TT):
                for k in range(KC):
                    mm = nc.tensor.matmul(c.ps[:, 0, t * n2:(t + 1) * n2], hv[:, k, t * P:(t + 1) * P],
                                          w[:, k, :], start=(k == 0), stop=(k == KC - 1))
            mm.then_inc(logits, 1)
            pe.wait_ge(step, DTA_DONE)
            nc.tensor.matmul(c.ps[:, 1, 0:P], c.upto[:], d.dta, start=True, stop=True)
            nc.tensor.matmul(c.ps[:, 2, 0:P], c.ones[:], d.dta, start=True, stop=True)\
                .then_inc(summed, 1)
            for t in range(TT):
                mm = nc.tensor.transpose(c.ps[0:HEADS, 3 + t // 4, (t % 4) * P:(t % 4 + 1) * P],
                                         heads(res, HEADS)[:, t, :], c.ident[:])
            mm.then_inc(turned, 1)

        @block.scalar
        def _(act):
            act.wait_ge(loaded, 96)
            nc.scalar.activation(a_neg, a_neg, ACT.Exp).then_inc(act_step, 1)
            act.wait_ge(step, 3)
            nc.scalar.activation(e, ax, ACT.Exp, scale=-1.0).then_inc(act_step, 1)
            act.wait_ge(step, 4)
            nc.scalar.activation(ln, u1, ACT.Ln).then_inc(act_step, 1)
            act.wait_ge(step, DECAY_ARGS)
            nc.scalar.activation(d.ecs, d.ncs, ACT.Exp, scale=-1.0).then_inc(act_step, 1)
            nc.scalar.activation(d.dte, d.dte, ACT.Exp).then_inc(act_step, 1)
            nc.scalar.activation(d.cdec, d.cdec, ACT.Exp).then_inc(act_step, 1)

        @block.vector
        def _(dve):
            st = Steps(dve, step)
            V = nc.vector
            dve.wait_ge(logits, 1)
            psv = c.ps[:, 0, 0:W]
            b = lambda t, n: t.unsqueeze(1).to_broadcast([P, TT, n])
            st.then_wait(V.tensor_tensor(v3(x), v3(psv), b(bias, n2), ALU.add))
            st.then_wait(V.tensor_scalar(heads(x, HEADS), heads(x, HEADS), -1.0, None, ALU.mult))
            st.then_wait(V.scalar_tensor_tensor(out=ax, in0=x, scalar=-1.0, in1=x, op0=ALU.mult,
                                                op1=ALU.max))
            dve.wait_ge(act_step, 2)
            st.then_wait(V.tensor_scalar(u1, e, 1.0, None, ALU.add))
            st.then_wait(V.tensor_scalar(eq, u1, 1.0, None, ALU.is_equal))
            st.then_wait(V.scalar_tensor_tensor(out=ax, in0=u1, scalar=-1.0, in1=eq, op0=ALU.add,
                                                op1=ALU.add))
            st.then_wait(V.reciprocal(ax, ax))
            dve.wait_ge(act_step, 3)
            st.then_wait(V.tensor_tensor(ln, ln, eq, ALU.add))
            st.then_wait(V.tensor_tensor(ln, ln, ax, ALU.mult))
            st.then_wait(V.tensor_tensor(ln, ln, e, ALU.mult))
            st.then_wait(V.scalar_tensor_tensor(out=res, in0=x, scalar=0.0, in1=ln, op0=ALU.max,
                                                op1=ALU.add))
            st.then_wait(V.tensor_scalar(a_neg, a_neg, -1.0, None, ALU.mult))
            st.done(V.tensor_copy(v3(d.dt), heads(res, 0)))
            st.done(V.tensor_tensor(v3(d.dta), heads(res, 0), b(a_neg, HEADS), ALU.mult))
            assert st.n == DTA_DONE
            st.done(V.memset(one_row, 1.0))
            dve.wait_ge(summed, 1)
            st.then_wait(V.tensor_scalar(d.ncs, c.ps[:, 1, 0:P], -1.0, None, ALU.mult))
            st.done(V.tensor_tensor(d.dte, c.ps[:, 2, 0:P], d.ncs, ALU.add))
            st.done(V.tensor_copy(d.cdec, c.ps[:, 2, 0:P]))
            assert st.n == DECAY_ARGS
            dve.wait_ge(turned, 1)
            st.then_wait(V.tensor_copy(fT, c.ps[0:HEADS, 3:5, :].rearrange("p b n -> p (b n)")))
            st.done(V.tensor_tensor_scan(run, one_row, fT, 0.0, ALU.mult, ALU.add))
            assert st.n == RUN_DONE
            dve.wait_ge(act_step, 5)
            st.then_wait(V.tensor_tensor(d.dte, d.dte, d.dt, ALU.mult))


DTA_DONE, DECAY_ARGS, RUN_DONE = 14, 18, 20


def phase_ssd(c, tok, bcT, y, tmp):
    nc = c.nc
    d = Decays(c)
    tokv = tok.rearrange("p (t n) -> p t n", t=TT)
    bcv = bcT.rearrange("p (b s) -> p b s", b=2 * GROUPS)
    N = HPG * P
    take = lambda a, n=512: tmp[:, a:a + n]
    decayed_in = [take(0), take(512)]
    dec = [take(1024), take(1536)]
    bTc, cTc, btok = take(2048), take(2560), take(3072)
    xdt, xde = take(3584, 1024), take(4608, 1024)
    prev, skipped = take(5632, 1024), take(6656, 1024)
    hv = lambda ap: ap.rearrange("p (h n) -> p h n", n=HD)
    with ExitStack() as ctx:
        S = lambda n: c.sem(ctx, "ssd_" + n)
        staged = S("staged")
        laid = S("laid")
        cb = S("cb")
        spread = S("spread")
        decayed = S("decayed")
        weighted = S("weighted")
        scaled = S("scaled")
        y_off, y_diag = S("y_off"), S("y_diag")
        state = S("state")
        skip = S("skip")
        part = S("part")
        carried = S("carried")
        summed = S("summed")
        block = ctx.enter_context(nc.Block())

        @block.scalar
        def _(act):
            act.sem_inc(y_diag, 4)
            act.sem_inc(state, 1)
            act.sem_inc(y_off, 1)
            with act.Fori(0, TT) as i:
                act.wait_ge(state, i + 1)
                for dst, src in ((bTc.rearrange("p (g s) -> p g s", g=4), bcv[:, 0:4, bass.ds(i * P, P)]),
                                 (cTc.rearrange("p (g s) -> p g s", g=4), bcv[:, 4:8, bass.ds(i * P, P)]),
                                 (btok, tokv[:, bass.ds(i, 1), D:D + 512].rearrange("p a n -> p (a n)"))):
                    nc.scalar.activation(dst, src, ACT.Identity).then_inc(staged, 1)
                for g in range(GROUPS):
                    act.wait_ge(spread, i * 4 + (g + 5))
                    act.wait_ge(y_diag, i * 4 + (g + 3))
                    for r in range(HPG):
                        h = g * HPG + r
                        x = nc.scalar.activation(dec[g % 2][:, r * P:(r + 1) * P],
                                                 c.ps[:, 1 + g % 2, r * P:(r + 1) * P], ACT.Exp,
                                                 bias=d.ncs[:, bass.ds(i * HEADS + h, 1)])
                    x.then_inc(decayed, 1)

        @block.gpsimd
        def _(pool):
            pool.sem_inc(spread, 4)
            with pool.Fori(0, TT) as i:
                for g in range(GROUPS):
                    pool.wait_ge(spread, i * 4 + (g + 3))
                    nc.gpsimd.tensor_tensor(
                        decayed_in[g % 2].rearrange("p (r l) -> p r l", r=HPG),
                        c.upto[:].unsqueeze(1).to_broadcast([P, HPG, P]),
                        d.dta[:, bass.ds(i * HEADS + g * HPG, HPG)].unsqueeze(2)
                        .to_broadcast([P, HPG, P]), ALU.mult).then_inc(laid, 1)
                pool.wait_ge(summed, i + 1)
                nc.gpsimd.tensor_tensor(
                    hv(skipped), hv(tokv[:, bass.ds(i, 1), 0:D].rearrange("p a n -> p (a n)")),
                    d.skip.unsqueeze(2).to_broadcast([P, HEADS, HD]), ALU.mult).then_inc(skip, 1)

        @block.tensor
        def _(pe):
            with pe.Fori(0, TT) as i:
                pe.wait_ge(staged, i * 3 + 3)
                pe.wait_ge(weighted, i * 4 + 4)
                pe.wait_ge(carried, i + 1)
                for g in range(GROUPS):
                    mm = nc.tensor.matmul(c.ps[:, 0, g * P:(g + 1) * P], bTc[:, g * P:(g + 1) * P],
                                          cTc[:, g * P:(g + 1) * P], start=True, stop=True)
                mm.then_inc(cb, 1)

                def running(g):
                    pe.wait_ge(laid, i * 4 + (g + 1))
                    pe.wait_ge(decayed, i * 4 + (g + 3))
                    bank = c.ps[:, 1 + g % 2, :]
                    nc.tensor.matmul(bank, c.identb[:], c.maskTb[:].rearrange("p r l -> p (r l)"),
                                     start=True, stop=False, skip_group_check=True)
                    nc.tensor.matmul(bank, c.ones[:], decayed_in[g % 2], start=False, stop=True,
                                     skip_group_check=True).then_inc(spread, 1)

                def diagonal(g):
                    pe.wait_ge(weighted, i * 4 + (g + 5))
                    for r in range(HPG):
                        h = g * HPG + r
                        mm = nc.tensor.matmul(c.ps[:, 3 + h // 8, (h % 8) * HD:(h % 8 + 1) * HD],
                                              dec[g % 2][:, r * P:(r + 1) * P],
                                              xdt[:, h * HD:(h + 1) * HD], start=True, stop=True)
                    mm.then_inc(y_diag, 1)

                running(0)
                running(1)
                pe.wait_ge(summed, i + 1)
                for g in range(GROUPS):
                    mm = nc.tensor.matmul(c.ps[:, 5 + g // 2, (g % 2) * 256:(g % 2 + 1) * 256],
                                          cTc[:, g * P:(g + 1) * P],
                                          prev[:, g * 256:(g + 1) * 256], start=True, stop=True)
                mm.then_inc(y_off, 1)
                running(2)
                pe.wait_ge(scaled, i * 2 + 2)
                diagonal(0)
                running(3)
                for g in range(1, GROUPS):
                    diagonal(g)
                for g in range(GROUPS):
                    mm = nc.tensor.matmul(c.ps[:, (7, 0)[g // 2], (g % 2) * 256:(g % 2 + 1) * 256],
                                          btok[:, g * P:(g + 1) * P],
                                          xde[:, g * 256:(g + 1) * 256], start=True, stop=True)
                mm.then_inc(state, 1)

        @block.vector
        def _(dve):
            V = nc.vector
            dve.sem_inc(decayed, 4)
            dve.sem_inc(weighted, 4)
            dve.sem_inc(summed, 1)
            dve.sem_inc(part, 1)
            V.memset(prev, 0.0).then_inc(carried, 1)
            with dve.Fori(0, TT) as i:
                xs = hv(tokv[:, bass.ds(i, 1), 0:D].rearrange("p a n -> p (a n)"))
                col = lambda t: t[:, bass.ds(i * HEADS, HEADS)].unsqueeze(2)\
                    .to_broadcast([P, HEADS, HD])
                dve.wait_ge(state, i + 1)
                V.tensor_tensor(hv(xdt), xs, col(d.dt), ALU.mult).then_inc(scaled, 1)
                V.tensor_tensor(hv(xde), xs, col(d.dte), ALU.mult).then_inc(scaled, 1)
                dve.wait_ge(cb, i + 1)
                for g in range(GROUPS):
                    dve.wait_ge(decayed, i * 4 + (g + 5))
                    m = dec[g % 2].rearrange("p (r l) -> p r l", r=HPG)
                    V.tensor_tensor(m, m, c.ps[:, 0, g * P:(g + 1) * P].unsqueeze(1)
                                    .to_broadcast([P, HPG, P]), ALU.mult).then_inc(weighted, 1)
                dve.wait_ge(y_off, i + 2)
                yc = y[:, bass.ds(i * D, D)]
                flat = lambda b: c.ps[:, b:b + 2, :].rearrange("p b n -> p (b n)")
                V.tensor_tensor(hv(yc), hv(flat(5)), col(d.ecs), ALU.mult).then_inc(part, 1)
                dve.wait_ge(carried, i + 1)
                V.tensor_tensor(hv(prev), hv(prev), col(d.cdec), ALU.mult).then_inc(part, 1)
                dve.wait_ge(part, i * 4 + 3)
                dve.wait_ge(y_diag, i * 4 + 8)
                V.tensor_tensor(yc, yc, flat(3), ALU.add).then_inc(part, 1)
                dve.wait_ge(state, i + 2)
                V.tensor_tensor(prev[:, 0:512], prev[:, 0:512], c.ps[:, 7, :], ALU.add)\
                    .then_inc(part, 1)
                V.tensor_tensor(prev[:, 512:1024], prev[:, 512:1024], c.ps[:, 0, :], ALU.add)\
                    .then_inc(carried, 1)
                dve.wait_ge(part, i * 4 + 5)
                dve.wait_ge(skip, i + 1)
                V.tensor_tensor(yc, yc, skipped, ALU.add).then_inc(summed, 1)


def convolve_tap(dve, x, taps, bias, src, acc, tapped):
    n = taps.shape[2]
    b, back = divmod(x, n)
    w = taps[:, b, n - 1 - back:n - back]
    if back == 0:
        ins = dve.tensor_scalar(acc[:, b, :], src[:, b, :], w, bias[:, b:b + 1], ALU.mult, ALU.add)
    else:
        ins = dve.scalar_tensor_tensor(out=acc[:, b, back:], in0=src[:, b, 0:SEQ - back], scalar=w,
                                       in1=acc[:, b, back:], op0=ALU.mult, op1=ALU.add)
    ins.then_inc(tapped, 1)


def phase_dense(c, name, jobs, region, aside=None, trailing=0, move=(), made_by=None):
    nc = c.nc
    raw = [c.at(region, u * 2 * BANK, 2 * BANK).rearrange("p (k n) -> p k n", k=2) for u in range(2)]
    wp = [c.rounded(f"{name}_w{s}", region, 4 * BANK + s * 2 * BANK, BANK) for s in range(2)]
    tp = [c.rounded(f"{name}_t{s}", region, 8 * BANK + s * 2 * SEQ, SEQ) for s in range(2)]
    steps = [(j, k) for j, job in enumerate(jobs) for k in range(job[1].shape[1])]
    NS = len(steps)
    last = [sum(j[1].shape[1] for j in jobs[:n + 1]) - 1 for n in range(len(jobs))]
    on_act = [j[2] in ("act", "act_T", "keep_T") for j in jobs]
    bank = lambda ap, t: ap[t] if isinstance(ap, list) else ap[:, t, :]
    before = lambda n, act: TT * sum(1 for x in on_act[:n] if x == act)
    keeps = [n for n, j in enumerate(jobs) if j[2] == "keep_T"]
    with ExitStack() as ctx:
        kept = [c.sem(ctx, f"{name}_kept{n}") for n in keeps]
        wload = [c.sem(ctx, f"{name}_wload{s}") for s in range(2)]
        w_high, w_low = c.sem(ctx, f"{name}_w_high"), c.sem(ctx, f"{name}_w_low")
        t_high, t_low = c.sem(ctx, f"{name}_t_high"), c.sem(ctx, f"{name}_t_low")
        stepped = c.sem(ctx, f"{name}_stepped")
        product = c.sem(ctx, f"{name}_product")
        by_act = c.sem(ctx, f"{name}_by_act")
        by_vec = c.sem(ctx, f"{name}_by_vec")
        multiplied = c.sem(ctx, f"{name}_multiplied")
        tapped, moved = c.sem(ctx, f"{name}_tapped"), c.sem(ctx, f"{name}_moved")
        block = ctx.enter_context(nc.Block())

        @block.sync
        def _(sp):
            for u in range(NS // 2):
                j, k = steps[2 * u]
                if u >= 2:
                    sp.wait_ge(w_low, 2 * (u - 1))
                sp.dma_start(raw[u % 2], jobs[j][1][:, k:k + 2, :]).then_inc(wload[u % 2], 16)

        @block.tensor
        def _(pe):
            for n, (j, k) in enumerate(steps):
                s = n % 2
                pe.wait_ge(w_low, n + 1)
                pe.wait_ge(t_low, n + 1)
                for t in range(TT):
                    if k == 0 and j >= 1:
                        pe.wait_ge(by_act if on_act[j - 1] else by_vec,
                                   before(j - 1, on_act[j - 1]) + t + 1)
                    if jobs[j][2].endswith("_T"):
                        a = [x[:, t // 2 * P:(t // 2 + 1) * P] for x in wp[s]]
                        b = [x[:, t % 2 * BANK:(t % 2 + 1) * BANK] for x in tp[s]]
                    else:
                        a, b = [x[:, t * P:(t + 1) * P] for x in tp[s]], wp[s]
                    nc.tensor.matmul(c.ps[:, t, :], a[0], b[0], start=(k == 0), stop=False)
                    nc.tensor.matmul(c.ps[:, t, :], a[0], b[1], start=False, stop=False)
                    mm = nc.tensor.matmul(c.ps[:, t, :], a[1], b[0], start=False,
                                          stop=(n == last[j]))
                    if n == last[j]:
                        mm.then_inc(product, 1)
                if n != last[j]:
                    mm.then_inc(stepped, 1)
                else:
                    pe.wait_ge(product, TT * (j + 1))
                    pe.sem_inc(stepped, 1)

        @block.scalar
        def _(act):
            def high_parts(n):
                j, k = steps[n]
                s = n % 2
                if n >= 2:
                    act.wait_ge(stepped, n - 1)
                if made_by and j in made_by:
                    act.wait_ge(by_vec, before(made_by[j], False) + 2 * k + 2)
                nc.scalar.activation(tp[s][0], jobs[j][0][:, k, :], ACT.Identity).then_inc(t_high, 1)
                act.wait_ge(wload[n // 2 % 2], 16 * (n // 4 + 1))
                nc.scalar.activation(wp[s][0], raw[n // 2 % 2][:, n % 2, :], ACT.Identity)\
                    .then_inc(w_high, 1)

            for dst, src in move:
                nc.scalar.activation(dst, src, ACT.Identity).then_inc(moved, 1)
            for n in range(NS + 1):
                if n < NS:
                    high_parts(n)
                j = steps[n - 1][0]
                if n >= 1 and n - 1 == last[j] and on_act[j]:
                    for m in keeps:
                        if m < j and jobs[m][3] is jobs[j][3]:
                            act.wait_ge(kept[keeps.index(m)], 16)
                    for t in range(TT):
                        act.wait_ge(product, TT * j + t + 1)
                        nc.scalar.activation(bank(jobs[j][3], t), c.ps[:, t, :], jobs[j][4],
                                             scale=jobs[j][6] if j in keeps else 1.0)\
                            .then_inc(by_act, 1)
                    if j in keeps:
                        act.wait_ge(by_act, before(j + 1, True))
                        act.dma_start(jobs[j][5].rearrange("(f p) s -> p f s", p=P),
                                      jobs[j][3].rearrange("p (f h) n -> p f (h n)", h=2))\
                            .then_inc(kept[keeps.index(j)], 16)
            for m in range(len(keeps)):
                act.wait_ge(kept[m], 16)

        @block.vector
        def _(dve):
            V = nc.vector

            def low_parts(n):
                j, k = steps[n]
                s = n % 2
                dve.wait_ge(t_high, n + 1)
                V.tensor_tensor(tp[s][1], jobs[j][0][:, k, :], tp[s][0].bitcast(F32), ALU.subtract)\
                    .then_inc(t_low, 1)
                dve.wait_ge(w_high, n + 1)
                V.tensor_tensor(wp[s][1], raw[n // 2 % 2][:, n % 2, :], wp[s][0].bitcast(F32),
                                ALU.subtract).then_inc(w_low, 1)

            pairs = 0
            for n in range(NS + max(1, trailing)):
                if n < NS:
                    low_parts(n)
                if aside is not None:
                    aside(n, tapped, by_act, by_vec, moved)
                if n > NS or n == 0 or n - 1 != last[steps[n - 1][0]]:
                    continue
                j = steps[n - 1][0]
                kind, dst, other = jobs[j][2:5]
                if on_act[j]:
                    continue
                if before(j, True):
                    dve.wait_ge(by_act, before(j, True))
                for t in range(TT):
                    dve.wait_ge(product, TT * j + t + 1)
                    src = c.ps[:, t, :]
                    if kind in ("mul", "mul_T"):
                        x = V.tensor_tensor(bank(dst, t), src, other[:, t, :], ALU.mult)
                    elif kind == "add":
                        x = V.tensor_tensor(dst[:, t, :], src, dst[:, t, :], ALU.add)
                    else:
                        V.tensor_tensor(other[:, t, :], src, other[:, t, :], ALU.mult)\
                            .then_inc(multiplied, 1)
                        pairs += 1
                        dve.wait_ge(multiplied, pairs)
                        x = V.tensor_tensor(dst[:, t, :], other[:, t, :], dst[:, t, :], ALU.add)
                    x.then_inc(by_vec, 1)


def phase_turn(c, name, src, dst, gate=None, groups=0, gain_dram=None, gain_times=1.0, width=D):
    nc = c.nc
    n_k = width // P
    gw = width // max(groups, 1)
    sv = src.rearrange("p (t d) -> p t d", t=TT)
    gv = gate.rearrange("p (t d) -> p t d", t=TT) if gate is not None else None
    dv = dst.rearrange("p (k s) -> p k s", k=n_k)
    ng = max(groups, 1)
    ss = c.small[:, 0:TT * ng]
    rstd, gain = c.small[:, 32:32 + TT * ng], c.small[:, 64:64 + n_k]
    with ExitStack() as ctx:
        loaded, squared = c.sem(ctx, f"{name}_loaded"), c.sem(ctx, f"{name}_squared")
        gated, rooted = c.sem(ctx, f"{name}_gated"), c.sem(ctx, f"{name}_rooted")
        step, ready = c.sem(ctx, f"{name}_step"), c.sem(ctx, f"{name}_ready")
        turned, placed = c.sem(ctx, f"{name}_turned"), c.sem(ctx, f"{name}_placed")
        block = ctx.enter_context(nc.Block())
        halves = n_k // 4

        @block.sync
        def _(sp):
            if gain_dram is not None:
                with nc.allow_non_contiguous_dma(reason="a gain vector by chunks"):
                    g = gain_dram.rearrange("(k p) -> p k", p=P)
                    if g.shape[1] == 1 and n_k > 1:
                        for k in range(n_k):
                            sp.dma_start(gain[:, k:k + 1], g).then_inc(loaded, 16)
                    else:
                        sp.dma_start(gain, g).then_inc(loaded, 16)

        loads = 0 if gain_dram is None else (16 * n_k if gain_dram.shape[0] == P else 16)

        @block.scalar
        def _(act):
            if groups:
                for t in range(TT):
                    if gate is not None:
                        act.wait_ge(gated, t + 1)
                    for g in range(groups):
                        nc.scalar.activation(dst[:, t * width + g * gw:t * width + (g + 1) * gw],
                                             sv[:, t, g * gw:(g + 1) * gw], ACT.Square,
                                             accum_out=ss[:, t * ng + g:t * ng + g + 1])\
                            .then_inc(squared, 1)
                act.wait_ge(step, 1)
                nc.scalar.activation(rstd, rstd, ACT.Sqrt).then_inc(rooted, 1)

        @block.vector
        def _(dve):
            V = nc.vector
            if gate is not None:
                for t in range(TT):
                    V.tensor_tensor(sv[:, t, :], sv[:, t, :], gv[:, t, :], ALU.mult).then_inc(gated, 1)
            if groups:
                st = Steps(dve, step)
                dve.wait_ge(squared, TT * groups)
                st.done(V.tensor_scalar(rstd, ss, 1.0 / gw, EPS, ALU.mult, ALU.add))
                dve.wait_ge(rooted, 1)
                st.then_wait(V.reciprocal(rstd, rstd))
                for t in range(TT):
                    row = sv[:, t, :].rearrange("p (g n) -> p g n", g=groups)
                    V.tensor_tensor(row, row, rstd[:, t * ng:(t + 1) * ng].unsqueeze(2)
                                    .to_broadcast([P, groups, gw]), ALU.mult).then_inc(ready, 1)
            if gain_dram is not None:
                dve.wait_ge(loaded, loads)
                if gain_times != 1.0:
                    V.tensor_scalar(gain, gain, gain_times, None, ALU.mult).then_inc(loaded, 16)
                    dve.wait_ge(loaded, loads + 16)
            for n in range(halves * TT):
                t, h = divmod(n, halves)
                dve.wait_ge(turned, n + 1)
                out = dv[:, 4 * h:4 * h + 4, t * P:(t + 1) * P]
                ps = c.ps[:, n % 8, :].rearrange("p (k s) -> p k s", k=4)
                if gain_dram is None:
                    x = V.tensor_copy(out, ps)
                else:
                    x = V.tensor_tensor(out, ps, gain[:, 4 * h:4 * h + 4].unsqueeze(2)
                                        .to_broadcast([P, 4, P]), ALU.mult)
                x.then_inc(placed, 1)

        @block.tensor
        def _(pe):
            for n in range(halves * TT):
                t, h = divmod(n, halves)
                if groups:
                    pe.wait_ge(ready, t + 1)
                elif gate is not None:
                    pe.wait_ge(gated, t + 1)
                if n >= 8:
                    pe.wait_ge(placed, n - 7)
                for k in range(4):
                    mm = nc.tensor.transpose(c.ps[:, n % 8, k * P:(k + 1) * P],
                                             sv[:, t, (4 * h + k) * P:(4 * h + k + 1) * P],
                                             c.ident[:])
                mm.then_inc(turned, 1)


def phase_forget_attention(c, q_dram, k_dram, fcum_dram, v, y, qk, probs):
    nc = c.nc
    vv = v.rearrange("p (t n) -> p t n", t=TT)
    q = [[qk[:, (4 * p + r) * SEQ:(4 * p + r + 1) * SEQ] for r in range(2)] for p in range(2)]
    k_ = [[qk[:, (4 * p + r + 2) * SEQ:(4 * p + r + 3) * SEQ] for r in range(2)] for p in range(2)]
    buf = lambda n: probs[:, n * SEQ:(n + 1) * SEQ]
    prob, probT = [buf(0), buf(1)], [buf(2), buf(3)]
    yv = y.rearrange("p (t n) -> p t n", t=TT)
    negmax, rowsum, rinv = c.small[:, 1400:1402], c.small[:, 1402:1404], c.small[:, 1404:1406]
    PAIRS = HEADS // 2
    UNITS = [(r, t) for t in range(TT) for r in range(2)]
    NU = len(UNITS)
    GR = [(u, g) for u, (r, t) in enumerate(UNITS) for g in range(t // 4 + 1)]
    NGR = len(GR)
    first_group = {u: n for n, (u, g) in reversed(list(enumerate(GR)))}
    S_BANK, T_BANK, O_BANK = (4, 6), (0, 1), (2, 3)
    flat = lambda b: c.ps[:, b:b + 2, :].rearrange("p b n -> p (b n)")
    U = lambda i, p, n: i * (2 * NU) + (p * NU + n)
    G = lambda i, p, n: i * (2 * NGR) + (p * NGR + n)
    LOAD = 6 * 16
    with ExitStack() as ctx:
        S = lambda n: c.sem(ctx, "fa_" + n)
        loaded = [S("loaded0"), S("loaded1")]
        padded = S("padded")
        scored = S("scored")
        negated = S("negated")
        exped = S("exped")
        inverted = S("inverted")
        turned = S("turned")
        placed = S("placed")
        summed = S("summed")
        stored = S("stored")
        block = ctx.enter_context(nc.Block())

        @block.sync
        def _(sp):
            def load(p, pair):
                for r in range(2):
                    rows = bass.ds(pair * P + r * HD, HD)
                    sp.dma_start(q[p][r][0:HD, :], q_dram[rows, :]).then_inc(loaded[p], 16)
                    sp.dma_start(k_[p][r][0:HD, :], k_dram[rows, :]).then_inc(loaded[p], 16)
                    sp.dma_start(k_[p][r][HD:HD + 1, :], fcum_dram[bass.ds(pair * 2 + r, 1), :])\
                        .then_inc(loaded[p], 16)

            sp.wait_ge(padded, 8)
            for p in range(2):
                load(p, p)
            with sp.Fori(1, PAIRS // 2) as i:
                for p in range(2):
                    sp.wait_ge(stored, U(i, p, 2 - NU))
                    load(p, i * 2 + p)
            sp.sem_inc(loaded[0], LOAD)

        @block.tensor
        def _(pe):
            def score(i, p, u):
                at = U(i, p, u + 1)
                if u >= NU:
                    p, u = 1 - p, u - NU
                r, t = UNITS[u]
                n = (t + 1) * P
                pe.wait_ge(exped, at)
                for b in range((n + BANK - 1) // BANK):
                    width = min(BANK, n - b * BANK)
                    has_diag = (b + 1) * BANK >= n
                    nc.tensor.matmul(c.ps[:, S_BANK[u % 2] + b, 0:width],
                                     q[p][r][:, t * P:(t + 1) * P],
                                     k_[p][r][:, b * BANK:b * BANK + width],
                                     start=True, stop=not has_diag, skip_group_check=True)
                nc.tensor.matmul(c.ps[:, S_BANK[u % 2] + b, width - P:width],
                                 c.identb[:], c.maskb[:], start=False, stop=True,
                                 skip_group_check=True).then_inc(scored, 1)

            def turn(i, p, u):
                r, t = UNITS[u]
                pe.wait_ge(exped, U(i, p, u + 3))
                for g in range(t // 4 + 1):
                    n = first_group[u] + g
                    pe.wait_ge(placed, G(i, p, n + 1))
                    for b in range(min(4, t + 1 - 4 * g)):
                        mm = nc.tensor.transpose(
                            c.ps[:, T_BANK[n % 2], b * P:(b + 1) * P],
                            prob[u % 2][:, (4 * g + b) * P:(4 * g + b + 1) * P], c.ident[:])
                    mm.then_inc(turned, 1)

            def values(i, p, u):
                r, t = UNITS[u]
                pe.wait_ge(stored, U(i, p, u + 1))
                pe.wait_ge(placed, G(i, p, first_group[u] + t // 4 + 3))
                for b in range(t + 1):
                    mm = nc.tensor.matmul(c.ps[:, O_BANK[u % 2], 0:HD],
                                          probT[u % 2][:, b * P:(b + 1) * P],
                                          vv[:, b, bass.ds(i * (2 * P) + (p * P + r * HD), HD)],
                                          start=(b == 0), stop=(b == t))
                mm.then_inc(summed, 1)

            pe.sem_inc(summed, 2)
            pe.sem_inc(turned, 1)
            pe.wait_ge(padded, 12)
            pe.wait_ge(loaded[0], LOAD)
            score(0, 0, 0)
            score(0, 0, 1)
            with pe.Fori(0, PAIRS // 2) as i:
                for p in range(2):
                    for u in range(NU):
                        if u == NU - 2:
                            pe.wait_ge(loaded[1 - p], i * LOAD + (p + 1) * LOAD)
                        score(i, p, u + 2)
                        turn(i, p, u)
                        if u:
                            values(i, p, u - 1)
                    values(i, p, NU - 1)

        @block.scalar
        def _(act):
            act.sem_inc(exped, 2)
            with act.Fori(0, PAIRS // 2) as i:
                for p in range(2):
                    for u, (r, t) in enumerate(UNITS):
                        n = (t + 1) * P
                        act.wait_ge(negated, U(i, p, u + 1))
                        last = (first_group[u - 2] + UNITS[u - 2][1] // 4 + 2 if u >= 2 else 1)
                        act.wait_ge(turned, G(i, p, last))
                        act.wait_ge(inverted, U(i, p, u + 1))
                        nc.scalar.activation(prob[u % 2][:, 0:n], flat(S_BANK[u % 2])[:, 0:n],
                                             ACT.Exp, bias=negmax[:, u % 2:u % 2 + 1],
                                             accum_out=rowsum[:, u % 2:u % 2 + 1])\
                            .then_inc(exped, 1)

        @block.gpsimd
        def _(pool):
            for p in range(2):
                for r in range(2):
                    for m in (q[p][r], k_[p][r]):
                        nc.gpsimd.memset(m[HD:P, :], 0.0).then_inc(padded, 1)
            pool.wait_ge(padded, 8)
            for p in range(2):
                for r in range(2):
                    nc.gpsimd.memset(q[p][r][HD:HD + 1, :], 1.0).then_inc(padded, 1)

        @block.vector
        def _(dve):
            V = nc.vector

            def maxima(i, p, u):
                at = U(i, p, u + 1)
                r, t = UNITS[u % NU]
                n = (t + 1) * P
                m = negmax[:, u % 2:u % 2 + 1]
                dve.wait_ge(scored, at)
                dve.wait_ge(exped, at)
                V.tensor_reduce(m, flat(S_BANK[u % 2])[:, 0:n], AX.X, ALU.max, negate=True)\
                    .then_inc(negated, 1)

            def invert(i, p, u):
                dve.wait_ge(exped, U(i, p, u + 3))
                dve.wait_ge(stored, U(i, p, u + 1))
                V.reciprocal(rinv[:, u % 2:u % 2 + 1], rowsum[:, u % 2:u % 2 + 1])\
                    .then_inc(inverted, 1)

            def take(i, p, u):
                r, t = UNITS[u]
                for g in range(t // 4 + 1):
                    n = first_group[u] + g
                    dve.wait_ge(turned, G(i, p, n + 2))
                    width = min(4, t + 1 - 4 * g) * P
                    if g == 0:
                        dve.wait_ge(summed, U(i, p, u + 1))
                    V.tensor_copy(probT[u % 2][:, 4 * g * P:4 * g * P + width],
                                  c.ps[:, T_BANK[n % 2], 0:width]).then_inc(placed, 1)

            def store(i, p, u):
                r, t = UNITS[u]
                dve.wait_ge(summed, U(i, p, u + 3))
                dve.wait_ge(inverted, U(i, p, u + 3))
                V.tensor_scalar(yv[:, t, bass.ds(i * (2 * P) + (p * P + r * HD), HD)],
                                c.ps[:, O_BANK[u % 2], 0:HD], rinv[:, u % 2:u % 2 + 1], None,
                                ALU.mult).then_inc(stored, 1)

            dve.sem_inc(placed, 2)
            dve.sem_inc(inverted, 2)
            dve.sem_inc(stored, 2)
            maxima(0, 0, 0)
            maxima(0, 0, 1)
            with dve.Fori(0, PAIRS // 2) as i:
                for p in range(2):
                    for u in range(NU):
                        invert(i, p, u)
                        maxima(i, p, u + 2)
                        take(i, p, u)
                        if u:
                            store(i, p, u - 1)
                    store(i, p, NU - 1)


def phase_post(c, x_dram, gain_dram, src, dst, tmp):
    nc = c.nc
    NG2 = TT // 2
    two = lambda ap, g: ap[:, 2 * g:2 * g + 2]
    v = lambda r: r.rearrange("p (t d) -> p t d", t=TT)
    sv, dv = v(src), v(dst)
    gain = tmp[:, 0:D]
    sq = tmp[:, D:2 * D]
    ss, rstd = c.small[:, 0:8], c.small[:, 8:16]
    with ExitStack() as ctx:
        loaded = [c.sem(ctx, f"post_loaded{t}") for t in range(3)]
        squared, rooted = c.sem(ctx, "post_squared"), c.sem(ctx, "post_rooted")
        meaned, inverted = c.sem(ctx, "post_meaned"), c.sem(ctx, "post_inverted")
        scaled = c.sem(ctx, "post_scaled")
        block = ctx.enter_context(nc.Block())

        @block.sync
        def _(sp):
            sp.dma_start(gain, bcast(gain_dram, D)).then_inc(loaded[2], 16)
            rows = x_dram.rearrange("(t p) d -> p t d", p=P)
            for t in range(2):
                sp.dma_start(dv[:, 4 * t:4 * t + 4, :], rows[:, 4 * t:4 * t + 4, :])\
                    .then_inc(loaded[t], 16)

        @block.scalar
        def _(act):
            for g in range(NG2 + 1):
                for t in range(2 * g, 2 * g + 2) if g < NG2 else ():
                    if t:
                        act.wait_ge(squared, t)
                    nc.scalar.activation(sq, sv[:, t, :], ACT.Square, accum_out=ss[:, t:t + 1])\
                        .then_inc(squared, 1)
                if g:
                    act.wait_ge(meaned, g)
                    nc.scalar.activation(two(rstd, g - 1), two(rstd, g - 1), ACT.Sqrt)\
                        .then_inc(rooted, 1)

        @block.vector
        def _(dve):
            V = nc.vector

            def scale(t):
                V.scalar_tensor_tensor(out=sv[:, t, :], in0=sv[:, t, :], scalar=rstd[:, t:t + 1],
                                       in1=gain, op0=ALU.mult, op1=ALU.mult).then_inc(scaled, 1)

            def add(t):
                dve.wait_ge(scaled, t + 1)
                if t % 4 == 0:
                    dve.wait_ge(loaded[t // 4], 16)
                V.tensor_tensor(dv[:, t, :], dv[:, t, :], sv[:, t, :], ALU.add)

            dve.wait_ge(loaded[2], 16)
            for g in range(NG2):
                dve.wait_ge(squared, 2 * g + 2)
                V.tensor_scalar(two(rstd, g), two(ss, g), 1.0 / D, EPS, ALU.mult, ALU.add)\
                    .then_inc(meaned, 1)
                if g:
                    add(2 * g - 2)
                    add(2 * g - 1)
                dve.wait_ge(rooted, g + 1)
                V.reciprocal(two(rstd, g), two(rstd, g)).then_inc(inverted, 1)
                dve.wait_ge(inverted, g + 1)
                scale(2 * g)
                scale(2 * g + 1)
            add(TT - 2)
            add(TT - 1)


def phase_taps(c, raw_taps, dw_w, dw_b):
    nc = c.nc
    NB = CCH // P
    with ExitStack() as ctx:
        params, turned = c.sem(ctx, "tp_params"), c.sem(ctx, "tp_turned")
        block = ctx.enter_context(nc.Block())

        @block.sync
        def _(sp):
            sp.dma_start(raw_taps[0:CW, 0:CCH], dw_w).then_inc(params, 16)
            with nc.allow_non_contiguous_dma(reason="a bias vector by chunks"):
                sp.dma_start(c.tap_bias2, dw_b.rearrange("(b p) -> p b", p=P)).then_inc(params, 16)
            sp.wait_ge(params, 32)

        @block.tensor
        def _(pe):
            pe.wait_ge(params, 32)
            for b in range(NB):
                mm = nc.tensor.transpose(c.ps[:, 7, b * CW:(b + 1) * CW],
                                         raw_taps[0:CW, b * P:(b + 1) * P], c.ident[0:CW, 0:CW])
            mm.then_inc(turned, 1)

        @block.vector
        def _(dve):
            dve.wait_ge(turned, 1)
            nc.vector.tensor_copy(c.taps2.rearrange("p b j -> p (b j)"), c.ps[:, 7, 0:NB * CW])


def phase_channel_norm(c, acc, sq, rstd, g_dram, b_dram):
    nc = c.nc
    NB = CCH // P
    av = acc.rearrange("p (b n) -> p b n", b=NB)
    qv = sq.rearrange("p (b n) -> p b n", b=NB)
    g, b_ = c.small[:, 0:NB], c.small[:, 8:8 + NB]
    flat = lambda b: c.ps[:, b:b + 2, :].rearrange("p b n -> p (b n)")
    with ExitStack() as ctx:
        S = lambda n: c.sem(ctx, "cn_" + n)
        params, meaned, centred, squared = S("params"), S("meaned"), S("centred"), S("squared")
        spread, step, rooted, scaled, done = S("spread"), S("step"), S("rooted"), S("scaled"), S("done")
        block = ctx.enter_context(nc.Block())

        @block.sync
        def _(sp):
            with nc.allow_non_contiguous_dma(reason="per-channel vectors by chunks"):
                sp.dma_start(g, g_dram.rearrange("(b p) -> p b", p=P)).then_inc(params, 16)
                sp.dma_start(b_, b_dram.rearrange("(b p) -> p b", p=P)).then_inc(params, 16)

        @block.tensor
        def _(pe):
            def over_channels(src, bank, ready):
                for b in range(NB):
                    if ready is not None:
                        pe.wait_ge(ready, b + 1)
                    for h in range(2):
                        mm = nc.tensor.matmul(c.ps[:, bank + h, :], c.ones[:],
                                              src[:, b, h * BANK:(h + 1) * BANK],
                                              start=(b == 0), stop=(b == NB - 1))
                return mm
            over_channels(av, 0, None).then_inc(meaned, 1)
            over_channels(qv, 2, squared).then_inc(spread, 1)

        @block.scalar
        def _(act):
            for b in range(NB):
                act.wait_ge(centred, b + 1)
                nc.scalar.activation(qv[:, b, :], av[:, b, :], ACT.Square).then_inc(squared, 1)
            act.wait_ge(step, 1)
            nc.scalar.activation(rstd, rstd, ACT.Sqrt).then_inc(rooted, 1)
            act.wait_ge(params, 32)
            for b in range(NB):
                act.wait_ge(scaled, b + 1)
                nc.scalar.activation(av[:, b, :], av[:, b, :], ACT.Silu, scale=g[:, b:b + 1],
                                     bias=b_[:, b:b + 1]).then_inc(done, 1)

        @block.vector
        def _(dve):
            V = nc.vector
            dve.wait_ge(meaned, 1)
            for b in range(NB):
                V.scalar_tensor_tensor(out=av[:, b, :], in0=flat(0), scalar=-1.0 / CCH, in1=av[:, b, :],
                                       op0=ALU.mult, op1=ALU.add).then_inc(centred, 1)
            dve.wait_ge(spread, 1)
            V.tensor_scalar(rstd, flat(2), 1.0 / CCH, EPS, ALU.mult, ALU.add).then_inc(step, 1)
            dve.wait_ge(rooted, 1)
            V.reciprocal(rstd, rstd).then_inc(step, 1)
            dve.wait_ge(step, 2)
            dve.wait_ge(squared, NB)
            for b in range(NB):
                V.tensor_tensor(av[:, b, :], av[:, b, :], rstd, ALU.mult).then_inc(scaled, 1)


def phase_diff_attention(c, raw, q_g, k_g, lambdas, v, o, q_at, k_at, work, work_T):
    nc = c.nc
    vv = v.rearrange("p (t n) -> p t n", t=TT)
    ov = o.rearrange("p (t n) -> p t n", t=TT)
    take = lambda ap, n: ap[:, n * SEQ:(n + 1) * SEQ]
    q_of = [[take(q_at, 2 * h + r) for r in range(2)] for h in range(DH)]
    k_of = [take(k_at, h) for h in range(DH)]
    prob = [[take(work, 2 * s + r) for r in range(2)] for s in range(2)]
    probT = [take(work_T, 0), take(work_T, 1)]
    sq = [take(work, 0), take(work, 1)]
    root = [take(work, 2), take(work, 3)]
    sm = lambda a, n=2: c.small[:, 1400 + a:1400 + a + n]
    negmax, gain, neglam, dots, eps = sm(0), sm(2), sm(4, 1), sm(5), sm(7, 1)
    rowsum, rinv, coef = [sm(8), sm(10)], [sm(12), sm(14)], [sm(16, 1), sm(17, 1)]
    halves_of = c.small[:, 1160:1160 + P]
    lam_rows = c.small[:, 0:4 * DHD].rearrange("p (j n) -> p j n", j=4)
    lam_prod = c.small[:, 4 * DHD:6 * DHD].rearrange("p (j n) -> p j n", j=2)
    UNITS = [(h, t) for h in range(DH) for t in range(TT)]
    NU = len(UNITS)
    GR = [(n, g) for n, (h, t) in enumerate(UNITS) for g in range(t // 4 + 1)]
    first = {n: x for x, (n, g) in reversed(list(enumerate(GR)))}
    flat = lambda b: c.ps[:, b:b + 2, :].rearrange("p b n -> p (b n)")
    S_BANK = (4, 6)
    NN = 2 * DH
    with ExitStack() as ctx:
        S = lambda n: c.sem(ctx, "da_" + n)
        params, lam_step, filled = S("params"), S("lam_step"), S("filled")
        lam_dots, lam_exped = S("lam_dots"), S("lam_exped")
        squared, meaned, rooted, inverted = S("squared"), S("meaned"), S("rooted"), S("inverted")
        normed = S("normed")
        scored = S("scored")
        negated = S("negated")
        exped = S("exped")
        weighed = S("weighed")
        combined = S("combined")
        turned, placed = S("turned"), S("placed")
        summed, stored = S("summed"), S("stored")
        block = ctx.enter_context(nc.Block())

        @block.gpsimd
        def _(pool):
            nc.gpsimd.memset(halves_of, 0.0).then_inc(filled, 1)
            nc.gpsimd.memset(eps, EPS).then_inc(filled, 1)
            pool.wait_ge(filled, 2)
            for r in range(2):
                nc.gpsimd.memset(halves_of[r * DHD:(r + 1) * DHD, r * DHD:(r + 1) * DHD],
                                 1.0 / DHD).then_inc(filled, 1)
            for h in range(DH):
                for r in range(2):
                    nc.gpsimd.memset(q_of[h][r][(1 - r) * DHD:(2 - r) * DHD, :], 0.0)\
                        .then_inc(filled, 1)

        @block.sync
        def _(sp):
            with nc.allow_non_contiguous_dma(reason="two gain vectors"):
                for j, g in enumerate((q_g, k_g)):
                    for r in range(2):
                        sp.dma_start(gain[r * DHD:(r + 1) * DHD, j:j + 1],
                                     g.rearrange("(p a) -> p a", a=1)).then_inc(params, 16)
            for j, l in enumerate(lambdas):
                sp.dma_start(lam_rows[:, j, :], bcast(l, DHD)).then_inc(params, 16)

        @block.tensor
        def _(pe):
            pe.wait_ge(filled, 4)
            for x in range(NN):
                pe.wait_ge(squared, x + 1)
                if x >= 4:
                    pe.wait_ge(rooted, x - 3)
                for b in range(2):
                    mm = nc.tensor.matmul(c.ps[:, 2 * (x % 4) + b, :], halves_of,
                                          sq[x % 2][:, b * BANK:(b + 1) * BANK], start=True, stop=True)
                mm.then_inc(meaned, 1)

            def score(m):
                h, t = UNITS[m // 2]
                n = (t + 1) * P
                if m >= 2:
                    pe.wait_ge(exped, m - 1)
                for b in range((n + BANK - 1) // BANK):
                    width = min(BANK, n - b * BANK)
                    nc.tensor.matmul(c.ps[:, S_BANK[m % 2] + b, 0:width],
                                     q_of[h][m % 2][:, t * P:(t + 1) * P],
                                     k_of[h][:, b * BANK:b * BANK + width],
                                     start=True, stop=False, skip_group_check=True)
                nc.tensor.matmul(c.ps[:, S_BANK[m % 2] + b, width - P:width], c.identb[:],
                                 c.maskb[:], start=False, stop=True,
                                 skip_group_check=True).then_inc(scored, 1)

            def turn(n):
                t = UNITS[n][1]
                pe.wait_ge(combined, n + 1)
                for g in range(t // 4 + 1):
                    x = first[n] + g
                    if x >= 2:
                        pe.wait_ge(placed, x - 1)
                    for b in range(min(4, t + 1 - 4 * g)):
                        mm = nc.tensor.transpose(c.ps[:, x % 2, b * P:(b + 1) * P],
                                                 prob[n % 2][0][:, (4 * g + b) * P:
                                                                (4 * g + b + 1) * P], c.ident[:])
                    mm.then_inc(turned, 1)

            def values(n):
                h, t = UNITS[n]
                if n >= 2:
                    pe.wait_ge(stored, n - 1)
                pe.wait_ge(placed, first[n] + t // 4 + 1)
                for b in range(t + 1):
                    mm = nc.tensor.matmul(c.ps[:, 2 + n % 2, 0:DV],
                                          probT[n % 2][:, b * P:(b + 1) * P],
                                          vv[:, b, h * DV:(h + 1) * DV],
                                          start=(b == 0), stop=(b == t))
                mm.then_inc(summed, 1)

            pe.wait_ge(filled, 4 + 2 * DH)
            pe.wait_ge(normed, 3 * DH)
            pe.wait_ge(rooted, NN)
            for n in range(NU + 1):
                for m in ((0, 1) if n == 0 else ()) + (2 * n + 2, 2 * n + 3):
                    if m < 2 * NU:
                        score(m)
                if n < NU:
                    turn(n)
                if n:
                    values(n - 1)

        @block.scalar
        def _(act):
            for x in range(NN + 1):
                if x < NN:
                    if x >= 2:
                        act.wait_ge(meaned, x - 1)
                    nc.scalar.activation(sq[x % 2], take(raw, x), ACT.Square).then_inc(squared, 1)
                if x >= 1:
                    y = x - 1
                    act.wait_ge(meaned, y + 1)
                    if y == 0:
                        act.wait_ge(filled, 2)
                    if y >= 2:
                        act.wait_ge(normed, 2 * (y - 1) if y - 1 <= DH else DH + y - 1)
                    nc.scalar.activation(root[y % 2], flat(2 * (y % 4)), ACT.Sqrt, bias=eps)\
                        .then_inc(rooted, 1)
            act.wait_ge(lam_dots, 1)
            nc.scalar.activation(dots, dots, ACT.Exp).then_inc(lam_exped, 1)
            act.wait_ge(normed, 3 * DH)
            for m in range(2 * NU):
                n, r = divmod(m, 2)
                w = (UNITS[n][1] + 1) * P
                act.wait_ge(negated, m + 1)
                if n >= 2:
                    act.wait_ge(turned, first[n - 1])
                nc.scalar.activation(prob[n % 2][r][:, 0:w], flat(S_BANK[r])[:, 0:w], ACT.Exp,
                                     bias=negmax[:, r:r + 1],
                                     accum_out=rowsum[n % 2][:, r:r + 1]).then_inc(exped, 1)

        @block.vector
        def _(dve):
            V = nc.vector
            dve.wait_ge(params, 16 * 8)
            V.tensor_scalar(gain[:, 0:1], gain[:, 0:1], float(DHD) ** -0.5, None, ALU.mult)\
                .then_inc(lam_step, 1)
            V.tensor_tensor(lam_prod, lam_rows[:, 0:4:2, :], lam_rows[:, 1:4:2, :], ALU.mult)\
                .then_inc(lam_step, 1)
            dve.wait_ge(lam_step, 2)
            for x in range(NN):
                r_ = root[x % 2]
                dve.wait_ge(rooted, x + 1)
                V.reciprocal(r_, r_).then_inc(inverted, 1)
                dve.wait_ge(inverted, x + 1)
                if x < DH:
                    for r in range(2):
                        rows = slice(r * DHD, (r + 1) * DHD)
                        V.scalar_tensor_tensor(out=q_of[x][r][rows, :], in0=take(raw, x)[rows, :],
                                               scalar=gain[rows, 0:1], in1=r_[rows, :],
                                               op0=ALU.mult, op1=ALU.mult).then_inc(normed, 1)
                else:
                    V.scalar_tensor_tensor(out=k_of[x - DH], in0=take(raw, x), scalar=gain[:, 1:2],
                                           in1=r_, op0=ALU.mult, op1=ALU.mult).then_inc(normed, 1)
            V.tensor_reduce(dots, lam_prod, AX.X, ALU.add).then_inc(lam_dots, 1)
            dve.wait_ge(lam_exped, 1)
            V.scalar_tensor_tensor(out=neglam, in0=dots[:, 1:2], scalar=-LAM_INIT, in1=dots[:, 0:1],
                                   op0=ALU.add, op1=ALU.subtract).then_inc(lam_step, 1)
            dve.wait_ge(lam_step, 3)

            def maxima(m):
                r = m % 2
                w = (UNITS[m // 2][1] + 1) * P
                dve.wait_ge(scored, m + 1)
                if m >= 2:
                    dve.wait_ge(exped, m - 1)
                V.tensor_reduce(negmax[:, r:r + 1], flat(S_BANK[r])[:, 0:w], AX.X, ALU.max,
                                negate=True).then_inc(negated, 1)

            def combine(n):
                s = n % 2
                w = (UNITS[n][1] + 1) * P
                dve.wait_ge(exped, 2 * n + 2)
                if n >= 2:
                    dve.wait_ge(stored, n - 1)
                V.reciprocal(rinv[s], rowsum[s]).then_inc(weighed, 1)
                dve.wait_ge(weighed, 2 * n + 1)
                V.scalar_tensor_tensor(out=coef[s], in0=rowsum[s][:, 0:1], scalar=neglam,
                                       in1=rinv[s][:, 1:2], op0=ALU.mult, op1=ALU.mult)\
                    .then_inc(weighed, 1)
                dve.wait_ge(weighed, 2 * n + 2)
                V.scalar_tensor_tensor(out=prob[s][0][:, 0:w], in0=prob[s][1][:, 0:w],
                                       scalar=coef[s], in1=prob[s][0][:, 0:w], op0=ALU.mult,
                                       op1=ALU.add).then_inc(combined, 1)

            def take_T(n):
                t = UNITS[n][1]
                for g in range(t // 4 + 1):
                    x = first[n] + g
                    dve.wait_ge(turned, x + 1)
                    if n >= 2:
                        dve.wait_ge(summed, n - 1)
                    w = min(4, t + 1 - 4 * g) * P
                    V.tensor_copy(probT[n % 2][:, 4 * g * P:4 * g * P + w],
                                  c.ps[:, x % 2, 0:w]).then_inc(placed, 1)

            def store(n):
                h, t = UNITS[n]
                dve.wait_ge(summed, n + 1)
                V.tensor_scalar(ov[:, t, h * DV:(h + 1) * DV], c.ps[:, 2 + n % 2, 0:DV],
                                rinv[n % 2][:, 0:1], None, ALU.mult).then_inc(stored, 1)

            maxima(0)
            maxima(1)
            for n in range(NU + 1):
                if n < NU:
                    combine(n)
                for m in (2 * n + 2, 2 * n + 3):
                    if m < 2 * NU:
                        maxima(m)
                if n < NU:
                    take_T(n)
                if n:
                    store(n - 1)


def phase_router(c, hT, w_group, w_expert, b_group, b_expert, slot_dram, tmp):
    nc = c.nc
    hv = hT.rearrange("p (k s) -> p k s", k=KC)
    NL = NG + NE
    pos_ = [0]

    def take(n, parts=P):
        a = pos_[0]
        pos_[0] += n
        return tmp[0:parts, a:a + n]

    t3 = lambda ap, t=TT: ap.rearrange("p (t n) -> p t n", t=t)
    w = take(KC * NL).rearrange("p (k n) -> p k n", k=KC)
    bias = take(NL)
    grp = t3(take(TT * 8))
    exl = t3(take(TT * NE))
    top = t3(take(TT * 8))
    gtop = t3(take(TT * 8))
    gidx, eidx = t3(take(TT * 8)), t3(take(TT * 8))
    no, no_grp = take(NE), take(NE)
    sel = [t3(take(TT * NE)) for _ in range(2)]
    both, pos, dst_, one = (t3(take(TT * NE)) for _ in range(4))
    base = t3(take(TT * NE))
    count, over, blocks, upto, k2 = (take(NE) for _ in range(5))
    ones_e = take(NE)
    gexp = t3(take(TT * NG))
    gsum, e2, s2 = take(TT), take(TT), take(TT)
    dest_f = [take(TT) for _ in range(2)]
    cmp_ = take(EXTRA * NE).rearrange("p (b n) -> p b n", b=EXTRA)
    bno, bex, bcount = take(EXTRA), take(EXTRA), take(1)
    NB = SLOTS // P
    slot_f = take(P, NB)
    zeros = take(2 * TT * NB).bitcast(I32)
    tables = take(2 * TT * P, NB).bitcast(I32).rearrange("p (t n) -> p t n", n=P)
    tables_f = take(2 * TT * P, NB).rearrange("p (t n) -> p t n", n=P)
    bl = lambda ap, n: ap.unsqueeze(2).to_broadcast([P, ap.shape[1], n])
    bt = lambda ap, t=TT: ap.unsqueeze(1).to_broadcast([P, t, ap.shape[1]])
    with ExitStack() as ctx:
        S = lambda n: c.sem(ctx, "rt_" + n)
        loaded, numbered, logits, step = S("loaded"), S("numbered"), S("logits"), S("step")
        act_step, ranked, zeroed = S("act_step"), S("ranked"), S("zeroed")
        scattered = [S(f"scattered{n}") for n in range(2 * TT)]
        read_back, turned = S("read_back"), S("turned")
        block = ctx.enter_context(nc.Block())

        @block.sync
        def _(sp):
            with nc.allow_non_contiguous_dma(reason="narrow router weights, once"):
                sp.dma_start(w[:, :, 0:NG], cols(w_group)).then_inc(loaded, 16)
                sp.dma_start(w[:, :, NG:NL], cols(w_expert)).then_inc(loaded, 16)
                sp.dma_start(bias[:, 0:NG], bcast(b_group, NG)).then_inc(loaded, 16)
                sp.dma_start(bias[:, NG:NL], bcast(b_expert, NE)).then_inc(loaded, 16)
            sp.wait_ge(numbered, 3)
            for n, table in enumerate(slot_dram):
                sp.dma_start(table.rearrange("(p b) a -> p (b a)", p=P), zeros[:, n * NB:(n + 1) * NB])\
                    .then_inc(zeroed, 16)
            for n, table in enumerate(slot_dram):
                sp.wait_ge(scattered[n], 16)
                sp.dma_start(tables[:, n, :], table.rearrange("(b p) a -> b (p a)", p=P))\
                    .then_inc(read_back, 16)

        @block.gpsimd
        def _(pool):
            pool.iota(c.expert_no, pattern=[[1, NE]], base=0, channel_multiplier=0)\
                .then_inc(numbered, 1)
            pool.iota(c.token_no, pattern=[[P, TT]], base=0, channel_multiplier=1)\
                .then_inc(numbered, 1)
            pool.memset(zeros, 0).then_inc(numbered, 1)
            pool.wait_ge(zeroed, 16 * 2 * TT)
            pool.wait_ge(numbered, 3)
            pool.wait_ge(step, DEST_DONE)
            for t in range(TT):
                for j in range(2):
                    n = 2 * t + j
                    pool.indirect_dma_start(
                        out=slot_dram[n],
                        out_offset=bass.IndirectOffsetOnAxis(c.dest[j][:, t:t + 1], 0),
                        in_=c.token_no[:, t:t + 1], in_offset=None).then_inc(scattered[n], 16)

        @block.tensor
        def _(pe):
            pe.wait_ge(loaded, 64)
            for t in range(TT):
                for k in range(KC):
                    mm = nc.tensor.matmul(c.ps[:, 0, t * NL:(t + 1) * NL], hv[:, k, t * P:(t + 1) * P],
                                          w[:, k, :], start=(k == 0), stop=(k == KC - 1))
            mm.then_inc(logits, 1)
            pe.wait_ge(step, BOTH_DONE)
            flat = both.rearrange("p t n -> p (t n)")
            nc.tensor.matmul(c.ps[:, 1, 0:TT * NE], c.before[:], flat, start=True, stop=True)
            nc.tensor.matmul(c.ps[:, 2, 0:TT * NE], c.ones[:], flat, start=True, stop=True)\
                .then_inc(ranked, 1)
            pe.wait_ge(step, SLOTS_READ)
            nc.tensor.transpose(c.ps[:, 3, 0:SLOTS // P], slot_f, c.ident[0:SLOTS // P, 0:SLOTS // P])\
                .then_inc(turned, 1)

        @block.scalar
        def _(act):
            act.wait_ge(step, GEXP_ARG)
            nc.scalar.activation(gexp, gexp, ACT.Exp).then_inc(act_step, 1)
            act.wait_ge(step, E2_ARG)
            nc.scalar.activation(e2, e2, ACT.Exp).then_inc(act_step, 1)

        @block.vector
        def _(dve):
            V = nc.vector
            st = Steps(dve, step)
            W = st.then_wait
            tt = lambda o, a, b, op: W(V.tensor_tensor(o, a, b, op))
            ts = lambda o, a, x, y, op0, op1: W(V.tensor_scalar(o, a, x, y, op0, op1))
            dve.wait_ge(numbered, 3)
            W(V.tensor_copy(no, c.expert_no))
            W(V.memset(grp, NEG))
            W(V.memset(ones_e, 1.0))
            ts(no_grp, no, float(EPG), None, ALU.is_ge, ALU.bypass)
            for g in range(2, NG):
                W(V.scalar_tensor_tensor(out=no_grp, in0=no, scalar=float(EPG * g), in1=no_grp,
                                         op0=ALU.is_ge, op1=ALU.add))
            dve.wait_ge(logits, 1)
            ps = t3(c.ps[:, 0, 0:TT * NL])
            tt(grp[:, :, 0:NG], ps[:, :, 0:NG], bt(bias[:, 0:NG]), ALU.add)
            tt(exl, ps[:, :, NG:NL], bt(bias[:, NG:NL]), ALU.add)
            for t in range(TT):
                st.done(V.max(gtop[:, t, :], grp[:, t, :]))
            dve.wait_ge(step, st.n)
            for t in range(TT):
                st.done(V.max_index(c.found[0][:, 8 * t:8 * t + 8].bitcast(U32), gtop[:, t, :],
                                    grp[:, t, :]))
            dve.wait_ge(step, st.n)
            W(V.tensor_copy(gidx.rearrange("p t n -> p (t n)"), c.found[0]))
            tt(gexp, grp[:, :, 0:NG], gtop[:, :, 0:1].to_broadcast([P, TT, NG]), ALU.subtract)
            assert st.n == GEXP_ARG, st.n
            tt(one, bt(no_grp), gidx[:, :, 0:1].to_broadcast([P, TT, NE]), ALU.is_equal)
            ts(one, one, -NEG, NEG, ALU.mult, ALU.add)
            tt(exl, exl, one, ALU.add)
            for t in range(TT):
                st.done(V.max(top[:, t, :], exl[:, t, :]))
            dve.wait_ge(step, st.n)
            for t in range(TT):
                st.done(V.max_index(c.found[1][:, 8 * t:8 * t + 8].bitcast(U32), top[:, t, :],
                                    exl[:, t, :]))
            dve.wait_ge(step, st.n)
            W(V.tensor_copy(eidx.rearrange("p t n -> p (t n)"), c.found[1]))
            for j in range(2):
                tt(sel[j], bt(no), eidx[:, :, j:j + 1].to_broadcast([P, TT, NE]), ALU.is_equal)
            tt(both, sel[0], sel[1], ALU.add)
            assert st.n == BOTH_DONE, st.n
            tt(e2.unsqueeze(2), top[:, :, 1:2], top[:, :, 0:1], ALU.subtract)
            assert st.n == E2_ARG, st.n
            dve.wait_ge(act_step, 1)
            W(V.tensor_reduce(gsum, gexp, AX.X, ALU.add))
            dve.wait_ge(act_step, 2)
            ts(s2, e2, 1.0, None, ALU.add, ALU.bypass)
            tt(s2, s2, gsum, ALU.mult)
            W(V.reciprocal(c.weight[0], s2))
            tt(c.weight[1], c.weight[0], e2, ALU.mult)
            dve.wait_ge(ranked, 1)
            total = t3(c.ps[:, 2, 0:TT * NE])
            W(V.memset(base[:, 0, :], 0.0))
            for t in range(1, TT):
                tt(base[:, t, :], base[:, t - 1, :], total[:, t - 1, :], ALU.add)
            tt(count, base[:, TT - 1, :], total[:, TT - 1, :], ALU.add)
            tt(pos, t3(c.ps[:, 1, 0:TT * NE]), base, ALU.add)
            ts(blocks, count, float(P), None, ALU.is_gt, ALU.bypass)
            for n in range(2, SEQ // P):
                W(V.scalar_tensor_tensor(out=blocks, in0=count, scalar=float(P * n), in1=blocks,
                                         op0=ALU.is_gt, op1=ALU.add))
            W(V.tensor_tensor_scan(upto, ones_e, blocks, 0.0, ALU.mult, ALU.add))
            tt(k2, upto, blocks, ALU.subtract)
            tt(k2, k2, no, ALU.subtract)
            ts(k2, k2, float(P), float(P * (NE - 1)), ALU.mult, ALU.add)
            ts(one, pos, float(P), None, ALU.is_ge, ALU.bypass)
            tt(one, one, bt(k2), ALU.mult)
            tt(dst_, pos, one, ALU.add)
            W(V.scalar_tensor_tensor(out=dst_, in0=bt(no), scalar=float(P), in1=dst_, op0=ALU.mult,
                                     op1=ALU.add))
            for j in range(2):
                tt(sel[j], sel[j], dst_, ALU.mult)
                W(V.tensor_reduce(dest_f[j], sel[j], AX.X, ALU.add))
                W(V.tensor_copy(c.dest[j], dest_f[j]))
            assert st.n == DEST_DONE, st.n
            W(V.tensor_copy(bno, c.expert_no[:, 0:EXTRA]))
            tt(cmp_, bl(bno, NE), bt(upto, EXTRA), ALU.is_ge)
            W(V.tensor_reduce(bex, cmp_, AX.X, ALU.add))
            ts(bex, bex, float(NE - 1), None, ALU.min, ALU.bypass)
            W(V.tensor_copy(c.extra_expert, bex))
            W(V.tensor_copy(c.extra_count, upto[:, NE - 1:NE]))
            dve.wait_ge(read_back, 16 * 2 * TT)
            W(V.tensor_copy(tables_f, tables))
            W(V.tensor_reduce(slot_f, tables_f.rearrange("p t n -> p n t"), AX.X, ALU.add))
            assert st.n == SLOTS_READ, st.n
            dve.wait_ge(turned, 1)
            W(V.tensor_copy(c.slot_token, c.ps[:, 3, 0:SLOTS // P]))


GEXP_ARG, BOTH_DONE, E2_ARG, DEST_DONE, SLOTS_READ = 26, 49, 50, 86, 94


def phase_experts(c, name, x_dram, y_dram, w_gate, w_up, w_down, extra):
    nc = c.nc
    ns = 1 if extra else 2
    steps = EXTRA if extra else NE // 2
    first = NE if extra else 0
    FC = DE // P
    W = KC * DE
    GATE, UP, DOWN = range(3)
    raw = [c.named(f"{name}_raw{m}", 0, m * W, W) for m in range(3)]
    part = [[p.rearrange("p (k n) -> p k n", k=(KC, KC, FC)[m])
             for p in c.rounded(f"{name}_w{m}", 0, (3 + 2 * m) * W, W)] for m in range(3)]
    at = 9 * W
    x = [c.at(0, at + s * D, D) for s in range(2)]
    at += 2 * D
    xT = [c.rounded(f"{name}_xT{s}", 0, at + 2 * s * D, D) for s in range(2)]
    at += 4 * D
    hid = [c.at(0, at + s * DE, DE) for s in range(2)]
    at += 2 * DE
    hidT = [c.rounded(f"{name}_hT{s}", 0, at + 2 * s * DE, DE) for s in range(2)]
    at += 4 * DE
    y = [c.at(0, at + s * D, D) for s in range(2)]
    assert at + 2 * D <= 6 * REGION
    flat = lambda b, n: c.ps[:, b:b + n, :].rearrange("p b n -> p (b n)")
    as_f32 = lambda r: r.bitcast(F32)
    half_of = lambda ap, h: ap.rearrange("p k n -> p (k n)")[:, h * W // 2:(h + 1) * W // 2]
    with ExitStack() as ctx:
        S = lambda n: c.sem(ctx, f"{name}_{n}")
        loaded = [[S(f"loaded{m}{h}") for h in range(2)] for m in range(3)]
        high = [S(f"high{m}") for m in range(3)]
        low = [S(f"low{m}") for m in range(3)]
        used = [S(f"used{m}") for m in range(3)]
        gathered = [S("gathered0"), S("gathered1")]
        indexed, asked = S("indexed"), S("asked")
        x_turned = S("x_turned")
        x_high, x_low = S("x_high"), S("x_low")
        opened = S("opened")
        hidden = S("hidden")
        h_turned = S("h_turned")
        h_high, h_low = S("h_high"), S("h_low")
        half0, half1 = S("half0"), S("half1")
        stored = [S("stored0"), S("stored1")]
        written = S("written")
        block = ctx.enter_context(nc.Block())

        def run(eng, cycle):
            if extra:
                count = eng.value_load(c.extra_count[0:1, 0:1], min_val=0, max_val=EXTRA)
                with eng.Fori(0, steps) as i:
                    with eng.If(i < count):
                        cycle(None, None, (i, 0))
                        cycle((i, 0), None, None)
                        cycle(None, (i, 0), None)
                return
            end = steps - 1
            cycle(None, None, (0, 0))
            cycle((0, 0), None, (0, 1))
            cycle((0, 1), (0, 0), (1, 0))
            with eng.Fori(1, end) as i:
                cycle((i, 0), (i - 1, 1), (i, 1))
                cycle((i, 1), (i, 0), (i + 1, 0))
            cycle((end, 0), (end - 1, 1), (end, 1))
            cycle((end, 1), (end, 0), None)
            cycle(None, (end, 1), None)

        @block.sync
        def _(sp):
            def load(i, s, which):
                b = i * ns + s
                if extra:
                    e = sp.value_load(c.extra_expert[0:1, bass.ds(i, 1)], min_val=0, max_val=NE - 1)
                else:
                    e = b
                for m in which:
                    kc = (KC, KC, FC)[m]
                    to = raw[m].rearrange("p (k n) -> p k n", k=kc)
                    of = (w_gate, w_up, w_down)[m][bass.ds(e, 1)]\
                        .rearrange("a (k p) n -> p (a k) n", p=P)
                    for h in range(2):
                        ks = slice(h * kc // 2, (h + 1) * kc // 2)
                        sp.wait_ge(low[m], b * 2 + (h + 1))
                        sp.dma_start(to[:, ks, :], of[:, ks, :]).then_inc(loaded[m][h], 16)

            def cycle(now, before, after):
                if after:
                    load(*after, (GATE, UP))
                if now:
                    load(*now, (DOWN,))

            sp.sem_inc(stored[0], 16)
            sp.sem_inc(stored[1], 16)
            run(sp, cycle)

        @block.gpsimd
        def _(pool):
            def gather(i, s):
                b = i * ns + s
                pool.wait_ge(x_turned, b + 1)
                nc.gpsimd.tensor_copy(c.gather_at[s], c.slot_token[:, bass.ds(b + first, 1)])\
                    .then_inc(indexed, 1)
                pool.wait_ge(indexed, b + 1)
                pool.sem_inc(asked, 1)
                pool.indirect_dma_start(
                    out=x[s], out_offset=None, in_=x_dram,
                    in_offset=bass.IndirectOffsetOnAxis(c.gather_at[s], 0)).then_inc(gathered[s], 16)

            run(pool, lambda now, before, after: after and gather(*after))

        @block.tensor
        def _(pe):
            def three(out, a, b, k, kc):
                for n, (l, r) in enumerate(((a[0], b[0]), (a[0], b[1]), (a[1], b[0]))):
                    mm = nc.tensor.matmul(out, l, r, start=(k == 0 and n == 0),
                                          stop=(k == kc - 1 and n == 2))
                return mm

            def turn_x(i, s):
                b = i * ns + s
                pe.wait_ge(gathered[s], i * 16 + 16)
                pe.wait_ge(x_low, b + 1)
                for k in range(KC):
                    mm = nc.tensor.transpose(c.ps[:, k // 4, (k % 4) * P:(k % 4 + 1) * P],
                                             x[s][:, k * P:(k + 1) * P], c.ident[:])
                mm.then_inc(x_turned, 1)

            def product(i, s, m, bank_free):
                b = i * ns + s
                pe.wait_ge(x_low, b + 2)
                pe.wait_ge(bank_free, b + 1)
                for k in range(KC):
                    if k % (KC // 2) == 0:
                        pe.wait_ge(low[m], b * 2 + (3 + k // (KC // 2)))
                    mm = three(c.ps[:, 2 + m, :], [p[:, k * P:(k + 1) * P] for p in xT[s]],
                               [p[:, k, :] for p in part[m]], k, KC)
                mm.then_inc(used[m], 1)

            def turn_h(i, s):
                b = i * ns + s
                pe.wait_ge(hidden, b + 2)
                pe.wait_ge(h_low, b + 1)
                for k in range(FC):
                    mm = nc.tensor.transpose(c.ps[:, 4, k * P:(k + 1) * P],
                                             hid[s][:, k * P:(k + 1) * P], c.ident[:])
                mm.then_inc(h_turned, 1)

            def down(i, s):
                b = i * ns + s
                pe.wait_ge(low[DOWN], b * 2 + 4)
                pe.wait_ge(h_low, b + 2)
                pe.wait_ge(half0, b + 1)
                pe.wait_ge(half1, b + 1)
                for h in range(2):
                    for k in range(FC):
                        mm = three(c.ps[:, 5 + h, :], [p[:, k * P:(k + 1) * P] for p in hidT[s]],
                                   [p[:, k, h * BANK:(h + 1) * BANK] for p in part[DOWN]], k, FC)
                mm.then_inc(used[DOWN], 1)

            def cycle(now, before, after):
                if now:
                    product(*now, GATE, opened)
                if before:
                    turn_h(*before)
                if now:
                    product(*now, UP, hidden)
                if after:
                    turn_x(*after)
                if before:
                    down(*before)

            for m in range(3):
                pe.sem_inc(used[m], 1)
            pe.sem_inc(x_turned, ns)
            run(pe, cycle)

        @block.scalar
        def _(act):
            def hi(m):
                def f(i, s):
                    b = i * ns + s
                    act.wait_ge(used[m], b + 1)
                    for h in range(2):
                        act.wait_ge(loaded[m][h], b * 16 + 16)
                        nc.scalar.activation(half_of(part[m][0], h), raw[m][:, h * W // 2:
                                                                            (h + 1) * W // 2],
                                             ACT.Identity).then_inc(high[m], 1)
                return f

            def hi_x(i, s):
                b = i * ns + s
                act.wait_ge(x_turned, b + (ns + 1))
                act.wait_ge(used[UP], b + 1)
                nc.scalar.activation(xT[s][0], flat(0, 2), ACT.Identity).then_inc(x_high, 1)

            def silu(i, s):
                act.wait_ge(used[GATE], i * ns + s + 2)
                nc.scalar.activation(hid[s], c.ps[:, 2 + GATE, :], ACT.Silu).then_inc(opened, 1)

            def hi_h(i, s):
                act.wait_ge(h_turned, i * ns + s + 1)
                nc.scalar.activation(hidT[s][0], c.ps[:, 4, :], ACT.Identity).then_inc(h_high, 1)

            def take_y(i, s):
                b = i * ns + s
                act.wait_ge(used[DOWN], b + 2)
                act.wait_ge(stored[s], i * 16 + 16)
                nc.scalar.activation(y[s][:, 0:BANK], c.ps[:, 5, :], ACT.Identity).then_inc(half0, 1)

            def store(i, s):
                b = i * ns + s
                act.wait_ge(half0, b + 2)
                act.wait_ge(half1, b + 2)
                act.dma_start(y_dram[bass.ds((b + first) * P, P), :], y[s]).then_inc(stored[s], 16)
                if extra:
                    act.wait_ge(stored[s], i * 16 + 32)
                    act.sem_inc(written, 1)

            def cycle(now, before, after):
                if now:
                    silu(*now)
                if before:
                    hi_h(*before)
                if after:
                    hi(GATE)(*after)
                    hi_x(*after)
                    hi(UP)(*after)
                if before:
                    take_y(*before)
                if now:
                    hi(DOWN)(*now)
                if before:
                    store(*before)

            act.sem_inc(opened, 1)
            act.sem_inc(half0, 1)
            run(act, cycle)
            if not extra:
                for s in range(ns):
                    act.wait_ge(stored[s], 16 * steps + 16)

        @block.vector
        def _(dve):
            V = nc.vector

            def lo(m):
                def f(i, s):
                    b = i * ns + s
                    for h in range(2):
                        dve.wait_ge(high[m], b * 2 + (h + 1))
                        V.tensor_tensor(half_of(part[m][1], h), raw[m][:, h * W // 2:
                                                                       (h + 1) * W // 2],
                                        half_of(as_f32(part[m][0]), h), ALU.subtract)\
                            .then_inc(low[m], 1)
                return f

            def lo_x(i, s):
                b = i * ns + s
                dve.wait_ge(x_high, b + 1)
                V.tensor_tensor(xT[s][1], flat(0, 2), as_f32(xT[s][0]), ALU.subtract)\
                    .then_inc(x_low, 1)

            def hide(i, s):
                b = i * ns + s
                dve.wait_ge(opened, b + 2)
                dve.wait_ge(used[UP], b + 2)
                V.tensor_tensor(hid[s], hid[s], c.ps[:, 2 + UP, :], ALU.mult).then_inc(hidden, 1)

            def lo_h(i, s):
                dve.wait_ge(h_high, i * ns + s + 1)
                V.tensor_tensor(hidT[s][1], c.ps[:, 4, :], as_f32(hidT[s][0]), ALU.subtract)\
                    .then_inc(h_low, 1)

            def take_y(i, s):
                dve.wait_ge(used[DOWN], i * ns + s + 2)
                dve.wait_ge(stored[s], i * 16 + 16)
                V.tensor_copy(y[s][:, BANK:D], c.ps[:, 6, :]).then_inc(half1, 1)

            def cycle(now, before, after):
                if before:
                    lo_h(*before)
                if after:
                    lo(GATE)(*after)
                if now:
                    hide(*now)
                if after:
                    lo_x(*after)
                    lo(UP)(*after)
                if before:
                    take_y(*before)
                if now:
                    lo(DOWN)(*now)

            for m in range(3):
                dve.sem_inc(low[m], 2)
            dve.sem_inc(x_low, 1)
            dve.sem_inc(hidden, 1)
            dve.sem_inc(h_low, 1)
            dve.sem_inc(half1, 1)
            run(dve, cycle)


def phase_combine(c, x2_dram, x2, y_dram, out_dram, tmp):
    nc = c.nc
    xv = x2.rearrange("p (t d) -> p t d", t=TT)
    rows = out_dram.rearrange("(t p) d -> p t d", p=P)
    NB = 8
    buf = [tmp[:, s * D:(s + 1) * D] for s in range(NB)]
    with ExitStack() as ctx:
        got = [c.sem(ctx, f"cb_got{s}") for s in range(NB)]
        back = [c.sem(ctx, f"cb_back{t}") for t in range(TT)]
        added, stored = c.sem(ctx, "cb_added"), c.sem(ctx, "cb_stored")
        block = ctx.enter_context(nc.Block())

        @block.gpsimd
        def _(pool):
            for n in range(2 * TT):
                t, j = divmod(n, 2)
                if n >= NB:
                    pool.wait_ge(added, n - NB + 1)
                pool.indirect_dma_start(
                    out=buf[n % NB], out_offset=None, in_=y_dram,
                    in_offset=bass.IndirectOffsetOnAxis(c.dest[j][:, t:t + 1], 0))\
                    .then_inc(got[n % NB], 16)

        @block.vector
        def _(dve):
            for n in range(2 * TT):
                t, j = divmod(n, 2)
                dve.wait_ge(got[n % NB], 16 * (n // NB + 1))
                if j:
                    dve.wait_ge(added, n)
                else:
                    dve.wait_ge(back[t], 16)
                nc.vector.scalar_tensor_tensor(out=xv[:, t, :], in0=buf[n % NB],
                                               scalar=c.weight[j][:, t:t + 1], in1=xv[:, t, :],
                                               op0=ALU.mult, op1=ALU.add).then_inc(added, 1)

        @block.sync
        def _(sp):
            kept = x2_dram.rearrange("(t p) d -> p t d", p=P)
            for t in range(TT):
                sp.dma_start(xv[:, t, :], kept[:, t, :]).then_inc(back[t], 16)
            for t in range(TT):
                sp.wait_ge(added, 2 * t + 2)
                sp.dma_start(rows[:, t, :], xv[:, t, :]).then_inc(stored, 16)
            sp.wait_ge(stored, 16 * TT)


def _build(nc, a, out, upto=99):
    with ExitStack() as ctx:
        c = Chip(nc, ctx)
        R = lambda r: c.at(r, 0, REGION)
        ys = nc.dram_tensor("expert_out", (SLOTS, D), F32).ap()
        zeroed = c.sem(ctx, "zeroed")
        zero = c.at(4, REGION - D, D)
        phase_constants(c, zero)

        def background(sp):
            with nc.allow_non_contiguous_dma(reason="per-channel vectors by chunks"):
                for j in range(CONV):
                    sp.dma_start(c.taps[:, :, j], a["conv_w"][0][j].rearrange("(b p) -> p b", p=P))\
                        .then_inc(zeroed, 16)
                sp.dma_start(c.tap_bias, a["conv_b"][0].rearrange("(b p) -> p b", p=P))\
                    .then_inc(zeroed, 16)
            for b in range(EXTRA):
                sp.dma_start(ys[(NE + b) * P:(NE + b + 1) * P, :], zero).then_inc(zeroed, 16)

        phase_norm_T(c, "pre", R(1), R(0), R(2), a["pre_norm_g"][0], src_dram=a["x"][0],
                     background=background)
        T = lambda r, k=KC: r.rearrange("p (k s) -> p k s", k=k)
        half = lambda r, n: r.rearrange("p (t d) -> p t d", t=TT)[:, :, n * BANK:(n + 1) * BANK]
        wide = lambda r, n: c.at(r, n * 4096, 4096).rearrange("p (b n) -> p b n", n=BANK)
        wcol = lambda w, a0, n: cols(w)[:, :, a0 + n * BANK:a0 + (n + 1) * BANK]
        w_in = a["w_in"][0]
        xbc_in, xbc_out = c.at(1, 0, 2 * REGION), c.at(3, 0, 2 * REGION)

        def convolve_xbc(n, tapped, by_act, by_vec, moved):
            for x in range(2 * (n - KC), 2 * (n - KC) + 2):
                if x >= 0:
                    b, back = divmod(x, CONV)
                    if back == 0:
                        nc.vector.wait_ge(by_act, 2 * b + 2)
                        if b == 0:
                            nc.vector.wait_ge(zeroed, 16 * (EXTRA + CONV + 1))
                    else:
                        nc.vector.wait_ge(tapped, x)
                    convolve_tap(nc.vector, x, c.taps, c.tap_bias, T(xbc_in, XBC // P),
                                 T(xbc_out, XBC // P), tapped)

        phase_dense(c, "xbc", [(T(R(0)), wcol(w_in, C_XBC, n), "act_T", wide(1 + n // 2, n % 2),
                                ACT.Identity) for n in range(XBC // BANK)], 5,
                    aside=convolve_xbc, trailing=KC)
        phase_xbc_turn(c, xbc_out, xbc_in)
        fcum = nc.dram_tensor("forget_sums", (HEADS, SEQ), F32).ap()
        phase_decays(c, R(0), a["w_in"][0], a["dt_bias"][0], a["a_log"][0], a["d_skip"][0],
                     a["fgate_b"][0], fcum, R(5))
        if upto < 2:
            return c
        phase_ssd(c, c.at(1, 0, 2 * REGION), R(4), R(3), R(5))
        if upto < 3:
            return c
        phase_dense(c, "z", [(T(R(0)), wcol(w_in, C_Z, n), "act", half(R(2), n), ACT.Silu)
                             for n in range(2)], 5)
        phase_turn(c, "y", R(3), R(1), gate=R(2), groups=GROUPS, gain_dram=a["ssm_norm_g"][0])
        if upto < 4:
            return c
        heads_T = [nc.dram_tensor(n, (D, SEQ), F32).ap() for n in ("att_q", "att_k")]
        phase_dense(c, "bs", [(T(R(0)), wcol(w_in, C_GS, n), "act_T", wide(4, n), ACT.Sigmoid)
                              for n in range(2)]
                    + [(T(R(1)), wcol(a["w_branch_ssm"][0], 0, n), "mul_T", wide(2, n), wide(4, n))
                       for n in range(2)]
                    + [(T(R(0)), wcol(w_in, C_V, n), "act", half(R(3), n), ACT.Identity)
                       for n in range(2)]
                    + [(T(R(0)), wcol(w_in, (C_Q, C_K)[n // 2], n % 2), "keep_T",
                        wide((1, 4)[n // 2], n % 2), ACT.Identity,
                        heads_T[n // 2][n % 2 * BANK:(n % 2 + 1) * BANK, :],
                        (float(HD) ** -0.5, 1.0)[n // 2]) for n in range(4)], 5)
        phase_forget_attention(c, *heads_T, fcum, R(3), R(4), R(1), R(5))
        if upto < 5:
            return c
        phase_dense(c, "za", [(T(R(0)), wcol(w_in, C_ZA, n), "act", half(R(1), n), ACT.Silu)
                              for n in range(2)]
                    + [(T(R(0)), wcol(w_in, C_GA, n), "act_T", wide(3, n), ACT.Sigmoid)
                       for n in range(2)], 5)
        phase_turn(c, "ya", R(4), R(5), gate=R(1))
        phase_dense(c, "ba", [(T(R(5)), wcol(a["w_branch_att"][0], 0, n), "muladd_T", wide(2, n),
                               wide(3, n)) for n in range(2)]
                    + [(T(R(2)), wcol(a["w_out"][0], 0, n), "act", half(R(3), n), ACT.Identity)
                       for n in range(2)], 1, made_by={2: 0, 3: 0})
        phase_post(c, a["x"][0], a["post_norm_g"][0], R(3), R(4), R(2))
        if upto < 6:
            return c
        phase_norm_T(c, "n2", R(4), R(0), R(1), a["attn_norm_g_2"][0])
        w_in = a["w_in_2"][0]
        h2 = T(R(0))
        v2 = c.at(2, 4096, 4096)
        v2h = v2.rearrange("p (t d) -> p t d", t=TT)
        conv = c.at(2, 0, 4096)
        phase_taps(c, c.at(5, 0, CCH), a["conv_dw_w_2"][0], a["conv_dw_b_2"][0])
        halfway = CCH // P // 2
        T2 = lambda r, at: T(c.at(r, at, 2 * SEQ), 2)
        y_late = T2(2, 2 * SEQ)
        y_parts = [T2(3, 0), y_late]
        if upto < 7:
            return c
        o2 = c.at(1, 0, 4096)
        def convolve_half(first, start, steps, src):
            taps, bias = c.taps2[:, first:first + 2, :], c.tap_bias2[:, first:first + 2]
            acc = T(conv, 4)[:, first:first + 2, :]

            def aside(n, tapped, by_act, by_vec, moved):
                n -= start
                if n < 0:
                    return
                if n == 0 and first:
                    nc.vector.wait_ge(moved, 2)
                elif n == 0:
                    nc.vector.wait_ge(by_vec, TT)
                for x in range(2 * CW * n // steps, 2 * CW * (n + 1) // steps if n < steps else 0):
                    if x % CW:
                        nc.vector.wait_ge(tapped, x)
                    convolve_tap(nc.vector, x, taps, bias, src, acc, tapped)
            return aside

        phase_dense(c, "q2", [(h2, wcol(w_in, CCH, 0), "act_T", wide(1, 0), ACT.Sigmoid),
                              (h2, wcol(w_in, 0, 0), "mul_T",
                               [y_parts[t // 4][:, t // 2 % 2, t % 2 * BANK:(t % 2 + 1) * BANK]
                                for t in range(TT)], wide(1, 0)),
                              (h2, wcol(w_in, C2_V, 0), "act", v2h, ACT.Identity)]
                    + [(h2, wcol(w_in, (C2_Q, C2_K)[n], 0), "act_T", wide(1, n), ACT.Identity)
                       for n in range(2)], 5,
                    aside=convolve_half(0, 2 * KC + 1, 3 * KC - 1, y_parts[0]))
        phase_diff_attention(c, R(1), a["q_norm_g_2"][0], a["k_norm_g_2"][0],
                             [a[f"lambda_{n}_2"][0] for n in ("q1", "k1", "q2", "k2")], v2, o2,
                             R(3), c.at(5, 0, 4 * SEQ), c.at(5, 4 * SEQ, 4 * SEQ), c.at(1, 4 * SEQ, 2 * SEQ))
        phase_turn(c, "o2", o2, v2, groups=DH, gain_dram=a["subln_g_2"][0], gain_times=1.0 - LAM_INIT,
                   width=DH * DV)
        if upto < 8:
            return c
        moved = T2(1, 0)
        phase_dense(c, "g2", [(h2, wcol(w_in, C2_G, n), "act_T", wide(3, n), ACT.Sigmoid)
                              for n in range(2)], 5, aside=convolve_half(2, 0, 2 * KC, moved),
                    move=[(moved[:, b, :], y_late[:, b, :]) for b in range(2)])
        phase_channel_norm(c, conv, c.at(1, 0, 4096), c.at(1, 4096, SEQ), a["conv_ln_g_2"][0],
                           a["conv_ln_b_2"][0])
        phase_dense(c, "b2", [(h2, wcol(w_in, C2_G, 2 + n), "act_T", wide(1, n), ACT.Sigmoid)
                              for n in range(2)]
                    + [(T(conv, 4), wcol(a["w_conv_out_2"][0], 0, n), "mul_T", wide(3, n),
                        wide(3, n)) for n in range(2)]
                    + [(T(v2, 4), wcol(a["w_attn_out_2"][0], 0, n), "muladd_T", wide(3, n),
                        wide(1, n)) for n in range(2)]
                    + [(T(R(3)), wcol(a["w_out_2"][0], 0, n), "add", half(R(4), n), None)
                       for n in range(2)], 5, made_by={6: 4, 7: 4})
        if upto < 9:
            return c
        xn = nc.dram_tensor("expert_in", (SEQ, D), F32).ap()
        slot_dram = [nc.dram_tensor(f"slot_tokens{n}", (SLOTS, 1), I32).ap() for n in range(2 * TT)]
        x2_dram = nc.dram_tensor("x2_kept", (SEQ, D), F32).ap()
        phase_norm_T(c, "n3", R(4), R(0), R(1), a["ffn_norm_g_2"][0], xn_dram=xn,
                     row_gain=c.at(5, 0, D), keep_dram=x2_dram)
        phase_router(c, R(0), a["w_router_group_2"][0], a["w_router_expert_2"][0],
                     a["b_router_group_2"][0], a["b_router_expert_2"][0], slot_dram, c.at(1, 0, 2 * REGION))
        if upto < 10:
            return c
        for extra in (False, True):
            phase_experts(c, "xe" if extra else "ex", xn, ys, a["w_gate_e_2"][0], a["w_up_e_2"][0],
                          a["w_down_e_2"][0], extra)
        phase_combine(c, x2_dram, R(4), ys, out[0], R(1))
        return c


_INS = ['x', 'pre_norm_g', 'w_in', 'conv_w', 'conv_b', 'dt_bias', 'a_log', 'd_skip', 'ssm_norm_g',
        'fgate_b', 'w_branch_ssm', 'w_branch_att', 'w_out', 'post_norm_g', 'attn_norm_g_2',
        'w_in_2', 'conv_dw_w_2', 'conv_dw_b_2', 'conv_ln_g_2', 'conv_ln_b_2', 'w_conv_out_2',
        'q_norm_g_2', 'k_norm_g_2', 'lambda_q1_2', 'lambda_k1_2', 'lambda_q2_2', 'lambda_k2_2',
        'subln_g_2', 'w_attn_out_2', 'w_out_2', 'ffn_norm_g_2', 'w_router_group_2',
        'b_router_group_2', 'w_router_expert_2', 'b_router_expert_2', 'w_gate_e_2', 'w_up_e_2',
        'w_down_e_2']


def kernel(**inputs):
    import numpy as _np
    import concourse.bacc as _bacc
    from concourse import mybir as _mybir
    from concourse.bass_utils import run_bass_kernel_spmd as _run

    nc = _bacc.Bacc("TRN2", target_bir_lowering=False, num_devices=1)
    arrays, args = {}, {}
    for name in _INS:
        v = _np.ascontiguousarray(inputs[name])
        arrays[f"in_{name}"] = v
        args[name] = nc.dram_tensor(f"in_{name}", v.shape, _mybir.dt.from_np(v.dtype),
                                    kind="ExternalInput").ap()
    out = nc.dram_tensor("out_0", (1, SEQ, D), _mybir.dt.float32, kind="ExternalOutput").ap()
    _build(nc, args, out)
    r = _run(nc, [arrays], core_ids=[0])
    return r.results[0]["out_0"]
```
